# Optimizing a Trainium2 kernel written in Bass

```python
import math
import jax
import jax.numpy as jnp
from jax import lax
import numpy as np

D_MODEL = 1024
BATCH = 1
SEQ = 256
DEPTH = 2

GRID_W = 64
CTX_LEN = 256
N_MIXERS = 4
DIFF_MIXER = 0
NA_MIXER = 1
GQA_MIXER = 2
CONV_MIXER = 3
HEAD_DIM = 64
ATTN_SCALE = HEAD_DIM ** -0.5
DIFF_HEADS = D_MODEL // (2 * HEAD_DIM)
NA_HEADS = D_MODEL // HEAD_DIM
NA_WR = 8
NA_WC = 16
NA_QC = 16
NA_KC = NA_QC + NA_WC
GQA_Q_HEADS = D_MODEL // HEAD_DIM
GQA_KV_HEADS = 4
GQA_GROUP = GQA_Q_HEADS // GQA_KV_HEADS
ROPE_THETA = 10000.0
Q_BLOCK = 128
CONV_WIDTH = 3
N_EXPERTS = 16
N_GROUPS = 4
GROUP_SIZE = N_EXPERTS // N_GROUPS
GROUP_SCORE_TOPK = 2
TOPK_GROUPS = 1
TOP_K = 2
EXPERT_FF = 512
NORM_EPS = 1e-6
NEG_INF = -1e30

kernel_name = 'hybrid_interleaved_diffusion_trunk_shared_router_moe'

def rms_norm(x, g):
    xf = x.astype(jnp.float32)
    y = xf * lax.rsqrt(jnp.mean(xf * xf, axis=-1, keepdims=True) + NORM_EPS)
    return (y * g.astype(jnp.float32)).astype(x.dtype)

def modulate(h, shift, scale):
    return h * (1.0 + scale) + shift

def axial_rope(n):
    t = jnp.arange(n)
    row = (t // GRID_W).astype(jnp.float32)
    col = (t % GRID_W).astype(jnp.float32)
    quarter = HEAD_DIM // 4
    inv_freq = ROPE_THETA ** (-jnp.arange(quarter, dtype=jnp.float32) / quarter)
    ang = jnp.concatenate([row[:, None] * inv_freq, col[:, None] * inv_freq], axis=-1)
    return jnp.cos(ang), jnp.sin(ang)

def apply_rope(x, cos, sin):
    x1, x2 = jnp.split(x, 2, axis=-1)
    cos = cos.astype(x.dtype)
    sin = sin.astype(x.dtype)
    return jnp.concatenate([x1 * cos - x2 * sin, x2 * cos + x1 * sin], axis=-1)

def sweep_query_blocks(block_fn, q):
    *lead, n, d = q.shape
    nb = n // Q_BLOCK
    qb = jnp.moveaxis(q.reshape(*lead, nb, Q_BLOCK, d), -3, 0)
    out = lax.map(block_fn, qb)
    out = jnp.moveaxis(out, 0, -3)
    return out.reshape(*out.shape[:-3], n, out.shape[-1])

def softmax_attend(q, k, v):
    s = jnp.einsum('bhgqd,bhkd->bhgqk', q, k).astype(jnp.float32)
    p = jax.nn.softmax(s, axis=-1).astype(v.dtype)
    return jnp.einsum('bhgqk,bhkd->bhgqd', p, v)

def diff_attend(q, k, v, lam):
    s = jnp.einsum('cbhqd,cbhkd->cbhqk', q, k).astype(jnp.float32)
    p = jax.nn.softmax(s, axis=-1)
    a = (p[0] - lam * p[1]).astype(v.dtype)
    return jnp.einsum('bhqk,bhkd->bhqd', a, v)

def diff_attention(h_lat, h_ctx, w_qkv, w_o, lq1, lk1, lq2, lk2, subln_g, lambda_init, cos, sin, ctx_out):
    f32 = jnp.float32
    lam = (jnp.exp(jnp.sum(lq1.astype(f32) * lk1.astype(f32)))
           - jnp.exp(jnp.sum(lq2.astype(f32) * lk2.astype(f32))) + lambda_init)

    def project(h):
        b, n, _ = h.shape
        q, k, v = jnp.split(h @ w_qkv, 3, axis=-1)
        q = q.reshape(b, n, DIFF_HEADS, 2, HEAD_DIM).transpose(3, 0, 2, 1, 4) * ATTN_SCALE
        k = k.reshape(b, n, DIFF_HEADS, 2, HEAD_DIM).transpose(3, 0, 2, 1, 4)
        v = v.reshape(b, n, DIFF_HEADS, 2 * HEAD_DIM).transpose(0, 2, 1, 3)
        return q, k, v

    ql, kl, vl = project(h_lat)
    qc, kc, vc = project(h_ctx)
    ql = apply_rope(ql, cos, sin)
    kl = apply_rope(kl, cos, sin)
    k_all = jnp.concatenate([kc, kl], axis=-2)
    v_all = jnp.concatenate([vc, vl], axis=-2)

    def finish(o):
        o = rms_norm(o, subln_g) * (1.0 - lambda_init)
        b, _, n, _ = o.shape
        return o.transpose(0, 2, 1, 3).reshape(b, n, D_MODEL) @ w_o

    y_lat = finish(sweep_query_blocks(lambda qb: diff_attend(qb, k_all, v_all, lam), ql))
    y_ctx = finish(diff_attend(qc, kc, vc, lam)) if ctx_out else None
    return y_lat, y_ctx

def neighborhood_attention(h_lat, h_ctx, w_qkv, w_o, rpb, ctx_out):
    b, n, _ = h_lat.shape
    rows = n // GRID_W
    wr = min(NA_WR, rows)
    n_cb = GRID_W // NA_QC

    def project(h):
        q, k, v = jnp.split(h @ w_qkv, 3, axis=-1)

        def heads(t):
            return t.reshape(b, t.shape[1], NA_HEADS, HEAD_DIM).transpose(0, 2, 1, 3)
        return heads(q) * ATTN_SCALE, heads(k), heads(v)

    q, k, v = project(h_lat)
    qc, kc, vc = project(h_ctx)
    qg = q.reshape(b, NA_HEADS, rows, GRID_W, HEAD_DIM)
    kg = k.reshape(b, NA_HEADS, rows, GRID_W, HEAD_DIM)
    vg = v.reshape(b, NA_HEADS, rows, GRID_W, HEAD_DIM)

    q_cols = np.arange(GRID_W).reshape(n_cb, NA_QC)
    win_c0 = np.clip(q_cols - NA_WC // 2, 0, GRID_W - NA_WC)
    key_c0 = np.clip(q_cols[:, 0] - NA_WC // 2, 0, GRID_W - NA_KC)
    key_cols = key_c0[:, None] + np.arange(NA_KC)
    kcol = key_cols[:, None, :]
    col_valid = (kcol >= win_c0[..., None]) & (kcol < win_c0[..., None] + NA_WC)
    col_off = np.clip(kcol - q_cols[..., None] + NA_WC - 1, 0, 2 * NA_WC - 2)
    valid = np.broadcast_to(col_valid[:, :, None, :], (n_cb, NA_QC, wr, NA_KC)).reshape(n_cb, NA_QC, wr * NA_KC)
    n_loc = wr * NA_KC

    def row_fn(r):
        rs = jnp.clip(r - wr // 2, 0, rows - wr)
        q_r = lax.dynamic_index_in_dim(qg, r, axis=2, keepdims=False).reshape(b, NA_HEADS, n_cb, NA_QC, HEAD_DIM)

        def gather(t):
            band = lax.dynamic_slice_in_dim(t, rs, wr, axis=2)
            blk = band[:, :, :, key_cols]
            return blk.transpose(0, 1, 3, 2, 4, 5).reshape(b, NA_HEADS, n_cb, n_loc, HEAD_DIM)

        k_blk = gather(kg)
        v_blk = gather(vg)
        row_idx = rs + jnp.arange(wr) - r + (NA_WR - 1)
        bias = jnp.take(rpb, row_idx, axis=1)[:, :, col_off]
        bias = bias.transpose(0, 2, 3, 1, 4).reshape(NA_HEADS, n_cb, NA_QC, n_loc).astype(jnp.float32)
        bias = jnp.where(valid, bias, NEG_INF)
        s_loc = jnp.einsum('bhjqd,bhjkd->bhjqk', q_r, k_blk).astype(jnp.float32) + bias
        s_ctx = jnp.einsum('bhjqd,bhkd->bhjqk', q_r, kc).astype(jnp.float32)
        p = jax.nn.softmax(jnp.concatenate([s_loc, s_ctx], axis=-1), axis=-1).astype(v.dtype)
        o = (jnp.einsum('bhjqk,bhjkd->bhjqd', p[..., :n_loc], v_blk)
             + jnp.einsum('bhjqk,bhkd->bhjqd', p[..., n_loc:], vc))
        return o.reshape(b, NA_HEADS, GRID_W, HEAD_DIM)

    o = lax.map(row_fn, jnp.arange(rows))
    y_lat = o.transpose(1, 0, 3, 2, 4).reshape(b, n, D_MODEL) @ w_o
    y_ctx = None
    if ctx_out:
        oc = softmax_attend(qc[:, :, None], kc, vc)[:, :, 0]
        y_ctx = oc.transpose(0, 2, 1, 3).reshape(b, -1, D_MODEL) @ w_o
    return y_lat, y_ctx

def gqa_attention(h_lat, h_ctx, w_qkv, w_o, q_norm_g, k_norm_g, cos, sin, ctx_out):
    q_w = GQA_Q_HEADS * HEAD_DIM
    kv_w = GQA_KV_HEADS * HEAD_DIM

    def project(h):
        b, n, _ = h.shape
        q, k, v = jnp.split(h @ w_qkv, [q_w, q_w + kv_w], axis=-1)
        q = rms_norm(q.reshape(b, n, GQA_KV_HEADS, GQA_GROUP, HEAD_DIM), q_norm_g).transpose(0, 2, 3, 1, 4) * ATTN_SCALE
        k = rms_norm(k.reshape(b, n, GQA_KV_HEADS, HEAD_DIM), k_norm_g).transpose(0, 2, 1, 3)
        v = v.reshape(b, n, GQA_KV_HEADS, HEAD_DIM).transpose(0, 2, 1, 3)
        return q, k, v

    ql, kl, vl = project(h_lat)
    qc, kc, vc = project(h_ctx)
    ql = apply_rope(ql, cos, sin)
    kl = apply_rope(kl, cos, sin)
    k_all = jnp.concatenate([kc, kl], axis=2)
    v_all = jnp.concatenate([vc, vl], axis=2)

    def merge(o):
        b, _, _, n, _ = o.shape
        return o.transpose(0, 3, 1, 2, 4).reshape(b, n, q_w) @ w_o

    y_lat = merge(sweep_query_blocks(lambda qb: softmax_attend(qb, k_all, v_all), ql))
    y_ctx = merge(softmax_attend(qc, kc, vc)) if ctx_out else None
    return y_lat, y_ctx

def short_conv_mixer(h, w_in, w_conv, w_out):
    gb, gc, u = jnp.split(h @ w_in, 3, axis=-1)
    z = lax.conv_general_dilated(gc * u, w_conv[:, None, :], window_strides=(1,),
                                 padding=((CONV_WIDTH // 2, CONV_WIDTH // 2),),
                                 dimension_numbers=('NWC', 'WIO', 'NWC'),
                                 feature_group_count=D_MODEL)
    return (gb * z) @ w_out

def moe_ffn(h, router_w, router_bias, w_gate, w_up, w_down):
    t = h.shape[0]
    scores = jax.nn.sigmoid((h @ router_w).astype(jnp.float32))
    sel = scores + router_bias.astype(jnp.float32)
    grp_score = lax.top_k(sel.reshape(t, N_GROUPS, GROUP_SIZE), GROUP_SCORE_TOPK)[0].sum(-1)
    _, grp_idx = lax.top_k(grp_score, TOPK_GROUPS)
    grp_mask = jax.nn.one_hot(grp_idx, N_GROUPS, dtype=jnp.float32).sum(1) > 0
    exp_mask = jnp.repeat(grp_mask, GROUP_SIZE, axis=-1)
    _, exp_idx = lax.top_k(jnp.where(exp_mask, sel, NEG_INF), TOP_K)
    w = jnp.take_along_axis(scores, exp_idx, axis=-1)
    w = w / jnp.sum(w, axis=-1, keepdims=True)
    gates = jnp.einsum('tk,tke->te', w, jax.nn.one_hot(exp_idx, N_EXPERTS, dtype=jnp.float32)).astype(h.dtype)
    y = jnp.zeros_like(h)
    for e in range(N_EXPERTS):
        a = jax.nn.silu(h @ w_gate[e]) * (h @ w_up[e])
        y = y + gates[:, e:e + 1] * (a @ w_down[e])
    return y

def setup_inputs(seed: int = 0) -> dict:
    key = jax.random.key(seed)
    keys = iter(jax.random.split(key, 64))

    def nrm(shape, scale):
        return jax.random.normal(next(keys), shape, jnp.float32) * scale

    def gain(shape):
        return 1.0 + nrm(shape, 0.02)

    n_a, n_b, n_c, n_d = (len(range(m, DEPTH, N_MIXERS)) for m in range(N_MIXERS))
    d = D_MODEL
    fan = d ** -0.5
    return {
        'x': nrm((BATCH, SEQ, d), 1.0),
        'c': nrm((BATCH, d), 1.0),
        'ctx': nrm((BATCH, CTX_LEN, d), 1.0),
        'c_ctx': nrm((d,), 1.0),
        'ada_w': nrm((DEPTH, d, 6 * d), 0.5 * fan),
        'ada_b': nrm((DEPTH, 6 * d), 0.02),
        'norm1_g': gain((DEPTH, d)),
        'norm2_g': gain((DEPTH, d)),
        'final_norm_g': gain((d,)),
        'diff_w_qkv': nrm((n_a, d, 3 * d), fan),
        'diff_w_o': nrm((n_a, d, d), fan),
        'diff_lambda_q1': nrm((n_a, HEAD_DIM), 0.1),
        'diff_lambda_k1': nrm((n_a, HEAD_DIM), 0.1),
        'diff_lambda_q2': nrm((n_a, HEAD_DIM), 0.1),
        'diff_lambda_k2': nrm((n_a, HEAD_DIM), 0.1),
        'diff_subln_g': gain((n_a, 2 * HEAD_DIM)),
        'na_w_qkv': nrm((n_b, d, 3 * d), fan),
        'na_w_o': nrm((n_b, d, d), fan),
        'na_rpb': nrm((n_b, NA_HEADS, 2 * NA_WR - 1, 2 * NA_WC - 1), 0.1),
        'gqa_w_qkv': nrm((n_c, d, (GQA_Q_HEADS + 2 * GQA_KV_HEADS) * HEAD_DIM), fan),
        'gqa_w_o': nrm((n_c, GQA_Q_HEADS * HEAD_DIM, d), fan),
        'gqa_q_norm_g': gain((n_c, HEAD_DIM)),
        'gqa_k_norm_g': gain((n_c, HEAD_DIM)),
        'conv_w_in': nrm((n_d, d, 3 * d), fan),
        'conv_w': nrm((n_d, CONV_WIDTH, d), CONV_WIDTH ** -0.5),
        'conv_w_out': nrm((n_d, d, d), fan),
        'router_w': nrm((d, N_EXPERTS), fan),
        'router_bias': nrm((N_EXPERTS,), 0.01),
        'moe_w_gate': nrm((DEPTH, N_EXPERTS, d, EXPERT_FF), fan),
        'moe_w_up': nrm((DEPTH, N_EXPERTS, d, EXPERT_FF), fan),
        'moe_w_down': nrm((DEPTH, N_EXPERTS, EXPERT_FF, d), EXPERT_FF ** -0.5),
    }

def reference(x, c, ctx, c_ctx, ada_w, ada_b, norm1_g, norm2_g, final_norm_g,
              diff_w_qkv, diff_w_o, diff_lambda_q1, diff_lambda_k1, diff_lambda_q2, diff_lambda_k2, diff_subln_g,
              na_w_qkv, na_w_o, na_rpb,
              gqa_w_qkv, gqa_w_o, gqa_q_norm_g, gqa_k_norm_g,
              conv_w_in, conv_w, conv_w_out,
              router_w, router_bias, moe_w_gate, moe_w_up, moe_w_down):
    b, n, d = x.shape
    n_ctx = ctx.shape[1]
    cos, sin = axial_rope(n)
    silu_c = jax.nn.silu(c)
    silu_cc = jax.nn.silu(c_ctx)
    reads_ctx = [i % N_MIXERS != CONV_MIXER for i in range(DEPTH)]
    ctx_needed = [any(reads_ctx[i + 1:]) for i in range(DEPTH)]
    for i in range(DEPTH):
        m = i % N_MIXERS
        j = i // N_MIXERS
        ctx_out = ctx_needed[i]
        sh1, sc1, g1, sh2, sc2, g2 = jnp.split((silu_c @ ada_w[i] + ada_b[i])[:, None, :], 6, axis=-1)
        hl = modulate(rms_norm(x, norm1_g[i]), sh1, sc1)
        hc = None
        if reads_ctx[i] or ctx_out:
            csh1, csc1, cg1, csh2, csc2, cg2 = jnp.split(silu_cc @ ada_w[i] + ada_b[i], 6)
            hc = modulate(rms_norm(ctx, norm1_g[i]), csh1, csc1)
        if m == DIFF_MIXER:
            lambda_init = 0.8 - 0.6 * math.exp(-0.3 * i)
            yl, yc = diff_attention(hl, hc, diff_w_qkv[j], diff_w_o[j], diff_lambda_q1[j], diff_lambda_k1[j],
                                    diff_lambda_q2[j], diff_lambda_k2[j], diff_subln_g[j], lambda_init,
                                    cos, sin, ctx_out)
        elif m == NA_MIXER:
            yl, yc = neighborhood_attention(hl, hc, na_w_qkv[j], na_w_o[j], na_rpb[j], ctx_out)
        elif m == GQA_MIXER:
            yl, yc = gqa_attention(hl, hc, gqa_w_qkv[j], gqa_w_o[j], gqa_q_norm_g[j], gqa_k_norm_g[j],
                                   cos, sin, ctx_out)
        else:
            yl = short_conv_mixer(hl, conv_w_in[j], conv_w[j], conv_w_out[j])
            yc = short_conv_mixer(hc, conv_w_in[j], conv_w[j], conv_w_out[j]) if ctx_out else None
        x = x + g1 * yl
        hl = modulate(rms_norm(x, norm2_g[i]), sh2, sc2).reshape(b * n, d)
        if ctx_out:
            ctx = ctx + cg1 * yc
            hc = modulate(rms_norm(ctx, norm2_g[i]), csh2, csc2).reshape(b * n_ctx, d)
            y = moe_ffn(jnp.concatenate([hc, hl], axis=0), router_w, router_bias,
                        moe_w_gate[i], moe_w_up[i], moe_w_down[i])
            ctx = ctx + cg2 * y[: b * n_ctx].reshape(b, n_ctx, d)
            y = y[b * n_ctx:]
        else:
            y = moe_ffn(hl, router_w, router_bias, moe_w_gate[i], moe_w_up[i], moe_w_down[i])
        x = x + g2 * y.reshape(b, n, d)
    return rms_norm(x, final_norm_g)


_drawn_inputs = setup_inputs


def setup_inputs(seed=0):
    import zlib

    import numpy as np

    out = dict(_drawn_inputs(seed))
    spreads = {}
    factors = {'final_norm_g': 9.164, 'diff_subln_g': 3.757, 'na_rpb': 25.848}
    for name, (base, spread) in spreads.items():
        noise = np.random.default_rng([zlib.crc32(name.encode()), seed]).standard_normal(out[name].shape)
        drawn = base * np.exp(spread * noise) if base else spread * noise
        out[name] = jnp.asarray(drawn.astype(out[name].dtype))
    for name, factor in factors.items():
        out[name] = (out[name] * factor).astype(out[name].dtype)
    return out
```

```python
import math
from contextlib import ExitStack

import numpy as np

import concourse.bass as bass
from concourse import mybir

F32 = mybir.dt.float32
I32 = mybir.dt.int32
ALU = mybir.AluOpType
ACT = mybir.ActivationFunctionType
X_AXIS = mybir.AxisListType.X

P = 128
D = 1024
KC = D // P
SEQ = 256
CTX = 256
LAYERS = 2
TILES = (SEQ + CTX) // P
CTX_TILES = CTX // P
GRID_W = 64
GRID_H = SEQ // GRID_W
HD = 64
SCALE = HD ** -0.5
EPS = 1e-6
DIFF_HEADS = D // (2 * HD)
NA_HEADS = D // HD
NA_WR, NA_WC = 8, 16
RPB_H, RPB_W = 2 * NA_WR - 1, 2 * NA_WC - 1
ROPE_THETA = 10000.0
LAMBDA_INIT = 0.8 - 0.6 * math.exp(-0.3 * 0)
N_EXP, N_GRP = 16, 4
GRP = N_EXP // N_GRP
FF = 512
STRIP = 512
NEG = 1e30
NO_ROW = 100000
MAX_BLOCKS = 23
BLK_COLS = MAX_BLOCKS + 1

TILES_OF = [list(range(TILES)), list(range(CTX_TILES, TILES))]

CONST_PARTS = [("ident", P), ("mirror", P), ("before", P), ("slot", P), ("block", BLK_COLS), ("rev_expert", N_EXP),
               ("rev_group", N_GRP), ("token", TILES), ("dest", 2 * TILES), ("cos", 2 * 32), ("sin", 2 * 32),
               ("valid", GRID_W), ("invalid", GRID_W)]
CONST_AT, _at = {}, 0
for _name, _n in CONST_PARTS:
    CONST_AT[_name] = (_at, _at + _n)
    _at += _n
CONST_COLS = _at

VEC_ROWS = {"c_ctx": (0, 8), "c": (8, 16), "norm1": (16, 32), "norm2": (32, 48), "subln": (48, 49)}
N_VEC = 49


def constants():
    t = np.zeros((P, CONST_COLS), np.float32)

    def put(name, a):
        lo, hi = CONST_AT[name]
        t[:, lo:hi] = a

    p = np.arange(P)
    put("ident", np.eye(P))
    mirrored = p // GRID_W * GRID_W + GRID_W - 1 - p % GRID_W
    put("mirror", mirrored[:, None] == p[None, :])
    put("before", p[:, None] < p[None, :])
    put("slot", np.broadcast_to(p, (P, P)))
    put("block", np.broadcast_to(np.arange(BLK_COLS), (P, BLK_COLS)))
    put("rev_expert", np.broadcast_to(N_EXP - np.arange(N_EXP), (P, N_EXP)))
    put("rev_group", np.broadcast_to(N_GRP - np.arange(N_GRP), (P, N_GRP)))
    put("token", p[:, None] + P * np.arange(TILES) + 1)
    put("dest", p[:, None] + P * np.arange(2 * TILES) + 1)
    tok = np.arange(SEQ)
    inv = (np.float32(ROPE_THETA) ** (-np.arange(HD // 4, dtype=np.float32) / np.float32(HD // 4))).astype(np.float32)
    row, col = (tok // GRID_W).astype(np.float32), (tok % GRID_W).astype(np.float32)
    ang = np.concatenate([row[:, None] * inv, col[:, None] * inv], -1).astype(np.float32)
    put("cos", np.cos(ang).reshape(2, P, 32).transpose(1, 0, 2).reshape(P, 64))
    put("sin", np.sin(ang).reshape(2, P, 32).transpose(1, 0, 2).reshape(P, 64))
    c = mirrored % GRID_W
    c0 = np.clip(c - NA_WC // 2, 0, GRID_W - NA_WC)[:, None]
    keys = np.arange(GRID_W)[None, :]
    valid = (keys >= c0) & (keys < c0 + NA_WC)
    put("valid", valid)
    put("invalid", np.where(valid, 0.0, -NEG))
    return t


def build_trunk(nc, x, c, ctx, c_ctx, ada_w, ada_b, norm1_g, norm2_g, final_norm_g, diff_w_qkv, diff_w_o,
                diff_lambda_q1, diff_lambda_k1, diff_lambda_q2, diff_lambda_k2, diff_subln_g,
                na_w_qkv, na_w_o, na_rpb, router_w, router_bias, moe_w_gate, moe_w_up, moe_w_down,
                consts, out):
    with ExitStack() as stack:
        def sb(name, shape, dt=F32):
            return stack.enter_context(nc.sbuf_tensor(name, shape, dt))

        def sem(name):
            return stack.enter_context(nc.semaphore(name))

        cst = sb("cst", [P, CONST_COLS])
        resid = sb("resid", [P, TILES, D])
        hT = sb("hT", [P, KC, TILES * P])
        tokm = sb("tokm", [P, TILES, D])
        val = sb("val", [P, TILES, D])
        qT = sb("qT", [P, KC, TILES * P])
        kT = sb("kT", [P, KC, TILES * P])
        ring = sb("ring", [P, 3, KC, STRIP])
        rows = sb("rows", [P, 8, D])
        bias = sb("bias", [P, NA_HEADS, 6, GRID_W])
        vec = sb("vec", [P, N_VEC])
        adab = sb("adab", [P, LAYERS * 48])
        cond = sb("cond", [P, KC, 2])
        mod = sb("mod", [P, LAYERS, 48, 2])
        mod_rows = sb("mod_rows", [96, P])
        rw = sb("rw", [P, KC, N_EXP])
        rbias = sb("rbias", [P, N_EXP])
        lam = sb("lam", [P, 8])
        subln = sb("subln", [P, 1])
        stat = sb("stat", [P, 4, 4 * DIFF_HEADS])
        att = sb("att", [P, 4, 8])
        ones = sb("ones", [P, P])
        zeros = sb("zeros", [P, N_EXP])
        wts = sb("wts", [P, 2, TILES])
        slot_tab = sb("slot_tab", [P, 2 * BLK_COLS])
        slot_idx = sb("slot_idx", [P, 2 * BLK_COLS], I32)
        plan = sb("plan", [1, BLK_COLS + 1], I32)
        gather_idx = sb("gather_idx", [P, 1], I32)
        scatter_idx = sb("scatter_idx", [P, 1], I32)
        ps = stack.enter_context(nc.psum_tensor("ps", [P, 8, 512], F32))

        vec_rows = val[:, 1, 0:P]
        adab_rows = val[:, 2, 0:P]
        lam_in = val[:, 3, 0:4 * HD].rearrange("p (a b) -> p a b", b=HD)

        blk_in = qT[:, 0:2, :].rearrange("p a b -> p (a b)")
        blk_inT = qT[:, 2:4, :].rearrange("p a b -> p (a b)").rearrange("p (k t) -> p k t", t=P)
        blk_silu = qT[:, 4, :]
        blk_act = qT[:, 5, :]
        blk_actT = qT[:, 6, :].rearrange("p (k t) -> p k t", t=P)
        blk_out = kT[:, 0:2, :].rearrange("p a b -> p (a b)")

        oh_slot = kT[:, 2:4, :].rearrange("p a b -> p (a b)").rearrange("p (q s) -> p q s", s=P)
        oh_blk = kT[:, 4, 0:8 * 2 * BLK_COLS].rearrange("p (q s) -> p q s", s=2 * BLK_COLS)
        rt = kT[:, 5:7, :].rearrange("p a b -> p (a b)").rearrange("p (i w) -> p i w", w=TILES * N_EXP)
        plan_f = kT[0:1, 7, 0:BLK_COLS * N_EXP]

        h_dram = [nc.dram_tensor(f"h_rows_{l}", [TILES * P, D], F32).ap() for l in range(LAYERS)]
        y_dram = [nc.dram_tensor(f"expert_rows_{l}", [2 * TILES * P, D], F32).ap() for l in range(LAYERS)]
        mod_dram = [nc.dram_tensor(f"mod_rows_{l}", [96, P], F32) for l in range(LAYERS)]

        def const(name, n=None):
            lo, hi = CONST_AT[name]
            return cst[:, lo:hi]

        ident = const("ident")

        s_small = sem("small_loaded")
        s_x = sem("streams_loaded")
        s_bias = sem("bias_loaded")
        s_bias_done = sem("bias_masked")
        s_set = sem("fills_done")
        s_vec_t = sem("vectors_turned")
        s_vec = sem("vectors_copied")
        s_cond = sem("cond_ready")
        s_lam = sem("lambda_steps")
        s_lam_exp = sem("lambda_exps")
        s_v = sem("vector_steps")
        s_ada = [sem(f"ada_strips_used_{l}") for l in range(LAYERS)]
        s_mod = sem("mod_ready")
        s_modT = sem("mod_turned")
        s_modR = sem("mod_rows_copied")
        s_modD = sem("mod_rows_stored")
        s_rows = sem("rows_loaded")
        s_sq = [sem(f"squares_{i}") for i in range(5)]
        s_ms = [sem(f"mean_squares_{i}") for i in range(5)]
        s_rt = [sem(f"roots_{i}") for i in range(5)]
        s_xn = [sem(f"normalised_{l}") for l in range(LAYERS)]
        s_ht = [[sem(f"h_turned_{l}_{s}") for s in range(2)] for l in range(LAYERS)]
        s_he = [[sem(f"h_modulated_{l}_{s}") for s in range(2)] for l in range(LAYERS)]
        s_qm = [sem(f"qkv_products_{l}") for l in range(LAYERS)]
        s_qeA = [sem(f"qkv_copied_act_{l}") for l in range(LAYERS)]
        s_qeD = [sem(f"qkv_copied_dve_{l}") for l in range(LAYERS)]
        s_qt = [sem(f"qk_turned_{l}") for l in range(LAYERS)]
        s_qc = [sem(f"qk_turned_copied_{l}") for l in range(LAYERS)]
        s_sc = [sem(f"scores_{l}") for l in range(LAYERS)]
        s_nm = [sem(f"maxima_{l}") for l in range(LAYERS)]
        s_ex = [sem(f"exps_{l}") for l in range(LAYERS)]
        s_pr = sem("diff_probs")
        s_pt = [sem(f"probs_turned_{l}") for l in range(LAYERS)]
        s_pc = [sem(f"probs_turned_copied_{l}") for l in range(LAYERS)]
        s_pv = [sem(f"attended_{l}") for l in range(LAYERS)]
        s_oe = [sem(f"attended_copied_{l}") for l in range(LAYERS)]
        s_on = sem("heads_normalised")
        s_ot = [sem(f"o_turned_{l}") for l in range(LAYERS)]
        s_oc = [sem(f"o_turned_copied_{l}") for l in range(LAYERS)]
        s_wm = [sem(f"wo_products_{l}") for l in range(LAYERS)]
        s_we = [sem(f"wo_added_{l}") for l in range(LAYERS)]
        s_h = [sem(f"h2_ready_{l}") for l in range(LAYERS)]
        s_hst = [sem(f"h2_stored_{l}") for l in range(LAYERS)]
        s_h2t = [sem(f"h2_turned_{l}") for l in range(LAYERS)]
        s_h2A = [sem(f"h2_turned_copied_act_{l}") for l in range(LAYERS)]
        s_h2D = [sem(f"h2_turned_copied_dve_{l}") for l in range(LAYERS)]
        s_lg = [sem(f"logits_{l}") for l in range(LAYERS)]
        s_le = [sem(f"logit_exps_{l}") for l in range(LAYERS)]
        s_ch = [sem(f"choices_{l}") for l in range(LAYERS)]
        s_rk = [sem(f"ranks_{l}") for l in range(LAYERS)]
        s_oh = [sem(f"slot_marks_{l}") for l in range(LAYERS)]
        s_tab = [sem(f"slot_table_{l}") for l in range(LAYERS)]
        s_idx = [sem(f"plan_ready_{l}") for l in range(LAYERS)]
        m_wl = [[sem(f"expert_{w}_loaded_{l}") for w in ("gate", "up", "down")] for l in range(LAYERS)]
        m_gt = [sem(f"block_gates_{l}") for l in range(LAYERS)]
        m_up = [sem(f"block_ups_{l}") for l in range(LAYERS)]
        m_dn = [sem(f"block_downs_{l}") for l in range(LAYERS)]
        m_xt = [sem(f"block_in_turned_{l}") for l in range(LAYERS)]
        m_xA = [sem(f"block_in_copied_act_{l}") for l in range(LAYERS)]
        m_xD = [sem(f"block_in_copied_dve_{l}") for l in range(LAYERS)]
        m_si = [sem(f"block_silu_{l}") for l in range(LAYERS)]
        m_ac = [sem(f"block_act_{l}") for l in range(LAYERS)]
        m_at = [sem(f"block_act_turned_{l}") for l in range(LAYERS)]
        m_ae = [sem(f"block_act_turned_copied_{l}") for l in range(LAYERS)]
        m_yA = [sem(f"block_out_act_{l}") for l in range(LAYERS)]
        m_yD = [sem(f"block_out_dve_{l}") for l in range(LAYERS)]
        m_ix = [sem(f"block_indices_{l}") for l in range(LAYERS)]
        m_ga = [sem(f"block_gathered_{l}") for l in range(LAYERS)]
        m_sc = [sem(f"block_scattered_{l}") for l in range(LAYERS)]
        s_yl = [[sem(f"expert_rows_loaded_{l}_{b}") for b in range(2)] for l in range(LAYERS)]
        s_cb = [sem(f"combined_{l}") for l in range(LAYERS)]
        s_fg = sem("final_gain_loaded")
        s_fms, s_frt = sem("final_mean_squares"), sem("final_roots")
        s_turn = sem("pool_turns")
        s_fin = sem("final_ready")
        s_out = sem("out_stored")
        s_ld = [[sem(f"strip_loaded_{l}_{s}") for s in range(3)] for l in range(LAYERS)]

        QKV = [diff_w_qkv, na_w_qkv]
        WO = [diff_w_o, na_w_o]
        qkv_jobs, strips = [], []
        for l in range(LAYERS):
            jobs = [(g, t) for g in range(6) for t in (TILES_OF[l] if g < 2 else range(TILES))]
            qkv_jobs.append(jobs)
            plan_l = []
            if l == 0:
                plan_l += [(ada_w[0], j, s_ada[0], j + 1) for j in range(12)]
            for g in range(6):
                last = max(n for n, (gg, _) in enumerate(jobs) if gg == g)
                plan_l.append((QKV[l][0], g, s_qm[l], last + 1))
            if l == 0:
                plan_l += [(ada_w[1], j, s_ada[1], j + 1) for j in range(12)]
            plan_l += [(WO[l][0], j, s_wm[l], 2 * len(TILES_OF[l]) - 1 + j) for j in range(2)]
            strips.append(plan_l)
        FIRST = {("ada", 0): 0, ("qkv", 0): 12, ("ada", 1): 18, ("wo", 0): 30, ("qkv", 1): 0, ("wo", 1): 6}

        def strip(l, j):
            return ring[:, j % 3]

        def wait_strip(eng, l, j):
            eng.wait_ge(s_ld[l][j % 3], 16 * (j // 3 + 1))

        qkv_copy, qk_index = [], []
        for l in range(LAYERS):
            n_act = n_dve = n_qk = 0
            copies, index = [], []
            for g, t in qkv_jobs[l]:
                if l == 0 and g < 4 and t >= CTX_TILES:
                    n_dve += 1
                    copies.append(("dve", s_qeD[l], n_dve))
                else:
                    n_act += 1
                    copies.append(("act", s_qeA[l], n_act))
                index.append(n_qk if g < 4 else None)
                n_qk += g < 4
            qkv_copy.append(copies)
            qk_index.append(index)
        N_QK = [sum(i is not None for i in qk_index[l]) for l in range(LAYERS)]

        units = [[(t, h) for t in TILES_OF[0] for h in range(DIFF_HEADS)],
                 [(t, h) for t in TILES_OF[1] for h in range(NA_HEADS)]]

        def key_tiles(t):
            return CTX_TILES if t < CTX_TILES else TILES

        NT = [len(t) for t in TILES_OF]
        HALF = D // 2
        VECTOR_LOADS = 7
        SMALL_LOADS_ALL = VECTOR_LOADS + 6
        block = stack.enter_context(nc.Block())

        @block.sync
        def _(sp):
            def small(dst, src):
                sp.dma_start(dst, src).then_inc(s_small, 16)

            small(cst[:], consts)
            small(vec_rows[8:16, :], c.rearrange("a (r p) -> (a r) p", p=P))
            small(vec_rows[0:8, :], c_ctx.rearrange("(r p) -> r p", p=P))
            small(vec_rows[16:32, :], norm1_g.rearrange("l (r p) -> (l r) p", p=P))
            small(vec_rows[32:48, :], norm2_g.rearrange("l (r p) -> (l r) p", p=P))
            small(vec_rows[48:49, :], diff_subln_g)
            small(adab_rows[0:96, :], ada_b.rearrange("l (r p) -> (l r) p", p=P))

            def load_strip(l, j):
                src, g, _, _ = strips[l][j]
                if j >= 3:
                    _, _, used, value = strips[l][j - 3]
                    sp.wait_ge(used, value)
                sp.dma_start(strip(l, j), src.rearrange("(k p) n -> p k n", p=P)[:, :, g * STRIP:(g + 1) * STRIP]) \
                    .then_inc(s_ld[l][j % 3], 16)

            for j in range(2):
                load_strip(0, j)
            sp.dma_start(resid[:, 0:CTX_TILES], ctx.rearrange("a (t p) d -> p (a t) d", p=P)).then_inc(s_x, 16)
            sp.dma_start(resid[:, CTX_TILES:TILES], x.rearrange("a (t p) d -> p (a t) d", p=P)).then_inc(s_x, 16)
            load_strip(0, 2)
            for i, v in enumerate((diff_lambda_q1, diff_lambda_k1, diff_lambda_q2, diff_lambda_k2)):
                small(lam_in[:, i, :], v.broadcast_to([P, HD]))
            small(rbias[:], router_bias.partition_broadcast(P))
            small(rw[:], router_w.rearrange("(k p) e -> p k e", p=P))

            def load_rows(l, targets):
                for slot, piece, s in targets:
                    src = bass.AP(mod_dram[l], (piece * KC * 2 + s) * P, [[0, P], [2 * P, KC], [1, P]])
                    sp.dma_start(rows[:, slot].rearrange("p (k n) -> p k n", n=P), src).then_inc(s_rows, 16)

            for j in range(3, 15):
                load_strip(0, j)
            sp.wait_ge(s_modR, 1)
            sp.dma_start(mod_dram[0].ap(), mod_rows[:]).then_inc(s_modD, 16)
            for j in range(15, 18):
                load_strip(0, j)
            sp.wait_ge(s_modD, 16)
            load_rows(0, [(2 * i + s, piece, s) for i, piece in enumerate((2, 3, 4, 5)) for s in range(2)])
            for par in range(2):
                for h in range(NA_HEADS):
                    src = bass.AP(na_rpb.tensor, h * RPB_H * RPB_W + (NA_WR - 1 - 2 - par) * RPB_W + NA_WC - GRID_W,
                                  [[1, GRID_W], [RPB_W, 6], [1, GRID_W]])
                    sp.dma_start(bias[par * GRID_W:(par + 1) * GRID_W, h], src).then_inc(s_bias, 16)
            for j in range(18, len(strips[0])):
                load_strip(0, j)
            sp.wait_ge(s_modR, 2)
            sp.dma_start(mod_dram[1].ap(), mod_rows[:]).then_inc(s_modD, 16)

            def store_h(l):
                for n, t in enumerate(TILES_OF[l]):
                    sp.wait_ge(s_h[l], n + 1)
                    sp.dma_start(h_dram[l][n * P:(n + 1) * P, :], tokm[:, t]).then_inc(s_hst[l], 16)

            def load_experts(l):
                sp.wait_ge(s_wm[l], 2 * NT[l])
                sp.wait_ge(s_idx[l], 1)
                n = sp.value_load(plan[0:1, BLK_COLS:BLK_COLS + 1], min_val=1, max_val=MAX_BLOCKS)
                gate = moe_w_gate[l].rearrange("e (k p) n -> e p k n", p=P)
                up = moe_w_up[l].rearrange("e (k p) n -> e p k n", p=P)
                down = moe_w_down[l].rearrange("e (k p) n -> e p k n", p=P)
                with sp.Fori(0, n) as i:
                    e = sp.value_load(plan[0:1, bass.ds(i, 1)], min_val=0, max_val=N_EXP - 1)
                    sp.wait_ge(m_gt[l], i + 1)
                    sp.dma_start(ring[:, 0], gate[bass.ds(e, 1)].rearrange("a p k n -> p (a k) n")).then_inc(m_wl[l][0], 16)
                    sp.wait_ge(m_up[l], i + 1)
                    sp.dma_start(ring[:, 1], up[bass.ds(e, 1)].rearrange("a p k n -> p (a k) n")).then_inc(m_wl[l][1], 16)
                    sp.wait_ge(m_dn[l], i * 2 + 2)
                    sp.dma_start(ring[:, 2].rearrange("p k n -> p (k n)").rearrange("p (k n) -> p k n", n=D),
                                 down[bass.ds(e, 1)].rearrange("a p k n -> p (a k) n")).then_inc(m_wl[l][2], 16)
                return n

            def load_expert_rows(l, n):
                sp.wait_ge(m_sc[l], n * 16 + 16)
                for m, t in enumerate(TILES_OF[l]):
                    if m >= 2:
                        sp.wait_ge(s_cb[l], m - 1)
                    for k in range(2):
                        src = y_dram[l][k * TILES * P + m * P:k * TILES * P + (m + 1) * P, :]
                        sp.dma_start(val[:, 2 * (m % 2) + k], src).then_inc(s_yl[l][m % 2], 16)

            store_h(0)
            sp.wait_ge(s_modD, 32)
            load_rows(1, [(i, piece, 1) for i, piece in enumerate((2, 3, 4))])
            n0 = load_experts(0)
            sp.wait_ge(m_dn[0], n0 * 2 + 2)
            for j in range(3):
                load_strip(1, j)
            load_expert_rows(0, n0)
            sp.wait_ge(s_cb[0], NT[0])
            load_rows(1, [(3, 5, 1)])
            sp.dma_start(rows[:, 4], final_norm_g.partition_broadcast(P)).then_inc(s_fg, 16)
            for j in range(3, len(strips[1])):
                load_strip(1, j)
            store_h(1)
            n1 = load_experts(1)
            load_expert_rows(1, n1)
            for m, t in enumerate(TILES_OF[1]):
                sp.wait_ge(s_fin, m + 1)
                sp.dma_start(out[0, m * P:(m + 1) * P, :], tokm[:, t]).then_inc(s_out, 16)
            sp.wait_ge(s_out, 16 * NT[1])

        @block.gpsimd
        def _(pool):
            def in_turn():
                pool.sem_inc(s_turn, 1)

            pool.memset(ones[:], 1.0).then_inc(s_set, 1)
            pool.memset(zeros[:], 0.0).then_inc(s_set, 1)
            pool.wait_ge(s_small, 16 * SMALL_LOADS_ALL)
            pool.wait_ge(s_bias, 16 * 2 * NA_HEADS)
            table = bias[:].rearrange("p h r c -> p (h r) c")
            valid = const("valid").unsqueeze(1).to_broadcast([P, NA_HEADS * 6, GRID_W])
            invalid = const("invalid").unsqueeze(1).to_broadcast([P, NA_HEADS * 6, GRID_W])
            pool.tensor_tensor(table, table, valid, ALU.mult).then_inc(s_bias_done, 1)
            pool.wait_ge(s_bias_done, 1)
            pool.tensor_tensor(table, table, invalid, ALU.add).then_inc(s_bias_done, 1)

            for l in range(LAYERS):
                rows_l = NT[l] * P
                pool.wait_ge(s_idx[l], 1)
                n = pool.value_load(plan[0:1, BLK_COLS:BLK_COLS + 1], min_val=1, max_val=MAX_BLOCKS)
                last_row, last_made = pool.to_reg(rows_l - 1), pool.to_reg(2 * TILES * P - 1)
                pool.memset(blk_in, 0.0).then_inc(m_ix[l], 1)
                pool.wait_ge(m_ix[l], 1)
                pool.tensor_copy(gather_idx[:], slot_idx[:, 0:1]).then_inc(m_ix[l], 1)
                pool.wait_ge(m_ix[l], 2)
                pool.wait_ge(s_hst[l], 16 * NT[l])
                pool.indirect_dma_start(blk_in, None, h_dram[l][0:rows_l], bass.IndirectOffsetOnAxis(ap=gather_idx[:], axis=0),
                                        bounds_check=last_row, oob_is_err=False).then_inc(m_ga[l], 16)
                pool.memset(blk_out, 0.0).then_inc(m_ix[l], 1)
                pool.tensor_copy(scatter_idx[:], slot_idx[:, 2 * BLK_COLS - 1:]).then_inc(m_ix[l], 1)
                pool.wait_ge(m_ix[l], 4)
                pool.indirect_dma_start(y_dram[l], bass.IndirectOffsetOnAxis(ap=scatter_idx[:], axis=0), blk_out, None,
                                        bounds_check=last_made, oob_is_err=False).then_inc(m_sc[l], 16)
                with pool.Fori(0, n) as i:
                    pool.wait_ge(m_ga[l], i * 16 + 16)
                    pool.wait_ge(m_xt[l], i * 2 + 2)
                    in_turn()
                    pool.tensor_copy(gather_idx[:], slot_idx[:, bass.ds(i + 1, 1)]).then_inc(m_ix[l], 1)
                    pool.wait_ge(m_ix[l], i * 2 + 5)
                    in_turn()
                    pool.indirect_dma_start(blk_in, None, h_dram[l][0:rows_l],
                                            bass.IndirectOffsetOnAxis(ap=gather_idx[:], axis=0),
                                            bounds_check=last_row, oob_is_err=False).then_inc(m_ga[l], 16)
                    pool.wait_ge(m_sc[l], i * 16 + 16)
                    in_turn()
                    pool.tensor_copy(scatter_idx[:], slot_idx[:, bass.ds(i + BLK_COLS, 1)]).then_inc(m_ix[l], 1)
                    pool.wait_ge(m_ix[l], i * 2 + 6)
                    pool.wait_ge(m_yA[l], i + 2)
                    pool.wait_ge(m_yD[l], i + 2)
                    in_turn()
                    pool.indirect_dma_start(y_dram[l], bass.IndirectOffsetOnAxis(ap=scatter_idx[:], axis=0), blk_out, None,
                                            bounds_check=last_made, oob_is_err=False).then_inc(m_sc[l], 16)

        @block.scalar
        def _(act):
            def square_rows(i, n, t, src, dst):
                act.activation(dst, src, ACT.Square, accum_out=stat[:, 0, t:t + 1]).then_inc(s_sq[i], 1)

            act.wait_ge(s_vec, 1)
            for s in range(2):
                act.activation(cond[:, :, s], vec[:, 8 * s:8 * s + 8], ACT.Silu).then_inc(s_cond, 1)
            act.wait_ge(s_lam, 1)
            act.activation(lam[:, 2:4], lam[:, 0:2], ACT.Exp).then_inc(s_lam_exp, 1)

            for l in range(LAYERS):
                if l == 0:
                    act.wait_ge(s_x, 32)
                    for n, t in enumerate(range(TILES)):
                        square_rows(0, n, t, resid[:, t], tokm[:, t])
                else:
                    for n, t in enumerate(range(TILES)):
                        act.wait_ge(s_cb[0], t + 1)
                        square_rows(2, n, t, resid[:, t], tokm[:, t])
                i = 2 * l
                act.wait_ge(s_ms[i], 1)
                act.activation(stat[:, 2, 0:TILES], stat[:, 1, 0:TILES], ACT.Sqrt).then_inc(s_rt[i], 1)

                act.wait_ge(s_mod, l + 1)
                for k in range(KC):
                    act.wait_ge(s_ht[l][0], k + 1)
                    act.activation(hT[:, k, 0:CTX], ps[:, k % 2, 0:CTX], ACT.Identity, bias=mod[:, l, k, 0:1],
                                   scale=mod[:, l, KC + k, 0:1]).then_inc(s_he[l][0], 1)

                def copy_turned(m, g, t):
                    act.wait_ge(s_qt[l], m + 1)
                    dst = (qT if g < 2 else kT)[:, 4 * (g % 2):4 * (g % 2) + 4, t * P:(t + 1) * P]
                    act.copy(dst, ps[:, 4 + m % 2].rearrange("p (k t) -> p k t", t=P)).then_inc(s_qc[l], 1)

                last = None
                for n, (g, t) in enumerate(qkv_jobs[l]):
                    if qkv_copy[l][n][0] == "act":
                        m = qk_index[l][n]
                        act.wait_ge(s_qm[l], n + 1)
                        if m is None:
                            dst = val[:, t, (g - 4) * STRIP:(g - 3) * STRIP]
                        else:
                            if m >= 2:
                                act.wait_ge(s_qt[l], m - 1)
                            dst = tokm[:, 0, (m % 2) * STRIP:(m % 2 + 1) * STRIP]
                        act.activation(dst, ps[:, n % 2], ACT.Copy,
                                       scale=SCALE if l == 1 and g < 2 else 1.0).then_inc(s_qeA[l], 1)
                    if last is not None:
                        copy_turned(*last)
                    last = (qk_index[l][n], g, t) if g < 4 else None
                if last is not None:
                    copy_turned(*last)

                if l == 0:
                    def copy_probs(u):
                        t, h = units[0][u]
                        nk = key_tiles(t) * P
                        act.wait_ge(s_pt[0], u + 1)
                        if u >= 2:
                            act.wait_ge(s_pv[0], u - 1)
                        act.copy(hT[:, 4 + u % 2, 0:nk], ps[:, (4, 7)[u % 2], 0:nk]).then_inc(s_pc[0], 1)

                    def copy_out(u):
                        t, h = units[0][u]
                        act.wait_ge(s_pv[0], u + 1)
                        act.copy(tokm[:, t, h * 2 * HD:(h + 1) * 2 * HD], ps[:, 5, 0:2 * HD]).then_inc(s_oe[0], 1)

                    for u, (t, h) in enumerate(units[0]):
                        nk = key_tiles(t) * P
                        for cc in range(2):
                            act.wait_ge(s_nm[0], 2 * u + cc + 1)
                            if u >= 2:
                                act.wait_ge(s_pt[0], u - 1)
                            act.activation(hT[:, 2 * (u % 2) + cc, 0:nk], ps[:, 2 * (u % 2) + cc, 0:nk], ACT.Exp,
                                           bias=att[:, u % 2, 2 + cc:3 + cc], scale=SCALE,
                                           accum_out=att[:, u % 2, 4 + cc:5 + cc]).then_inc(s_ex[0], 1)
                        if u >= 1:
                            copy_probs(u - 1)
                        if u >= 2:
                            copy_out(u - 2)
                    U = len(units[0])
                    copy_probs(U - 1)
                    copy_out(U - 2)
                    copy_out(U - 1)
                    act.wait_ge(s_ms[4], 1)
                    act.activation(stat[:, 2], stat[:, 1], ACT.Sqrt).then_inc(s_rt[4], 1)
                else:
                    def copy_probs1(u):
                        act.wait_ge(s_pt[1], u + 1)
                        if u >= 2:
                            act.wait_ge(s_pv[1], u - 1)
                        act.copy(hT[:, 4 + u % 2], ps[:, (4, 7)[u % 2]]).then_inc(s_pc[1], 1)

                    U = len(units[1])
                    for u, (t, h) in enumerate(units[1]):
                        act.wait_ge(s_nm[1], u + 1)
                        if u >= 4:
                            act.wait_ge(s_pt[1], u - 3)
                        act.activation(hT[:, u % 4], ps[:, u % 4], ACT.Exp, bias=att[:, u % 4, 1:2],
                                       accum_out=att[:, u % 4, 2:3]).then_inc(s_ex[1], 1)
                        if u >= 2:
                            copy_probs1(u - 2)
                    copy_probs1(U - 2)
                    copy_probs1(U - 1)

                def turned_out(m):
                    t = TILES_OF[l][m]
                    if l == 0 and m == 0:
                        act.wait_ge(s_lam, 3)
                    for hf in range(2):
                        act.wait_ge(s_ot[l], 2 * m + hf + 1)
                        dst = hT[:, 4 * hf:4 * hf + 4, t * P:(t + 1) * P]
                        src = ps[:, 4 + hf].rearrange("p (k t) -> p k t", t=P)
                        if l == 0:
                            act.activation(dst, src, ACT.Copy, scale=subln[:, 0:1]).then_inc(s_oc[l], 1)
                        else:
                            act.copy(dst, src).then_inc(s_oc[l], 1)

                def norm2(m):
                    t = TILES_OF[l][m]
                    i = 2 * l + 1
                    act.wait_ge(s_we[l], 2 * m + 2)
                    act.wait_ge(s_ot[l], 2 * m + 2)
                    square_rows(i, m, t, resid[:, t], tokm[:, t])
                    act.wait_ge(s_ms[i], m + 1)
                    act.activation(stat[:, 2, t:t + 1], stat[:, 1, t:t + 1], ACT.Sqrt).then_inc(s_rt[i], 1)

                def turned_h(m):
                    t = TILES_OF[l][m]
                    act.wait_ge(s_h2t[l], 2 * m + 1)
                    act.copy(hT[:, 0:4, t * P:(t + 1) * P],
                             ps[:, 2].rearrange("p (k t) -> p k t", t=P)).then_inc(s_h2A[l], 1)

                for m in range(NT[l]):
                    turned_out(m)
                    if m >= 1:
                        norm2(m - 1)
                        turned_h(m - 1)
                norm2(NT[l] - 1)
                turned_h(NT[l] - 1)

                act.wait_ge(s_lg[l], NT[l])
                act.activation(rt[:, 0, 0:NT[l] * N_EXP], ps[:, 6, 0:NT[l] * N_EXP], ACT.Exp, scale=-1.0).then_inc(s_le[l], 1)

                act.wait_ge(s_idx[l], 1)
                n = act.value_load(plan[0:1, BLK_COLS:BLK_COLS + 1], min_val=1, max_val=MAX_BLOCKS)
                act.sem_inc(m_yA[l], 1)
                act.wait_ge(m_xt[l], 1)
                act.copy(blk_inT[:, 0:4], ps[:, 2].rearrange("p (k t) -> p k t", t=P)).then_inc(m_xA[l], 1)
                with act.Fori(0, n) as i:
                    act.wait_ge(m_gt[l], i + 2)
                    act.wait_ge(m_ac[l], i + 1)
                    act.activation(blk_silu, ps[:, 0], ACT.Silu).then_inc(m_si[l], 1)
                    act.wait_ge(m_xt[l], i * 2 + 3)
                    act.copy(blk_inT[:, 0:4], ps[:, 2].rearrange("p (k t) -> p k t", t=P)).then_inc(m_xA[l], 1)
                    act.wait_ge(m_at[l], i + 2)
                    act.copy(blk_actT, ps[:, 4].rearrange("p (k t) -> p k t", t=P)).then_inc(m_ae[l], 1)
                    act.wait_ge(m_dn[l], i * 2 + 3)
                    act.wait_ge(m_sc[l], i * 16 + 16)
                    act.copy(blk_out[:, 0:HALF], ps[:, 5]).then_inc(m_yA[l], 1)

            for m, t in enumerate(TILES_OF[1]):
                act.wait_ge(s_cb[1], m + 1)
                act.activation(tokm[:, t], resid[:, t], ACT.Square, accum_out=stat[:, 0, t:t + 1]).then_inc(s_sq[4], 1)
            act.wait_ge(s_fms, 1)
            act.activation(stat[:, 2, 0:TILES], stat[:, 1, 0:TILES], ACT.Sqrt).then_inc(s_frt, 1)

        @block.vector
        def _(dve):
            steps = [0]

            def step(ins):
                steps[0] += 1
                ins.then_inc(s_v, 1)
                dve.wait_ge(s_v, steps[0])

            def sync(ins, s, counts={}):
                counts[s.name] = counts.get(s.name, 0) + 1
                ins.then_inc(s, 1)
                dve.wait_ge(s, counts[s.name])

            tt, ts, stt = dve.tensor_tensor, dve.tensor_scalar, dve.scalar_tensor_tensor

            dve.wait_ge(s_vec_t, 2)
            sync(dve.tensor_copy(vec[:], ps[:, 7, 0:N_VEC]), s_vec)
            step(dve.tensor_copy(adab[:], ps[:, 7, P:P + 96]))
            dve.wait_ge(s_small, 16 * SMALL_LOADS_ALL)
            step(tt(val[:, 0, 0:2 * HD].rearrange("p (a b) -> p a b", b=HD), lam_in[:, 0::2, :], lam_in[:, 1::2, :], ALU.mult))
            sync(dve.tensor_reduce(lam[:, 0:2], val[:, 0, 0:2 * HD].rearrange("p (a b) -> p a b", b=HD), X_AXIS, ALU.add), s_lam)
            dve.wait_ge(s_lam_exp, 1)
            step(tt(lam[:, 4:5], lam[:, 3:4], lam[:, 2:3], ALU.subtract))
            sync(ts(lam[:, 5:6], lam[:, 4:5], -LAMBDA_INIT, None, ALU.add), s_lam)
            sync(ts(subln[:], vec[:, 48:49], 1.0 - LAMBDA_INIT, None, ALU.mult), s_lam)

            def mean_square(dst, src, n):
                return ts(dst, src, 1.0 / n, EPS, ALU.mult, ALU.add)

            def modulation(l):
                b = adab[:, 48 * l:48 * l + 48].unsqueeze(2).to_broadcast([P, 48, 2])
                step(tt(mod[:, l], ps[:, 6, 0:96].rearrange("p (j s) -> p j s", s=2), b, ALU.add))
                n1 = vec[:, 16 + 8 * l:24 + 8 * l].unsqueeze(2).to_broadcast([P, KC, 2])
                n2 = vec[:, 32 + 8 * l:40 + 8 * l].unsqueeze(2).to_broadcast([P, KC, 2])
                step(stt(mod[:, l, 8:16], mod[:, l, 8:16], 1.0, n1, ALU.add, ALU.mult))
                sync(stt(mod[:, l, 32:40], mod[:, l, 32:40], 1.0, n2, ALU.add, ALU.mult), s_mod)

            def modulation_rows(l):
                dve.wait_ge(s_modT, l + 1)
                dve.tensor_copy(mod_rows[:], ps[0:96, 7, 0:P]).then_inc(s_modR, 1)

            for l in range(LAYERS):
                i = 2 * l
                dve.wait_ge(s_sq[i], TILES)
                sync(mean_square(stat[:, 1, 0:TILES], stat[:, 0, 0:TILES], D), s_ms[i])
                dve.wait_ge(s_rt[i], 1)
                step(dve.reciprocal(stat[:, 3, 0:TILES], stat[:, 2, 0:TILES]))
                for t in range(TILES):
                    ts(tokm[:, t], resid[:, t], stat[:, 3, t:t + 1], None, ALU.mult).then_inc(s_xn[l], 1)
                if l == 0:
                    dve.wait_ge(s_ada[0], 12)
                    modulation(0)
                    modulation_rows(0)
                for k in range(KC):
                    dve.wait_ge(s_ht[l][1], k + 1)
                    ts(hT[:, k, CTX:CTX + SEQ], ps[:, 2 + k % 2, 0:SEQ], mod[:, l, KC + k, 1:2], mod[:, l, k, 1:2],
                       ALU.mult, ALU.add).then_inc(s_he[l][1], 1)

                for n, (g, t) in enumerate(qkv_jobs[l]):
                    if qkv_copy[l][n][0] != "dve":
                        continue
                    m = qk_index[l][n]
                    dve.wait_ge(s_qm[l], n + 1)
                    lo = CONST_AT["cos"][0] + 32 * (t - CTX_TILES)
                    cos = cst[:, lo:lo + 32].unsqueeze(1).to_broadcast([P, 16, 32])
                    lo = CONST_AT["sin"][0] + 32 * (t - CTX_TILES)
                    sin = cst[:, lo:lo + 32].unsqueeze(1).to_broadcast([P, 16, 32])
                    src = ps[:, n % 2].rearrange("p (a b) -> p a b", b=32)
                    by_cos = tokm[:, 1, 0:STRIP].rearrange("p (a b) -> p a b", b=32)
                    by_sin = tokm[:, 1, STRIP:2 * STRIP].rearrange("p (a b) -> p a b", b=32)
                    step(tt(by_cos, src, cos, ALU.mult))
                    step(tt(by_sin, src, sin, ALU.mult))
                    if m >= 2:
                        dve.wait_ge(s_qt[l], m - 1)
                    dst = tokm[:, 0, (m % 2) * STRIP:(m % 2 + 1) * STRIP].rearrange("p (a b) -> p a b", b=32)
                    step(tt(dst[:, 0::2], by_cos[:, 0::2], by_sin[:, 1::2], ALU.subtract))
                    sync(tt(dst[:, 1::2], by_cos[:, 1::2], by_sin[:, 0::2], ALU.add), s_qeD[l])

                if l == 0:
                    def head_squares(m):
                        dve.wait_ge(s_oe[0], DIFF_HEADS * (m + 1))
                        o, sq = [a.rearrange("p (h d) -> p h d", d=2 * HD) for a in
                                 (tokm[:, m], hT[:, 6:8].rearrange("p a b -> p (a b)"))]
                        step(tt(sq, o, o, ALU.mult))
                        step(dve.tensor_reduce(stat[:, 0, 8 * m:8 * m + 8], sq, X_AXIS, ALU.add))

                    for u, (t, h) in enumerate(units[0]):
                        nk = key_tiles(t) * P
                        a = att[:, u % 2]
                        for cc in range(2):
                            dve.wait_ge(s_sc[0], 2 * u + cc + 1)
                            step(dve.tensor_reduce(a[:, cc:cc + 1], ps[:, 2 * (u % 2) + cc, 0:nk], X_AXIS, ALU.max))
                            ts(a[:, 2 + cc:3 + cc], a[:, cc:cc + 1], -SCALE, None, ALU.mult).then_inc(s_nm[0], 1)
                        dve.wait_ge(s_ex[0], 2 * u + 2)
                        step(dve.reciprocal(a[:, 6:8], a[:, 4:6]))
                        step(tt(a[:, 7:8], a[:, 7:8], lam[:, 5:6], ALU.mult))
                        p0, p1 = hT[:, 2 * (u % 2), 0:nk], hT[:, 2 * (u % 2) + 1, 0:nk]
                        step(ts(p1, p1, a[:, 7:8], None, ALU.mult))
                        stt(p0, p0, a[:, 6:7], p1, ALU.mult, ALU.add).then_inc(s_pr, 1)
                        if u % DIFF_HEADS == 3 and u > DIFF_HEADS:
                            head_squares(u // DIFF_HEADS - 1)
                    head_squares(TILES - 1)
                    sync(mean_square(stat[:, 1], stat[:, 0], 2 * HD), s_ms[4])
                    dve.wait_ge(s_rt[4], 1)
                    step(dve.reciprocal(stat[:, 3], stat[:, 2]))
                    for m in range(TILES):
                        o = tokm[:, m].rearrange("p (h d) -> p h d", d=2 * HD)
                        r = stat[:, 3, 8 * m:8 * m + 8].unsqueeze(2).to_broadcast([P, DIFF_HEADS, 2 * HD])
                        tt(o, o, r, ALU.mult).then_inc(s_on, 1)
                    dve.wait_ge(s_ada[1], 12)
                    modulation(1)
                    modulation_rows(1)
                else:
                    dve.wait_ge(s_bias_done, 2)

                    def scale_out(u):
                        t, h = units[1][u]
                        step(dve.reciprocal(att[:, u % 4, 3:4], att[:, u % 4, 2:3]))
                        dve.wait_ge(s_pv[1], u + 1)
                        ts(tokm[:, t, h * HD:(h + 1) * HD], ps[:, 5 + u % 2, 0:HD], att[:, u % 4, 3:4], None,
                           ALU.mult).then_inc(s_oe[1], 1)

                    for u, (t, h) in enumerate(units[1]):
                        a = att[:, u % 4]
                        lo = 2 - 2 * (t - CTX_TILES)
                        dve.wait_ge(s_sc[1], u + 1)
                        loc = ps[:, u % 4, CTX:CTX + SEQ]
                        step(tt(loc, loc, bias[:, h, lo:lo + GRID_H].rearrange("p r c -> p (r c)"), ALU.add))
                        step(dve.tensor_reduce(a[:, 0:1], ps[:, u % 4], X_AXIS, ALU.max))
                        ts(a[:, 1:2], a[:, 0:1], -1.0, None, ALU.mult).then_inc(s_nm[1], 1)
                        if u >= 3:
                            scale_out(u - 3)
                    for u in range(len(units[1]) - 3, len(units[1])):
                        scale_out(u)

                if l == 0:
                    dve.wait_ge(s_rows, 16 * 8)
                else:
                    dve.wait_ge(s_rows, 16 * (8 + 4))

                def row(piece, t):
                    return rows[:, 2 * piece + (t >= CTX_TILES) if l == 0 else piece]

                def add_out(m, hf):
                    t = TILES_OF[l][m]
                    j = 2 * m + hf
                    cols = slice(hf * HALF, (hf + 1) * HALF)
                    dve.wait_ge(s_wm[l], j + 1)
                    step(tt(val[:, 0, cols], ps[:, j % 2], row(0, t)[:, cols], ALU.mult))
                    sync(tt(resid[:, t, cols], resid[:, t, cols], val[:, 0, cols], ALU.add), s_we[l])

                def norm2(m):
                    t = TILES_OF[l][m]
                    i = 2 * l + 1
                    dve.wait_ge(s_sq[i], m + 1)
                    sync(mean_square(stat[:, 1, t:t + 1], stat[:, 0, t:t + 1], D), s_ms[i])
                    dve.wait_ge(s_rt[i], m + 1)
                    step(dve.reciprocal(stat[:, 3, t:t + 1], stat[:, 2, t:t + 1]))
                    step(stt(tokm[:, t], resid[:, t], stat[:, 3, t:t + 1], row(2, t), ALU.mult, ALU.mult))
                    sync(tt(tokm[:, t], tokm[:, t], row(1, t), ALU.add), s_h[l])

                def turned_h(m):
                    t = TILES_OF[l][m]
                    dve.wait_ge(s_h2t[l], 2 * m + 2)
                    dve.tensor_copy(hT[:, 4:8, t * P:(t + 1) * P],
                                    ps[:, 3].rearrange("p (k t) -> p k t", t=P)).then_inc(s_h2D[l], 1)

                for m in range(NT[l]):
                    add_out(m, 0)
                    add_out(m, 1)
                    norm2(m)
                    turned_h(m)

                nt = NT[l]
                w = nt * N_EXP

                def r3(i, a=nt, b=N_EXP, off=0):
                    return rt[:, i, off:off + a * b].rearrange("p (a b) -> p a b", b=b)

                dve.wait_ge(s_le[l], 1)
                step(ts(rt[:, 0, 0:w], rt[:, 0, 0:w], 1.0, None, ALU.add))
                step(dve.reciprocal(rt[:, 1, 0:w], rt[:, 0, 0:w]))
                rb = rbias[:].unsqueeze(1).to_broadcast([P, nt, N_EXP])
                step(tt(r3(2), r3(1), rb, ALU.add))
                sel = r3(2, nt * N_GRP, GRP)
                hi, lo = r3(3, nt * N_GRP, 2), r3(4, nt * N_GRP, 2)
                step(tt(hi, sel[:, :, 0:2], sel[:, :, 2:4], ALU.max))
                step(tt(lo, sel[:, :, 0:2], sel[:, :, 2:4], ALU.min))
                g5, g6, g7 = rt[:, 5, 0:nt * N_GRP], rt[:, 6, 0:nt * N_GRP], rt[:, 7, 0:nt * N_GRP]
                step(tt(g5.unsqueeze(2), hi[:, :, 0:1], hi[:, :, 1:2], ALU.max))
                step(tt(g6.unsqueeze(2), hi[:, :, 0:1], hi[:, :, 1:2], ALU.min))
                step(tt(g7.unsqueeze(2), lo[:, :, 0:1], lo[:, :, 1:2], ALU.max))
                step(tt(g6, g6, g7, ALU.max))
                step(tt(g5, g5, g6, ALU.add))

                def first_best(dst, src, rev, a, b, tmp):
                    mx = rt[:, 15, 0:a]
                    step(dve.tensor_reduce(mx, src, X_AXIS, ALU.max))
                    step(tt(tmp, src, mx.unsqueeze(2).to_broadcast([P, a, b]), ALU.is_equal))
                    step(tt(tmp, tmp, rev.unsqueeze(1).to_broadcast([P, a, b]), ALU.mult))
                    step(dve.tensor_reduce(mx, tmp, X_AXIS, ALU.max))
                    step(tt(dst, tmp, mx.unsqueeze(2).to_broadcast([P, a, b]), ALU.is_equal))

                first_best(r3(6, nt, N_GRP), r3(5, nt, N_GRP), const("rev_group"), nt, N_GRP, r3(7, nt, N_GRP))
                step(ts(g7, g6, NEG, -NEG, ALU.mult, ALU.add))
                s4 = r3(3, nt * N_GRP, GRP)
                step(tt(s4, sel, g6.unsqueeze(2).to_broadcast([P, nt * N_GRP, GRP]), ALU.mult))
                step(tt(s4, s4, g7.unsqueeze(2).to_broadcast([P, nt * N_GRP, GRP]), ALU.add))
                first_best(r3(8), r3(3), const("rev_expert"), nt, N_EXP, r3(4))
                step(stt(rt[:, 3, 0:w], rt[:, 8, 0:w], -3.0 * NEG, rt[:, 3, 0:w], ALU.mult, ALU.add))
                first_best(r3(9), r3(3), const("rev_expert"), nt, N_EXP, r3(4))
                sync(tt(rt[:, 10, 0:w], rt[:, 8, 0:w], rt[:, 9, 0:w], ALU.add), s_ch[l])
                for k in range(2):
                    step(tt(r3(4), r3(1), r3(8 + k), ALU.mult))
                    step(dve.tensor_reduce(wts[:, k, 0:nt], r3(4), X_AXIS, ALU.add))
                step(tt(rt[:, 5, 0:nt], wts[:, 0, 0:nt], wts[:, 1, 0:nt], ALU.add))
                step(dve.reciprocal(rt[:, 6, 0:nt], rt[:, 5, 0:nt]))
                step(tt(wts[:, :, 0:nt], wts[:, :, 0:nt], rt[:, 6, 0:nt].unsqueeze(1).to_broadcast([P, 2, nt]), ALU.mult))

                dve.wait_ge(s_rk[l], 1)
                total = ps[:, 7, 64:64 + N_EXP]
                nb, cum, base = rt[:, 5, 0:N_EXP], rt[:, 6, 0:N_EXP], rt[:, 7, 0:N_EXP]
                step(dve.tensor_copy(rt[:, 12, 0:N_EXP], total))
                step(ts(nb, rt[:, 12, 0:N_EXP], 0.0, None, ALU.is_gt))
                for b in range(1, nt):
                    step(stt(nb, rt[:, 12, 0:N_EXP], float(P * b), nb, ALU.is_gt, ALU.add))
                step(dve.tensor_tensor_scan(cum, nb, zeros[:], 0.0, ALU.add, ALU.add))
                step(tt(base, cum, nb, ALU.subtract))
                rank, full = rt[:, 2, 0:w], rt[:, 3, 0:w]
                step(dve.tensor_copy(rank, ps[:, 7, 0:w]))
                step(ts(full, rank, float(P), None, ALU.is_ge))
                for b in range(2, nt):
                    step(stt(full, rank, float(P * b), full, ALU.is_ge, ALU.add))
                step(stt(rank, full, -float(P), rank, ALU.mult, ALU.add))
                step(tt(r3(3), r3(3), base.unsqueeze(1).to_broadcast([P, nt, N_EXP]), ALU.add))
                for k in range(2):
                    for i, src in ((13, 3), (14, 2)):
                        step(tt(r3(4), r3(8 + k), r3(src), ALU.mult))
                        step(dve.tensor_reduce(rt[:, i, nt * k:nt * (k + 1)], r3(4), X_AXIS, ALU.add))
                for k in range(2):
                    for m in range(nt):
                        q = k * nt + m
                        dest = CONST_AT["dest"][0] + k * TILES + m
                        tok = CONST_AT["token"][0] + m
                        at_blk = rt[:, 13, q:q + 1]
                        ts(oh_slot[:, q], const("slot"), rt[:, 14, q:q + 1], None, ALU.is_equal).then_inc(s_oh[l], 1)
                        ts(oh_blk[:, q, 0:BLK_COLS], const("block"), at_blk, cst[:, tok:tok + 1],
                           ALU.is_equal, ALU.mult).then_inc(s_oh[l], 1)
                        ts(oh_blk[:, q, BLK_COLS:], const("block"), at_blk, cst[:, dest:dest + 1],
                           ALU.is_equal, ALU.mult).then_inc(s_oh[l], 1)
                pf = plan_f.rearrange("p (b e) -> p b e", e=N_EXP)
                blk0 = cst[0:1, CONST_AT["block"][0]:CONST_AT["block"][1]]
                step(tt(pf, blk0.unsqueeze(2).to_broadcast([1, BLK_COLS, N_EXP]),
                        cum[0:1].unsqueeze(1).to_broadcast([1, BLK_COLS, N_EXP]), ALU.is_ge))
                step(dve.tensor_reduce(slot_tab[0:1, 0:BLK_COLS], pf, X_AXIS, ALU.add))
                step(dve.tensor_copy(plan[:, 0:BLK_COLS], slot_tab[0:1, 0:BLK_COLS]))
                step(dve.tensor_copy(plan[:, BLK_COLS:], cum[0:1, N_EXP - 1:N_EXP]))
                dve.wait_ge(s_tab[l], 1)
                tab = ps[:, 7, P:P + 2 * BLK_COLS]
                step(ts(slot_tab[:], tab, 0.0, float(NO_ROW), ALU.is_equal, ALU.mult))
                sync(stt(slot_idx[:], tab, -1.0, slot_tab[:], ALU.add, ALU.add), s_idx[l])

                n = dve.value_load(plan[0:1, BLK_COLS:BLK_COLS + 1], min_val=1, max_val=MAX_BLOCKS)
                dve.sem_inc(m_ac[l], 1)
                dve.sem_inc(m_yD[l], 1)
                dve.wait_ge(m_xt[l], 2)
                dve.tensor_copy(blk_inT[:, 4:8], ps[:, 3].rearrange("p (k t) -> p k t", t=P)).then_inc(m_xD[l], 1)
                with dve.Fori(0, n) as i:
                    dve.wait_ge(m_si[l], i + 1)
                    dve.wait_ge(m_up[l], i + 2)
                    dve.wait_ge(m_at[l], i + 1)
                    tt(blk_act, ps[:, 1], blk_silu, ALU.mult).then_inc(m_ac[l], 1)
                    dve.wait_ge(m_xt[l], i * 2 + 4)
                    dve.tensor_copy(blk_inT[:, 4:8], ps[:, 3].rearrange("p (k t) -> p k t", t=P)).then_inc(m_xD[l], 1)
                    dve.wait_ge(m_dn[l], i * 2 + 4)
                    dve.wait_ge(m_sc[l], i * 16 + 16)
                    dve.tensor_copy(blk_out[:, HALF:], ps[:, 6]).then_inc(m_yD[l], 1)

                for m, t in enumerate(TILES_OF[l]):
                    dve.wait_ge(s_yl[l][m % 2], 32 * (m // 2 + 1))
                    y1, y2 = val[:, 2 * (m % 2)], val[:, 2 * (m % 2) + 1]
                    step(ts(y1, y1, wts[:, 0, m:m + 1], None, ALU.mult))
                    step(stt(y1, y2, wts[:, 1, m:m + 1], y1, ALU.mult, ALU.add))
                    step(tt(y1, y1, row(3, t), ALU.mult))
                    sync(tt(resid[:, t], resid[:, t], y1, ALU.add), s_cb[l])

            dve.wait_ge(s_sq[4], NT[1])
            dve.wait_ge(s_fg, 16)
            sync(mean_square(stat[:, 1, 0:TILES], stat[:, 0, 0:TILES], D), s_fms)
            dve.wait_ge(s_frt, 1)
            step(dve.reciprocal(stat[:, 3, 0:TILES], stat[:, 2, 0:TILES]))
            for m, t in enumerate(TILES_OF[1]):
                stt(tokm[:, t], resid[:, t], stat[:, 3, t:t + 1], rows[:, 4], ALU.mult, ALU.mult).then_inc(s_fin, 1)

        @block.tensor
        def _(pe):
            def turn(dst, src, rows_n=P):
                return pe.transpose(dst, src, ident[0:rows_n, 0:rows_n])

            def turn_mirrored(dst, src):
                return pe.matmul(dst, src, const("mirror"), start=True, stop=True)

            pe.wait_ge(s_small, 16 * SMALL_LOADS_ALL)
            turn(ps[:, 7, 0:N_VEC], vec_rows[0:N_VEC, :], N_VEC).then_inc(s_vec_t, 1)
            turn(ps[:, 7, P:P + 96], adab_rows[0:96, :], 96).then_inc(s_vec_t, 1)
            pe.wait_ge(s_cond, 2)
            pe.wait_ge(s_v, 1)

            def ada_chunk(l, j):
                st = FIRST["ada", l] + j // 4
                if j % 4 == 0:
                    wait_strip(pe, 0, st)
                for k in range(KC):
                    mm = pe.matmul(ps[:, 6, 2 * j:2 * j + 2], strip(0, st)[:, k, (j % 4) * P:(j % 4 + 1) * P],
                                   cond[:, k, :], start=(k == 0), stop=(k == KC - 1))
                if j % 4 == 3:
                    mm.then_inc(s_ada[l], 1)

            def modulation_rows(l):
                pe.wait_ge(s_mod, l + 1)
                turn(ps[0:96, 7, 0:P], mod[:, l].rearrange("p j s -> p (j s)")).then_inc(s_modT, 1)

            for j in range(48):
                ada_chunk(0, j)
            modulation_rows(0)

            for l in range(LAYERS):
                for k in range(KC):
                    for s in range(2):
                        if k == 0:
                            pe.wait_ge(s_xn[l], CTX_TILES * (s + 1))
                        if k >= 2:
                            pe.wait_ge(s_he[l][s], k - 1)
                        for t in range(2):
                            mm = turn(ps[:, 2 * s + k % 2, t * P:(t + 1) * P],
                                      tokm[:, 2 * s + t, k * P:(k + 1) * P])
                        mm.then_inc(s_ht[l][s], 1)
                for s in range(2):
                    pe.wait_ge(s_he[l][s], KC)

                def turn_qk(n):
                    m = qk_index[l][n]
                    _, copied, value = qkv_copy[l][n]
                    pe.wait_ge(copied, value)
                    if m >= 2:
                        pe.wait_ge(s_qc[l], m - 1)
                    mirrored = l == 1 and qkv_jobs[l][n][0] < 2
                    for k in range(4):
                        mm = (turn_mirrored if mirrored else turn)(ps[:, 4 + m % 2, k * P:(k + 1) * P],
                                  tokm[:, 0, (m % 2) * STRIP + k * P:(m % 2) * STRIP + (k + 1) * P])
                    mm.then_inc(s_qt[l], 1)

                for n, (g, t) in enumerate(qkv_jobs[l]):
                    st = FIRST["qkv", l] + g
                    wait_strip(pe, l, st)
                    if n >= 2:
                        kind, copied, value = qkv_copy[l][n - 2]
                        pe.wait_ge(copied, value)
                    for k in range(KC):
                        mm = pe.matmul(ps[:, n % 2], hT[:, k, t * P:(t + 1) * P], strip(l, st)[:, k, :],
                                       start=(k == 0), stop=(k == KC - 1))
                    mm.then_inc(s_qm[l], 1)
                    if n >= 1 and qk_index[l][n - 1] is not None:
                        turn_qk(n - 1)
                pe.wait_ge(s_qc[l], N_QK[l])
                for _, copied, value in qkv_copy[l][-2:]:
                    pe.wait_ge(copied, value)

                if l == 0:
                    def scores(u):
                        t, h = units[0][u]
                        nk = key_tiles(t) * P
                        if u >= 2:
                            pe.wait_ge(s_ex[0], 2 * (u - 1))
                        for cc in range(2):
                            part = slice(cc * HD, (cc + 1) * HD)
                            pe.matmul(ps[:, 2 * (u % 2) + cc, 0:nk], qT[part, h, t * P:(t + 1) * P], kT[part, h, 0:nk],
                                      start=True, stop=True).then_inc(s_sc[0], 1)

                    def turn_probs(u):
                        t, h = units[0][u]
                        pe.wait_ge(s_pr, u + 1)
                        if u >= 2:
                            pe.wait_ge(s_pc[0], u - 1)
                        for k in range(key_tiles(t)):
                            mm = turn(ps[:, (4, 7)[u % 2], k * P:(k + 1) * P], hT[:, 2 * (u % 2), k * P:(k + 1) * P])
                        mm.then_inc(s_pt[0], 1)

                    def attend(u):
                        t, h = units[0][u]
                        nk = key_tiles(t)
                        pe.wait_ge(s_pc[0], u + 1)
                        if u >= 1:
                            pe.wait_ge(s_oe[0], u)
                        for k in range(nk):
                            mm = pe.matmul(ps[:, 5, 0:2 * HD], hT[:, 4 + u % 2, k * P:(k + 1) * P],
                                           val[:, k, h * 2 * HD:(h + 1) * 2 * HD], start=(k == 0), stop=(k == nk - 1))
                        mm.then_inc(s_pv[0], 1)

                    U = len(units[0])
                    chunk = 0
                    pe.wait_ge(s_modR, 1)
                    for u in range(U + 2):
                        if u < U:
                            scores(u)
                        while chunk < 48 and chunk < (48 * (u + 1)) // U:
                            ada_chunk(1, chunk)
                            chunk += 1
                        if 1 <= u <= U:
                            turn_probs(u - 1)
                        if u >= 2:
                            attend(u - 2)
                    modulation_rows(1)
                else:
                    def scores1(u):
                        t, h = units[1][u]
                        if u >= 4:
                            pe.wait_ge(s_ex[1], u - 3)
                        part = slice((h % 2) * HD, (h % 2 + 1) * HD)
                        pe.matmul(ps[:, u % 4], qT[part, h // 2, t * P:(t + 1) * P], kT[part, h // 2, :],
                                  start=True, stop=True).then_inc(s_sc[1], 1)

                    def turn_probs1(u):
                        pe.wait_ge(s_ex[1], u + 1)
                        if u >= 2:
                            pe.wait_ge(s_pc[1], u - 1)
                        for k in range(TILES):
                            mm = turn(ps[:, (4, 7)[u % 2], k * P:(k + 1) * P], hT[:, u % 4, k * P:(k + 1) * P])
                        mm.then_inc(s_pt[1], 1)

                    def attend1(u):
                        t, h = units[1][u]
                        pe.wait_ge(s_pc[1], u + 1)
                        if u >= 2:
                            pe.wait_ge(s_oe[1], u - 1)
                        for k in range(TILES):
                            mm = pe.matmul(ps[:, 5 + u % 2, 0:HD], hT[:, 4 + u % 2, k * P:(k + 1) * P],
                                           val[:, k, h * HD:(h + 1) * HD], start=(k == 0), stop=(k == TILES - 1))
                        mm.then_inc(s_pv[1], 1)

                    U = len(units[1])
                    for u in range(U + 3):
                        if u < U:
                            scores1(u)
                        if 2 <= u < U + 2:
                            turn_probs1(u - 2)
                        if u >= 3:
                            attend1(u - 3)

                def turn_out(m):
                    t = TILES_OF[l][m]
                    if l == 0:
                        pe.wait_ge(s_on, m + 1)
                    elif m == 0:
                        pe.wait_ge(s_oe[1], len(units[1]))
                    for hf in range(2):
                        if m >= 1:
                            pe.wait_ge(s_oc[l], 2 * (m - 1) + hf + 1)
                        for k in range(4):
                            mm = (turn_mirrored if l == 1 else turn)(
                                ps[:, 4 + hf, k * P:(k + 1) * P], tokm[:, t, (4 * hf + k) * P:(4 * hf + k + 1) * P])
                        mm.then_inc(s_ot[l], 1)

                def project_out(m):
                    t = TILES_OF[l][m]
                    pe.wait_ge(s_oc[l], 2 * m + 2)
                    for hf in range(2):
                        j = 2 * m + hf
                        wait_strip(pe, l, FIRST["wo", l] + hf)
                        if j >= 2:
                            pe.wait_ge(s_we[l], j - 1)
                        for k in range(KC):
                            mm = pe.matmul(ps[:, j % 2], hT[:, k, t * P:(t + 1) * P],
                                           strip(l, FIRST["wo", l] + hf)[:, k, :], start=(k == 0), stop=(k == KC - 1))
                        mm.then_inc(s_wm[l], 1)

                def logits(m):
                    t = TILES_OF[l][m]
                    pe.wait_ge(s_h[l], m + 1)
                    for hf in range(2):
                        if m >= 1:
                            pe.wait_ge((s_h2A, s_h2D)[hf][l], m)
                        for k in range(4):
                            mm = turn(ps[:, 2 + hf, k * P:(k + 1) * P], tokm[:, t, (4 * hf + k) * P:(4 * hf + k + 1) * P])
                        mm.then_inc(s_h2t[l], 1)
                    pe.wait_ge(s_h2A[l], m + 1)
                    pe.wait_ge(s_h2D[l], m + 1)
                    for k in range(KC):
                        mm = pe.matmul(ps[:, 6, m * N_EXP:(m + 1) * N_EXP], hT[:, k, t * P:(t + 1) * P], rw[:, k, :],
                                       start=(k == 0), stop=(k == KC - 1))
                    mm.then_inc(s_lg[l], 1)

                if l == 0:
                    pe.wait_ge(s_modR, 2)
                for m in range(NT[l]):
                    turn_out(m)
                    project_out(m)
                    if m >= 1:
                        logits(m - 1)
                logits(NT[l] - 1)

                pe.wait_ge(s_set, 2)
                pe.wait_ge(s_ch[l], 1)
                nt = NT[l]
                for m in range(nt):
                    for j in range(m + 1):
                        pe.matmul(ps[:, 7, m * N_EXP:(m + 1) * N_EXP], const("before") if j == m else ones[:],
                                  rt[:, 10, j * N_EXP:(j + 1) * N_EXP], start=(j == 0), stop=(j == m))
                for j in range(nt):
                    mm = pe.matmul(ps[:, 7, 64:64 + N_EXP], ones[:], rt[:, 10, j * N_EXP:(j + 1) * N_EXP],
                                   start=(j == 0), stop=(j == nt - 1))
                mm.then_inc(s_rk[l], 1)
                pe.wait_ge(s_oh[l], 3 * 2 * nt)
                for q in range(2 * nt):
                    mm = pe.matmul(ps[:, 7, P:P + 2 * BLK_COLS], oh_slot[:, q], oh_blk[:, q], start=(q == 0),
                                   stop=(q == 2 * nt - 1))
                mm.then_inc(s_tab[l], 1)

                def turn_block(gathered):
                    pe.wait_ge(m_ga[l], gathered)
                    for hf in range(2):
                        for k in range(4):
                            mm = turn(ps[:, 2 + hf, k * P:(k + 1) * P],
                                      blk_in[:, (4 * hf + k) * P:(4 * hf + k + 1) * P])
                        mm.then_inc(m_xt[l], 1)

                pe.wait_ge(s_idx[l], 1)
                n = pe.value_load(plan[0:1, BLK_COLS:BLK_COLS + 1], min_val=1, max_val=MAX_BLOCKS)
                for count, start in ((m_gt, 1), (m_up, 1), (m_dn, 2), (m_at, 1)):
                    pe.sem_inc(count[l], start)
                turn_block(16)
                down = ring[:, 2].rearrange("p k n -> p (k n)").rearrange("p (k n) -> p k n", n=D)
                with pe.Fori(0, n) as i:
                    pe.wait_ge(m_xA[l], i + 1)
                    pe.wait_ge(m_xD[l], i + 1)
                    pe.wait_ge(m_wl[l][0], i * 16 + 16)
                    for k in range(KC):
                        mm = pe.matmul(ps[:, 0], blk_inT[:, k, :], ring[:, 0, k, :], start=(k == 0), stop=(k == KC - 1))
                    mm.then_inc(m_gt[l], 1)
                    pe.wait_ge(m_wl[l][1], i * 16 + 16)
                    for k in range(KC):
                        mm = pe.matmul(ps[:, 1], blk_inT[:, k, :], ring[:, 1, k, :], start=(k == 0), stop=(k == KC - 1))
                    mm.then_inc(m_up[l], 1)
                    turn_block(i * 16 + 32)
                    pe.wait_ge(m_ac[l], i + 2)
                    for k in range(FF // P):
                        mm = turn(ps[:, 4, k * P:(k + 1) * P], blk_act[:, k * P:(k + 1) * P])
                    mm.then_inc(m_at[l], 1)
                    pe.wait_ge(m_ae[l], i + 1)
                    pe.wait_ge(m_wl[l][2], i * 16 + 16)
                    for hf in range(2):
                        pe.wait_ge((m_yA, m_yD)[hf][l], i + 1)
                        for k in range(FF // P):
                            mm = pe.matmul(ps[:, 5 + hf], blk_actT[:, k, :], down[:, k, hf * HALF:(hf + 1) * HALF],
                                           start=(k == 0), stop=(k == FF // P - 1))
                        mm.then_inc(m_dn[l], 1)
                pe.wait_ge(m_xA[l], n + 1)
                pe.wait_ge(m_xD[l], n + 1)
                pe.wait_ge(m_yA[l], n + 1)
                pe.wait_ge(m_yD[l], n + 1)


_INS = ["x", "c", "ctx", "c_ctx", "ada_w", "ada_b", "norm1_g", "norm2_g", "final_norm_g", "diff_w_qkv", "diff_w_o",
        "diff_lambda_q1", "diff_lambda_k1", "diff_lambda_q2", "diff_lambda_k2", "diff_subln_g",
        "na_w_qkv", "na_w_o", "na_rpb", "router_w", "router_bias", "moe_w_gate", "moe_w_up", "moe_w_down"]


def kernel(**inputs):
    import concourse.bacc as bacc
    from concourse.bass_utils import run_bass_kernel_spmd

    nc = bacc.Bacc("TRN2", target_bir_lowering=False, num_devices=1)
    arrays, args = {}, []
    for name in _INS + ["consts"]:
        a = constants() if name == "consts" else np.ascontiguousarray(inputs[name])
        arrays[f"in_{name}_dram"] = a
        args.append(nc.dram_tensor(f"in_{name}_dram", a.shape, mybir.dt.from_np(a.dtype), kind="ExternalInput").ap())
    out = nc.dram_tensor("out_dram", (1, SEQ, D), F32, kind="ExternalOutput").ap()
    build_trunk(nc, *args, out)
    r = run_bass_kernel_spmd(nc, [arrays], core_ids=[0])
    return r.results[0]["out_dram"]
```

```python
import math
from contextlib import ExitStack

import numpy as np

import concourse.bass as bass
from concourse import mybir

F32 = mybir.dt.float32
I32 = mybir.dt.int32
ALU = mybir.AluOpType
ACT = mybir.ActivationFunctionType
X_AXIS = mybir.AxisListType.X

P = 128
D = 1024
KC = D // P
SEQ = 256
CTX = 256
LAYERS = 2
TILES = (SEQ + CTX) // P
CTX_TILES = CTX // P
GRID_W = 64
GRID_H = SEQ // GRID_W
HD = 64
SCALE = HD ** -0.5
EPS = 1e-6
DIFF_HEADS = D // (2 * HD)
NA_HEADS = D // HD
NA_WR, NA_WC = 8, 16
RPB_H, RPB_W = 2 * NA_WR - 1, 2 * NA_WC - 1
ROPE_THETA = 10000.0
LAMBDA_INIT = 0.8 - 0.6 * math.exp(-0.3 * 0)
N_EXP, N_GRP = 16, 4
GRP = N_EXP // N_GRP
FF = 512
STRIP = 512
NEG = 1e30
NO_ROW = 100000
MAX_BLOCKS = 23
BLK_COLS = MAX_BLOCKS + 1

TILES_OF = [list(range(TILES)), list(range(CTX_TILES, TILES))]

CONST_PARTS = [("ident", P), ("mirror", P), ("before", P), ("slot", P), ("block", BLK_COLS), ("rev_expert", N_EXP),
               ("rev_group", N_GRP), ("token", TILES), ("dest", 2 * TILES), ("cos", 2 * 32), ("sin", 2 * 32),
               ("valid", GRID_W), ("invalid", GRID_W)]
CONST_AT, _at = {}, 0
for _name, _n in CONST_PARTS:
    CONST_AT[_name] = (_at, _at + _n)
    _at += _n
CONST_COLS = _at

VEC_ROWS = {"c_ctx": (0, 8), "c": (8, 16), "norm1": (16, 32), "norm2": (32, 48), "subln": (48, 49)}
N_VEC = 49


def constants():
    t = np.zeros((P, CONST_COLS), np.float32)

    def put(name, a):
        lo, hi = CONST_AT[name]
        t[:, lo:hi] = a

    p = np.arange(P)
    put("ident", np.eye(P))
    mirrored = p // GRID_W * GRID_W + GRID_W - 1 - p % GRID_W
    put("mirror", mirrored[:, None] == p[None, :])
    put("before", p[:, None] < p[None, :])
    put("slot", np.broadcast_to(p, (P, P)))
    put("block", np.broadcast_to(np.arange(BLK_COLS), (P, BLK_COLS)))
    put("rev_expert", np.broadcast_to(N_EXP - np.arange(N_EXP), (P, N_EXP)))
    put("rev_group", np.broadcast_to(N_GRP - np.arange(N_GRP), (P, N_GRP)))
    put("token", p[:, None] + P * np.arange(TILES) + 1)
    put("dest", p[:, None] + P * np.arange(2 * TILES) + 1)
    tok = np.arange(SEQ)
    inv = (np.float32(ROPE_THETA) ** (-np.arange(HD // 4, dtype=np.float32) / np.float32(HD // 4))).astype(np.float32)
    row, col = (tok // GRID_W).astype(np.float32), (tok % GRID_W).astype(np.float32)
    ang = np.concatenate([row[:, None] * inv, col[:, None] * inv], -1).astype(np.float32)
    put("cos", np.cos(ang).reshape(2, P, 32).transpose(1, 0, 2).reshape(P, 64))
    put("sin", np.sin(ang).reshape(2, P, 32).transpose(1, 0, 2).reshape(P, 64))
    c = mirrored % GRID_W
    c0 = np.clip(c - NA_WC // 2, 0, GRID_W - NA_WC)[:, None]
    keys = np.arange(GRID_W)[None, :]
    valid = (keys >= c0) & (keys < c0 + NA_WC)
    put("valid", valid)
    put("invalid", np.where(valid, 0.0, -NEG))
    return t


def build_trunk(nc, x, c, ctx, c_ctx, ada_w, ada_b, norm1_g, norm2_g, final_norm_g, diff_w_qkv, diff_w_o,
                diff_lambda_q1, diff_lambda_k1, diff_lambda_q2, diff_lambda_k2, diff_subln_g,
                na_w_qkv, na_w_o, na_rpb, router_w, router_bias, moe_w_gate, moe_w_up, moe_w_down,
                consts, out):
    with ExitStack() as stack:
        def sb(name, shape, dt=F32):
            return stack.enter_context(nc.sbuf_tensor(name, shape, dt))

        def sem(name):
            return stack.enter_context(nc.semaphore(name))

        cst = sb("cst", [P, CONST_COLS])
        resid = sb("resid", [P, TILES, D])
        hT = sb("hT", [P, KC, TILES * P])
        tokm = sb("tokm", [P, TILES, D])
        val = sb("val", [P, TILES, D])
        qT = sb("qT", [P, KC, TILES * P])
        kT = sb("kT", [P, KC, TILES * P])
        ring = sb("ring", [P, 3, KC, STRIP])
        rows = sb("rows", [P, 8, D])
        bias = sb("bias", [P, NA_HEADS, 6, GRID_W])
        vec = sb("vec", [P, N_VEC])
        adab = sb("adab", [P, LAYERS * 48])
        cond = sb("cond", [P, KC, 32])
        mod = sb("mod", [P, LAYERS, 48, 2])
        mod_rows = sb("mod_rows", [96, P])
        rw = sb("rw", [P, KC, N_EXP])
        rbias = sb("rbias", [P, N_EXP])
        lam = sb("lam", [P, 8])
        subln = sb("subln", [P, 1])
        stat = sb("stat", [P, 4, 4 * DIFF_HEADS])
        att = sb("att", [P, 4, 8])
        zeros = sb("zeros", [P, N_EXP])
        wts = sb("wts", [P, 2, TILES])
        slot_idx = sb("slot_idx", [P, 2 * BLK_COLS], I32)
        plan = sb("plan", [1, BLK_COLS + 1], I32)
        gather_idx = sb("gather_idx", [P, 1], I32)
        scatter_idx = sb("scatter_idx", [P, 1], I32)
        ps = stack.enter_context(nc.psum_tensor("ps", [P, 8, 512], F32))

        vec_rows = val[:, 1, 0:P]
        adab_rows = val[:, 2, 0:P]
        lam_in = val[:, 3, 0:4 * HD].rearrange("p (a b) -> p a b", b=HD)

        NORM_AT = {"1 of 0": 0, "sub": TILES, "2 of 0": TILES + 1, "1 of 1": 2 * TILES + 1, "2 of 1": 3 * TILES + 1}

        def norm_step(name):
            return NORM_AT[name] + 1

        def squares(name):
            return NORM_AT[name] + (name == "1 of 0")

        blk_in = qT[:, 0:2, :].rearrange("p a b -> p (a b)")
        blk_inT = qT[:, 2:4, :].rearrange("p a b -> p (a b)").rearrange("p (k t) -> p k t", t=P)
        blk_silu = qT[:, 4, :]
        blk_act = qT[:, 5, :]
        blk_actT = qT[:, 6, :].rearrange("p (k t) -> p k t", t=P)
        blk_out = kT[:, 0:2, :].rearrange("p a b -> p (a b)")

        oh_slot = kT[:, 2:4, :].rearrange("p a b -> p (a b)").rearrange("p (q s) -> p q s", s=P)
        oh_blk = kT[:, 4, 0:8 * 2 * BLK_COLS].rearrange("p (q s) -> p q s", s=2 * BLK_COLS)
        rt = kT[:, 5:7, :].rearrange("p a b -> p (a b)").rearrange("p (i w) -> p i w", w=TILES * N_EXP)
        slot_tab = kT[:, 4, 8 * 2 * BLK_COLS:9 * 2 * BLK_COLS]
        plan_f = kT[0:1, 7, 0:BLK_COLS * N_EXP]
        ones = kT[:, 7, BLK_COLS * N_EXP:BLK_COLS * N_EXP + P]

        h_dram = [nc.dram_tensor(f"h_rows_{l}", [TILES * P, D], F32).ap() for l in range(LAYERS)]
        y_dram = [nc.dram_tensor(f"expert_rows_{l}", [2 * TILES * P, D], F32).ap() for l in range(LAYERS)]
        mod_dram = [nc.dram_tensor(f"mod_rows_{l}", [96, P], F32) for l in range(LAYERS)]

        def const(name, n=None):
            lo, hi = CONST_AT[name]
            return cst[:, lo:hi]

        ident = const("ident")

        s_small = sem("small_loaded")
        s_x = sem("streams_loaded")
        s_bias = sem("bias_loaded")
        s_bias_done = sem("bias_masked")
        s_set = sem("fills_done")
        s_vec_t = sem("vectors_turned")
        s_vec = sem("vectors_copied")
        s_cond = sem("cond_ready")
        s_lam = sem("lambda_steps")
        s_lam_exp = sem("lambda_exps")
        s_v = sem("vector_steps")
        s_ada = sem("mod_products")
        s_adc = sem("mod_products_copied")
        s_adt = sem("mod_products_turned")
        s_adr = sem("mod_products_summed")
        s_mod = sem("mod_ready")
        s_modT = sem("mod_turned")
        s_modR = sem("mod_rows_copied")
        s_modD = sem("mod_rows_stored")
        s_rows = sem("rows_loaded")
        s_sq = sem("squares")
        s_ms = sem("mean_squares")
        s_rt = sem("roots")
        s_xn = [sem(f"normalised_{l}") for l in range(LAYERS)]
        s_ht = [[sem(f"h_turned_{l}_{s}") for s in range(2)] for l in range(LAYERS)]
        s_he = [[sem(f"h_modulated_{l}_{s}") for s in range(2)] for l in range(LAYERS)]
        s_qm = [sem(f"qkv_products_{l}") for l in range(LAYERS)]
        s_qeA = [sem(f"qkv_copied_act_{l}") for l in range(LAYERS)]
        s_qeD = [sem(f"qkv_copied_dve_{l}") for l in range(LAYERS)]
        s_qt = [sem(f"qk_turned_{l}") for l in range(LAYERS)]
        s_qc = [sem(f"qk_turned_copied_{l}") for l in range(LAYERS)]
        s_sc = [sem(f"scores_{l}") for l in range(LAYERS)]
        s_nm = [sem(f"maxima_{l}") for l in range(LAYERS)]
        s_ex = [sem(f"exps_{l}") for l in range(LAYERS)]
        s_pr = sem("diff_probs")
        s_pt = [sem(f"probs_turned_{l}") for l in range(LAYERS)]
        s_pc = [sem(f"probs_turned_copied_{l}") for l in range(LAYERS)]
        s_pv = [sem(f"attended_{l}") for l in range(LAYERS)]
        s_oe = [sem(f"attended_copied_{l}") for l in range(LAYERS)]
        s_on = sem("heads_normalised")
        s_hs = sem("head_squares")
        s_w1 = [sem(f"first_experts_weighed_{l}") for l in range(LAYERS)]
        s_ot = [sem(f"o_turned_{l}") for l in range(LAYERS)]
        s_oc = [sem(f"o_turned_copied_{l}") for l in range(LAYERS)]
        s_wm = [sem(f"wo_products_{l}") for l in range(LAYERS)]
        s_we = [sem(f"wo_added_{l}") for l in range(LAYERS)]
        s_h = [sem(f"h2_ready_{l}") for l in range(LAYERS)]
        s_hst = [sem(f"h2_stored_{l}") for l in range(LAYERS)]
        s_h2t = [sem(f"h2_turned_{l}") for l in range(LAYERS)]
        s_h2A = [sem(f"h2_turned_copied_act_{l}") for l in range(LAYERS)]
        s_h2D = [sem(f"h2_turned_copied_dve_{l}") for l in range(LAYERS)]
        s_lg = [sem(f"logits_{l}") for l in range(LAYERS)]
        s_le = [sem(f"logit_exps_{l}") for l in range(LAYERS)]
        s_ch = [sem(f"choices_{l}") for l in range(LAYERS)]
        s_rk = [sem(f"ranks_{l}") for l in range(LAYERS)]
        s_oh = [sem(f"slot_marks_{l}") for l in range(LAYERS)]
        s_tab = [sem(f"slot_table_{l}") for l in range(LAYERS)]
        s_idx = [sem(f"plan_ready_{l}") for l in range(LAYERS)]
        m_wl = [[sem(f"expert_{w}_loaded_{l}") for w in ("gate", "up", "down")] for l in range(LAYERS)]
        m_gt = [sem(f"block_gates_{l}") for l in range(LAYERS)]
        m_up = [sem(f"block_ups_{l}") for l in range(LAYERS)]
        m_dn = [sem(f"block_downs_{l}") for l in range(LAYERS)]
        m_xt = [sem(f"block_in_turned_{l}") for l in range(LAYERS)]
        m_xA = [sem(f"block_in_copied_act_{l}") for l in range(LAYERS)]
        m_xD = [sem(f"block_in_copied_dve_{l}") for l in range(LAYERS)]
        m_si = [sem(f"block_silu_{l}") for l in range(LAYERS)]
        m_ac = [sem(f"block_act_{l}") for l in range(LAYERS)]
        m_at = [sem(f"block_act_turned_{l}") for l in range(LAYERS)]
        m_ae = [sem(f"block_act_turned_copied_{l}") for l in range(LAYERS)]
        m_yA = [sem(f"block_out_act_{l}") for l in range(LAYERS)]
        m_yD = [sem(f"block_out_dve_{l}") for l in range(LAYERS)]
        m_ix = [sem(f"block_indices_{l}") for l in range(LAYERS)]
        m_ga = [sem(f"block_gathered_{l}") for l in range(LAYERS)]
        m_sc = [sem(f"block_scattered_{l}") for l in range(LAYERS)]
        s_yl = [[sem(f"expert_rows_loaded_{l}_{b}") for b in range(2)] for l in range(LAYERS)]
        s_cb = [sem(f"combined_{l}") for l in range(LAYERS)]
        s_fg = sem("final_gain_loaded")
        s_fms, s_frt = sem("final_mean_squares"), sem("final_roots")
        s_turn = sem("pool_turns")
        s_fin = sem("final_ready")
        s_out = sem("out_stored")
        s_ld = [[sem(f"strip_loaded_{l}_{s}") for s in range(3)] for l in range(LAYERS)]

        QKV = [diff_w_qkv, na_w_qkv]
        WO = [diff_w_o, na_w_o]
        ADA, ADA_QKV, ADA_ATT, ADA_PLAN = 12, 4, 10, 19
        qkv_jobs, strips, at = [], [], []
        for l in range(LAYERS):
            jobs = [(g, t) for g in range(6) for t in (TILES_OF[l] if g < 2 else range(TILES))]
            qkv_jobs.append(jobs)
            plan_l = []
            index = {}

            def add(kind, j, entry):
                index[kind, j] = len(plan_l)
                plan_l.append(entry)

            def add_ada(a):
                add("ada", a, (ada_w[a // ADA], a % ADA, s_ada, a + 1))

            if l == 0:
                for a in range(ADA_QKV):
                    add_ada(a)
            for g in range(6):
                last = max(n for n, (gg, _) in enumerate(jobs) if gg == g)
                add("qkv", g, (QKV[l][0], g, s_qm[l], last + 1))
                if l == 0:
                    add_ada(ADA_QKV + g)
            if l == 0:
                for a in range(ADA_ATT, ADA_PLAN):
                    add_ada(a)
            for j in range(2):
                add("wo", j, (WO[l][0], j, s_wm[l], 2 * len(TILES_OF[l]) - 1 + j))
            if l == 0:
                for a in range(ADA_PLAN, 2 * ADA):
                    add_ada(a)
            strips.append(plan_l)
            at.append(index)

        def strip(l, j):
            return ring[:, j % 3]

        def wait_strip(eng, l, j):
            eng.wait_ge(s_ld[l][j % 3], 16 * (j // 3 + 1))

        qkv_copy, qk_index = [], []
        for l in range(LAYERS):
            n_act = n_dve = n_qk = 0
            copies, index = [], []
            for g, t in qkv_jobs[l]:
                if l == 0 and g < 4 and t >= CTX_TILES:
                    n_dve += 1
                    copies.append(("dve", s_qeD[l], n_dve))
                else:
                    n_act += 1
                    copies.append(("act", s_qeA[l], n_act))
                index.append(n_qk if g < 4 else None)
                n_qk += g < 4
            qkv_copy.append(copies)
            qk_index.append(index)
        N_QK = [sum(i is not None for i in qk_index[l]) for l in range(LAYERS)]

        units = [[(t, h) for t in TILES_OF[0] for h in range(DIFF_HEADS)],
                 [(t, h) for t in TILES_OF[1] for h in range(NA_HEADS)]]

        def mod_banks(a):
            return (6, 7) if a < ADA_ATT else (6, 6) if a < ADA_PLAN else (0, 1)

        def mod_part(a):
            return rows[:, 7, 0:STRIP] if a < ADA else tokm[:, 3, STRIP:] if a < ADA_PLAN else qT[:, 7]

        def key_tiles(t):
            return CTX_TILES if t < CTX_TILES else TILES

        NT = [len(t) for t in TILES_OF]
        HALF = D // 2
        VECTOR_LOADS = 7
        SMALL_LOADS_ALL = VECTOR_LOADS + 6
        block = stack.enter_context(nc.Block())

        @block.sync
        def _(sp):
            def small(dst, src):
                sp.dma_start(dst, src).then_inc(s_small, 16)

            small(cst[:], consts)
            small(vec_rows[8:16, :], c.rearrange("a (r p) -> (a r) p", p=P))
            small(vec_rows[0:8, :], c_ctx.rearrange("(r p) -> r p", p=P))
            small(vec_rows[16:32, :], norm1_g.rearrange("l (r p) -> (l r) p", p=P))
            small(vec_rows[32:48, :], norm2_g.rearrange("l (r p) -> (l r) p", p=P))
            small(vec_rows[48:49, :], diff_subln_g)
            small(adab_rows[0:96, :], ada_b.rearrange("l (r p) -> (l r) p", p=P))

            def load_strip(l, j):
                src, g, _, _ = strips[l][j]
                if j >= 3:
                    _, _, used, value = strips[l][j - 3]
                    sp.wait_ge(used, value)
                sp.dma_start(strip(l, j), src.rearrange("(k p) n -> p k n", p=P)[:, :, g * STRIP:(g + 1) * STRIP]) \
                    .then_inc(s_ld[l][j % 3], 16)

            for j in range(2):
                load_strip(0, j)
            sp.dma_start(resid[:, 0:CTX_TILES], ctx.rearrange("a (t p) d -> p (a t) d", p=P)).then_inc(s_x, 16)
            sp.dma_start(resid[:, CTX_TILES:TILES], x.rearrange("a (t p) d -> p (a t) d", p=P)).then_inc(s_x, 16)
            load_strip(0, 2)
            for i, v in enumerate((diff_lambda_q1, diff_lambda_k1, diff_lambda_q2, diff_lambda_k2)):
                small(lam_in[:, i, :], v.broadcast_to([P, HD]))
            small(rbias[:], router_bias.partition_broadcast(P))
            small(rw[:], router_w.rearrange("(k p) e -> p k e", p=P))

            def load_rows(l, targets):
                for slot, piece, s in targets:
                    src = bass.AP(mod_dram[l], (piece * KC * 2 + s) * P, [[0, P], [2 * P, KC], [1, P]])
                    sp.dma_start(rows[:, slot].rearrange("p (k n) -> p k n", n=P), src).then_inc(s_rows, 16)

            first_rows = at[0]["ada", ADA + 1] + 1
            for j in range(3, first_rows):
                load_strip(0, j)
            sp.wait_ge(s_modR, 1)
            sp.dma_start(mod_dram[0].ap(), mod_rows[:]).then_inc(s_modD, 16)
            sp.wait_ge(s_modD, 16)
            load_rows(0, [(2 * i + s, piece, s) for i, piece in enumerate((2, 3, 4, 5)) for s in range(2)])
            for par in range(2):
                for h in range(NA_HEADS):
                    src = bass.AP(na_rpb.tensor, h * RPB_H * RPB_W + (NA_WR - 1 - 2 - par) * RPB_W + NA_WC - GRID_W,
                                  [[1, GRID_W], [RPB_W, 6], [1, GRID_W]])
                    sp.dma_start(bias[par * GRID_W:(par + 1) * GRID_W, h], src).then_inc(s_bias, 16)
            for j in range(first_rows, at[0]["ada", ADA_PLAN] + 1):
                load_strip(0, j)

            def store_h(l):
                for n, t in enumerate(TILES_OF[l]):
                    sp.wait_ge(s_h[l], n + 1)
                    sp.dma_start(h_dram[l][n * P:(n + 1) * P, :], tokm[:, t]).then_inc(s_hst[l], 16)

            def load_experts(l):
                sp.wait_ge(s_wm[l], 2 * NT[l])
                if l == 0:
                    sp.wait_ge(s_modR, 2)
                sp.wait_ge(s_idx[l], 1)
                n = sp.value_load(plan[0:1, BLK_COLS:BLK_COLS + 1], min_val=1, max_val=MAX_BLOCKS)
                gate = moe_w_gate[l].rearrange("e (k p) n -> e p k n", p=P)
                up = moe_w_up[l].rearrange("e (k p) n -> e p k n", p=P)
                down = moe_w_down[l].rearrange("e (k p) n -> e p k n", p=P)
                with sp.Fori(0, n) as i:
                    e = sp.value_load(plan[0:1, bass.ds(i, 1)], min_val=0, max_val=N_EXP - 1)
                    sp.wait_ge(m_gt[l], i + 1)
                    sp.dma_start(ring[:, 0], gate[bass.ds(e, 1)].rearrange("a p k n -> p (a k) n")).then_inc(m_wl[l][0], 16)
                    sp.wait_ge(m_up[l], i + 1)
                    sp.dma_start(ring[:, 1], up[bass.ds(e, 1)].rearrange("a p k n -> p (a k) n")).then_inc(m_wl[l][1], 16)
                    sp.wait_ge(m_dn[l], i * 2 + 2)
                    sp.dma_start(ring[:, 2].rearrange("p k n -> p (k n)").rearrange("p (k n) -> p k n", n=D),
                                 down[bass.ds(e, 1)].rearrange("a p k n -> p (a k) n")).then_inc(m_wl[l][2], 16)
                return n

            def load_expert_rows(l, n):
                sp.wait_ge(m_sc[l], n * 16 + 16)
                for m, t in enumerate(TILES_OF[l]):
                    if m >= 2:
                        sp.wait_ge(s_cb[l], m - 1)
                    for k in range(2):
                        src = y_dram[l][k * TILES * P + m * P:k * TILES * P + (m + 1) * P, :]
                        sp.dma_start(val[:, 2 * (m % 2) + k], src).then_inc(s_yl[l][m % 2], 16)

            store_h(0)
            for j in range(at[0]["ada", ADA_PLAN] + 1, len(strips[0])):
                load_strip(0, j)
            n0 = load_experts(0)
            sp.dma_start(mod_dram[1].ap(), mod_rows[:]).then_inc(s_modD, 16)
            sp.wait_ge(s_modD, 32)
            load_rows(1, [(i, piece, 1) for i, piece in enumerate((2, 3, 4))])
            sp.wait_ge(m_dn[0], n0 * 2 + 2)
            for j in range(3):
                load_strip(1, j)
            load_expert_rows(0, n0)
            sp.wait_ge(s_cb[0], NT[0])
            load_rows(1, [(3, 5, 1)])
            sp.dma_start(rows[:, 4], final_norm_g.partition_broadcast(P)).then_inc(s_fg, 16)
            for j in range(3, len(strips[1])):
                load_strip(1, j)
            store_h(1)
            n1 = load_experts(1)
            load_expert_rows(1, n1)
            for m, t in enumerate(TILES_OF[1]):
                sp.wait_ge(s_fin, m + 1)
                sp.dma_start(out[0, m * P:(m + 1) * P, :], tokm[:, t]).then_inc(s_out, 16)
            sp.wait_ge(s_out, 16 * NT[1])

        @block.gpsimd
        def _(pool):
            def in_turn():
                pool.sem_inc(s_turn, 1)

            pool.memset(cond[:], 0.0).then_inc(s_set, 1)
            pool.memset(zeros[:], 0.0).then_inc(s_set, 1)
            pool.wait_ge(s_small, 16 * SMALL_LOADS_ALL)
            pool.wait_ge(s_bias, 16 * 2 * NA_HEADS)
            table = bias[:].rearrange("p h r c -> p (h r) c")
            valid = const("valid").unsqueeze(1).to_broadcast([P, NA_HEADS * 6, GRID_W])
            invalid = const("invalid").unsqueeze(1).to_broadcast([P, NA_HEADS * 6, GRID_W])
            pool.tensor_tensor(table, table, valid, ALU.mult).then_inc(s_bias_done, 1)
            pool.wait_ge(s_bias_done, 1)
            pool.tensor_tensor(table, table, invalid, ALU.add).then_inc(s_bias_done, 1)

            for l in range(LAYERS):
                rows_l = NT[l] * P
                pool.wait_ge(s_sc[l], len(units[l]))
                pool.memset(ones, 1.0).then_inc(s_set, 1)
                pool.wait_ge(s_idx[l], 1)
                n = pool.value_load(plan[0:1, BLK_COLS:BLK_COLS + 1], min_val=1, max_val=MAX_BLOCKS)
                last_row, last_made = pool.to_reg(rows_l - 1), pool.to_reg(2 * TILES * P - 1)
                pool.memset(blk_in, 0.0).then_inc(m_ix[l], 1)
                pool.wait_ge(m_ix[l], 1)
                pool.tensor_copy(gather_idx[:], slot_idx[:, 0:1]).then_inc(m_ix[l], 1)
                pool.wait_ge(m_ix[l], 2)
                pool.wait_ge(s_hst[l], 16 * NT[l])
                pool.indirect_dma_start(blk_in, None, h_dram[l][0:rows_l], bass.IndirectOffsetOnAxis(ap=gather_idx[:], axis=0),
                                        bounds_check=last_row, oob_is_err=False).then_inc(m_ga[l], 16)
                pool.memset(blk_out, 0.0).then_inc(m_ix[l], 1)
                pool.tensor_copy(scatter_idx[:], slot_idx[:, 2 * BLK_COLS - 1:]).then_inc(m_ix[l], 1)
                pool.wait_ge(m_ix[l], 4)
                pool.indirect_dma_start(y_dram[l], bass.IndirectOffsetOnAxis(ap=scatter_idx[:], axis=0), blk_out, None,
                                        bounds_check=last_made, oob_is_err=False).then_inc(m_sc[l], 16)
                with pool.Fori(0, n) as i:
                    pool.wait_ge(m_ga[l], i * 16 + 16)
                    pool.wait_ge(m_xt[l], i * 2 + 2)
                    in_turn()
                    pool.tensor_copy(gather_idx[:], slot_idx[:, bass.ds(i + 1, 1)]).then_inc(m_ix[l], 1)
                    pool.wait_ge(m_ix[l], i * 2 + 5)
                    in_turn()
                    pool.indirect_dma_start(blk_in, None, h_dram[l][0:rows_l],
                                            bass.IndirectOffsetOnAxis(ap=gather_idx[:], axis=0),
                                            bounds_check=last_row, oob_is_err=False).then_inc(m_ga[l], 16)
                    pool.wait_ge(m_sc[l], i * 16 + 16)
                    in_turn()
                    pool.tensor_copy(scatter_idx[:], slot_idx[:, bass.ds(i + BLK_COLS, 1)]).then_inc(m_ix[l], 1)
                    pool.wait_ge(m_ix[l], i * 2 + 6)
                    pool.wait_ge(m_yA[l], i + 2)
                    pool.wait_ge(m_yD[l], i + 2)
                    in_turn()
                    pool.indirect_dma_start(y_dram[l], bass.IndirectOffsetOnAxis(ap=scatter_idx[:], axis=0), blk_out, None,
                                            bounds_check=last_made, oob_is_err=False).then_inc(m_sc[l], 16)

        @block.scalar
        def _(act):
            def square_rows(t, src, dst):
                act.activation(dst, src, ACT.Square, accum_out=stat[:, 0, t:t + 1]).then_inc(s_sq, 1)

            act.wait_ge(s_vec, 1)
            act.wait_ge(s_set, 1)
            for s in range(2):
                act.activation(cond[:, :, s], vec[:, 8 * s:8 * s + 8], ACT.Silu).then_inc(s_cond, 1)
            act.wait_ge(s_lam, 1)
            act.activation(lam[:, 2:4], lam[:, 0:2], ACT.Exp).then_inc(s_lam_exp, 1)

            def copy_mod(a):
                act.wait_ge(s_ada, a + 1)
                if a >= 1:
                    act.wait_ge(s_adt, a)
                act.copy(mod_part(a), ps[:, mod_banks(a)[0]]).then_inc(s_adc, 1)

            def norm1(l, t):
                square_rows(t, resid[:, t], tokm[:, t])
                act.wait_ge(s_ms, norm_step(f"1 of {l}") + t)
                act.activation(stat[:, 2, t:t + 1], stat[:, 1, t:t + 1], ACT.Sqrt).then_inc(s_rt, 1)

            def weigh_first(l, m):
                act.wait_ge(s_yl[l][m % 2], 32 * (m // 2 + 1))
                y1 = val[:, 2 * (m % 2)]
                act.activation(y1, y1, ACT.Copy, scale=wts[:, 0, m:m + 1]).then_inc(s_w1[l], 1)

            act.wait_ge(s_x, 32)
            for t in range(TILES):
                norm1(0, t)
            for a in range(ADA_QKV):
                copy_mod(a)

            for l in range(LAYERS):
                act.wait_ge(s_mod, (1, 3)[l])
                for k in range(KC):
                    act.wait_ge(s_ht[l][0], k + 1)
                    act.activation(hT[:, k, 0:CTX], ps[:, k % 2, 0:CTX], ACT.Identity, bias=mod[:, l, k, 0:1],
                                   scale=mod[:, l, KC + k, 0:1]).then_inc(s_he[l][0], 1)

                def copy_turned(m, g, t):
                    act.wait_ge(s_qt[l], m + 1)
                    dst = (qT if g < 2 else kT)[:, 4 * (g % 2):4 * (g % 2) + 4, t * P:(t + 1) * P]
                    act.copy(dst, ps[:, 4 + m % 2].rearrange("p (k t) -> p k t", t=P)).then_inc(s_qc[l], 1)

                last = None
                for n, (g, t) in enumerate(qkv_jobs[l]):
                    if qkv_copy[l][n][0] == "act":
                        m = qk_index[l][n]
                        act.wait_ge(s_qm[l], n + 1)
                        if m is None:
                            dst = val[:, t, (g - 4) * STRIP:(g - 3) * STRIP]
                        else:
                            if m >= 2:
                                act.wait_ge(s_qt[l], m - 1)
                            dst = tokm[:, 0, (m % 2) * STRIP:(m % 2 + 1) * STRIP]
                        act.activation(dst, ps[:, n % 2], ACT.Copy,
                                       scale=SCALE if g < 2 else 1.0).then_inc(s_qeA[l], 1)
                    if last is not None:
                        copy_turned(*last)
                    last = (qk_index[l][n], g, t) if g < 4 else None
                    if l == 0 and n % TILES == 1:
                        copy_mod(ADA_QKV + n // TILES)
                if last is not None:
                    copy_turned(*last)

                if l == 0:
                    def exps(u):
                        t, h = units[0][u]
                        nk = key_tiles(t) * P
                        act.wait_ge(s_nm[0], u + 1)
                        if u >= 3:
                            act.wait_ge(s_pt[0], u - 2)
                        for cc in range(2):
                            act.activation(hT[:, 2 * (u % 3) + cc, 0:nk], ps[:, 2 * (u % 2) + cc, 0:nk], ACT.Exp,
                                           bias=att[:, u % 3, cc:cc + 1],
                                           accum_out=att[:, u % 3, 4 + cc:5 + cc]).then_inc(s_ex[0], 1)

                    def copy_probs(u):
                        t, h = units[0][u]
                        nk = key_tiles(t) * P
                        act.wait_ge(s_pt[0], u + 1)
                        if u >= 2:
                            act.wait_ge(s_pv[0], u - 1)
                        act.copy(hT[:, 6 + u % 2, 0:nk], ps[:, (4, 7)[u % 2], 0:nk]).then_inc(s_pc[0], 1)

                    def copy_out(u):
                        t, h = units[0][u]
                        act.wait_ge(s_pv[0], u + 1)
                        act.activation(ps[:, 5, 2 * HD:4 * HD], ps[:, 5, 0:2 * HD], ACT.Square,
                                       accum_out=stat[:, 0, 8 * t + h:8 * t + h + 1]).then_inc(s_hs, 1)
                        act.copy(tokm[:, t, h * 2 * HD:(h + 1) * 2 * HD], ps[:, 5, 0:2 * HD]).then_inc(s_oe[0], 1)

                    U = len(units[0])
                    for u in range(U + 3):
                        if u < U:
                            exps(u)
                        if u % 3 == 0 and u // 3 < ADA_PLAN - ADA_ATT:
                            copy_mod(ADA_ATT + u // 3)
                        if 2 <= u < U + 2:
                            copy_probs(u - 2)
                        if u >= 3:
                            copy_out(u - 3)
                    act.wait_ge(s_ms, norm_step("sub"))
                    act.activation(stat[:, 2], stat[:, 1], ACT.Sqrt).then_inc(s_rt, 1)
                else:
                    def copy_probs1(u):
                        act.wait_ge(s_pt[1], u + 1)
                        if u >= 2:
                            act.wait_ge(s_pv[1], u - 1)
                        act.copy(hT[:, 4 + u % 2], ps[:, (4, 7)[u % 2]]).then_inc(s_pc[1], 1)

                    U = len(units[1])
                    for u, (t, h) in enumerate(units[1]):
                        act.wait_ge(s_nm[1], u + 1)
                        if u >= 4:
                            act.wait_ge(s_pt[1], u - 3)
                        act.activation(hT[:, u % 4], ps[:, u % 4], ACT.Exp, bias=att[:, u % 4, 0:1],
                                       accum_out=att[:, u % 4, 2:3]).then_inc(s_ex[1], 1)
                        if u >= 2:
                            copy_probs1(u - 2)
                    copy_probs1(U - 2)
                    copy_probs1(U - 1)

                def turned_out(m):
                    t = TILES_OF[l][m]
                    if l == 0 and m == 0:
                        act.wait_ge(s_lam, 3)
                    for hf in range(2):
                        act.wait_ge(s_ot[l], 2 * m + hf + 1)
                        dst = hT[:, 4 * hf:4 * hf + 4, t * P:(t + 1) * P]
                        src = ps[:, 4 + hf].rearrange("p (k t) -> p k t", t=P)
                        if l == 0:
                            act.activation(dst, src, ACT.Copy, scale=subln[:, 0:1]).then_inc(s_oc[l], 1)
                        else:
                            act.copy(dst, src).then_inc(s_oc[l], 1)

                def norm2(m):
                    t = TILES_OF[l][m]
                    act.wait_ge(s_we[l], 2 * m + 2)
                    act.wait_ge(s_ot[l], 2 * m + 2)
                    square_rows(t, resid[:, t], tokm[:, t])
                    act.wait_ge(s_ms, norm_step(f"2 of {l}") + m)
                    act.activation(stat[:, 2, t:t + 1], stat[:, 1, t:t + 1], ACT.Sqrt).then_inc(s_rt, 1)

                def turned_h(m):
                    t = TILES_OF[l][m]
                    act.wait_ge(s_h2t[l], 2 * m + 1)
                    act.copy(hT[:, 0:4, t * P:(t + 1) * P],
                             ps[:, 2].rearrange("p (k t) -> p k t", t=P)).then_inc(s_h2A[l], 1)

                for m in range(NT[l]):
                    turned_out(m)
                    if m >= 1:
                        norm2(m - 1)
                        turned_h(m - 1)
                norm2(NT[l] - 1)
                turned_h(NT[l] - 1)

                act.wait_ge(s_lg[l], NT[l])
                act.activation(rt[:, 0, 0:NT[l] * N_EXP], ps[:, 6, 0:NT[l] * N_EXP], ACT.Exp, scale=-1.0).then_inc(s_le[l], 1)

                if l == 0:
                    for a in range(ADA_PLAN, 2 * ADA):
                        copy_mod(a)

                act.wait_ge(s_idx[l], 1)
                n = act.value_load(plan[0:1, BLK_COLS:BLK_COLS + 1], min_val=1, max_val=MAX_BLOCKS)
                act.sem_inc(m_yA[l], 1)
                act.wait_ge(m_xt[l], 1)
                act.copy(blk_inT[:, 0:4], ps[:, 2].rearrange("p (k t) -> p k t", t=P)).then_inc(m_xA[l], 1)
                with act.Fori(0, n) as i:
                    act.wait_ge(m_gt[l], i + 2)
                    act.wait_ge(m_ac[l], i + 1)
                    act.activation(blk_silu, ps[:, 0], ACT.Silu).then_inc(m_si[l], 1)
                    act.wait_ge(m_xt[l], i * 2 + 3)
                    act.copy(blk_inT[:, 0:4], ps[:, 2].rearrange("p (k t) -> p k t", t=P)).then_inc(m_xA[l], 1)
                    act.wait_ge(m_at[l], i + 2)
                    act.copy(blk_actT, ps[:, 4].rearrange("p (k t) -> p k t", t=P)).then_inc(m_ae[l], 1)
                    act.wait_ge(m_dn[l], i * 2 + 3)
                    act.wait_ge(m_sc[l], i * 16 + 16)
                    act.copy(blk_out[:, 0:HALF], ps[:, 5]).then_inc(m_yA[l], 1)

                for m in range(NT[l]):
                    weigh_first(l, m)
                    if l == 0 and m >= 1:
                        act.wait_ge(s_cb[0], m)
                        norm1(1, m - 1)
                if l == 0:
                    act.wait_ge(s_cb[0], TILES)
                    norm1(1, TILES - 1)

            for m, t in enumerate(TILES_OF[1]):
                act.wait_ge(s_cb[1], m + 1)
                act.activation(tokm[:, t], resid[:, t], ACT.Square, accum_out=stat[:, 0, t:t + 1]).then_inc(s_sq, 1)
            act.wait_ge(s_fms, 1)
            act.activation(stat[:, 2, 0:TILES], stat[:, 1, 0:TILES], ACT.Sqrt).then_inc(s_frt, 1)

        @block.vector
        def _(dve):
            steps = [0]

            def step(ins):
                steps[0] += 1
                ins.then_inc(s_v, 1)
                dve.wait_ge(s_v, steps[0])

            def sync(ins, s, counts={}):
                counts[s.name] = counts.get(s.name, 0) + 1
                ins.then_inc(s, 1)
                dve.wait_ge(s, counts[s.name])

            tt, ts, stt = dve.tensor_tensor, dve.tensor_scalar, dve.scalar_tensor_tensor

            dve.wait_ge(s_vec_t, 2)
            sync(dve.tensor_copy(vec[:], ps[:, 7, 0:N_VEC]), s_vec)
            step(dve.tensor_copy(adab[:], ps[:, 7, P:P + 96]))
            dve.wait_ge(s_small, 16 * SMALL_LOADS_ALL)
            step(tt(val[:, 0, 0:2 * HD].rearrange("p (a b) -> p a b", b=HD), lam_in[:, 0::2, :], lam_in[:, 1::2, :], ALU.mult))
            sync(dve.tensor_reduce(lam[:, 0:2], val[:, 0, 0:2 * HD].rearrange("p (a b) -> p a b", b=HD), X_AXIS, ALU.add), s_lam)
            dve.wait_ge(s_lam_exp, 1)
            step(tt(lam[:, 4:5], lam[:, 3:4], lam[:, 2:3], ALU.subtract))
            sync(ts(lam[:, 5:6], lam[:, 4:5], -LAMBDA_INIT, None, ALU.add), s_lam)
            sync(ts(subln[:], vec[:, 48:49], 1.0 - LAMBDA_INIT, None, ALU.mult), s_lam)

            def mean_square(dst, src, n):
                return ts(dst, src, 1.0 / n, EPS, ALU.mult, ALU.add)

            def sum_mod(a):
                dve.wait_ge(s_adt, a + 1)
                part = ps[:, mod_banks(a)[1]].rearrange("p (c q s) -> p c s q", q=4, s=32)[:, :, 0:2, :]
                j = a % ADA
                sync(dve.tensor_reduce(mod[:, a // ADA, 4 * j:4 * j + 4], part, X_AXIS, ALU.add), s_adr)

            def modulation(l, first, last):
                cols = slice(first * KC, last * KC)
                b = adab[:, 48 * l + first * KC:48 * l + last * KC].unsqueeze(2).to_broadcast([P, (last - first) * KC, 2])
                step(tt(mod[:, l, cols], mod[:, l, cols], b, ALU.add))
                for piece, gain in ((1, 16), (4, 32)):
                    if first <= piece < last:
                        g = vec[:, gain + 8 * l:gain + 8 * l + 8].unsqueeze(2).to_broadcast([P, KC, 2])
                        m = mod[:, l, piece * KC:(piece + 1) * KC]
                        step(stt(m, m, 1.0, g, ALU.add, ALU.mult))
                dve.sem_inc(s_mod, 1)

            def modulation_rows(l):
                dve.wait_ge(s_modT, l + 1)
                dve.tensor_copy(mod_rows[:], ps[0:96, (6, 1)[l], 0:P]).then_inc(s_modR, 1)

            def norm1(l, t):
                dve.wait_ge(s_sq, squares(f"1 of {l}") + t)
                sync(mean_square(stat[:, 1, t:t + 1], stat[:, 0, t:t + 1], D), s_ms)
                dve.wait_ge(s_rt, norm_step(f"1 of {l}") + t)
                step(dve.reciprocal(stat[:, 3, t:t + 1], stat[:, 2, t:t + 1]))
                ts(tokm[:, t], resid[:, t], stat[:, 3, t:t + 1], None, ALU.mult).then_inc(s_xn[l], 1)

            for l in range(LAYERS):
                if l == 0:
                    for t in range(TILES):
                        norm1(0, t)
                    for a in range(ADA_QKV):
                        sum_mod(a)
                    modulation(0, 0, 2)
                for k in range(KC):
                    dve.wait_ge(s_ht[l][1], k + 1)
                    ts(hT[:, k, CTX:CTX + SEQ], ps[:, 2 + k % 2, 0:SEQ], mod[:, l, KC + k, 1:2], mod[:, l, k, 1:2],
                       ALU.mult, ALU.add).then_inc(s_he[l][1], 1)

                for n, (g, t) in enumerate(qkv_jobs[l]):
                    if l == 0 and n % TILES == 0 and n > 0:
                        sum_mod(ADA_QKV + n // TILES - 1)
                    if qkv_copy[l][n][0] != "dve":
                        continue
                    m = qk_index[l][n]
                    dve.wait_ge(s_qm[l], n + 1)
                    lo = CONST_AT["cos"][0] + 32 * (t - CTX_TILES)
                    cos = cst[:, lo:lo + 32].unsqueeze(1).to_broadcast([P, 16, 32])
                    lo = CONST_AT["sin"][0] + 32 * (t - CTX_TILES)
                    sin = cst[:, lo:lo + 32].unsqueeze(1).to_broadcast([P, 16, 32])
                    src = ps[:, n % 2].rearrange("p (a b) -> p a b", b=32)
                    by_cos = tokm[:, 1, 0:STRIP].rearrange("p (a b) -> p a b", b=32)
                    by_sin = tokm[:, 1, STRIP:2 * STRIP].rearrange("p (a b) -> p a b", b=32)
                    scale = SCALE if g < 2 else 1.0
                    step(stt(by_cos, src, scale, cos, ALU.mult, ALU.mult))
                    step(stt(by_sin, src, scale, sin, ALU.mult, ALU.mult))
                    if m >= 2:
                        dve.wait_ge(s_qt[l], m - 1)
                    dst = tokm[:, 0, (m % 2) * STRIP:(m % 2 + 1) * STRIP].rearrange("p (a b) -> p a b", b=32)
                    step(tt(dst[:, 0::2], by_cos[:, 0::2], by_sin[:, 1::2], ALU.subtract))
                    sync(tt(dst[:, 1::2], by_cos[:, 1::2], by_sin[:, 0::2], ALU.add), s_qeD[l])

                if l == 0:
                    sum_mod(ADA_ATT - 1)

                    def maxima(u):
                        t, h = units[0][u]
                        nk = key_tiles(t) * P
                        dve.wait_ge(s_sc[0], u + 1)
                        if u >= 3:
                            dve.wait_ge(s_ex[0], 2 * (u - 2))
                        dve.tensor_reduce(att[:, u % 3, 0:2], ps[:, 2 * (u % 2):2 * (u % 2) + 2, 0:nk], X_AXIS, ALU.max,
                                          negate=True).then_inc(s_nm[0], 1)

                    def probs(u):
                        t, h = units[0][u]
                        nk = key_tiles(t) * P
                        a = att[:, u % 3]
                        dve.wait_ge(s_ex[0], 2 * u + 2)
                        step(dve.reciprocal(a[:, 6:8], a[:, 4:6]))
                        p0, p1 = hT[:, 2 * (u % 3), 0:nk], hT[:, 2 * (u % 3) + 1, 0:nk]
                        step(ts(p1, p1, a[:, 7:8], lam[:, 5:6], ALU.mult, ALU.mult))
                        stt(p0, p0, a[:, 6:7], p1, ALU.mult, ALU.add).then_inc(s_pr, 1)

                    U = len(units[0])
                    for u in range(U + 1):
                        if u < U:
                            maxima(u)
                        if u % 3 == 2 and u // 3 < ADA_PLAN - ADA_ATT:
                            a = ADA_ATT + u // 3
                            sum_mod(a)
                            if a == ADA - 1:
                                modulation(0, 2, 6)
                                modulation_rows(0)
                        if u >= 1:
                            probs(u - 1)
                    dve.wait_ge(s_hs, U)
                    dve.wait_ge(s_oe[0], U)
                    sync(mean_square(stat[:, 1], stat[:, 0], 2 * HD), s_ms)
                    dve.wait_ge(s_rt, norm_step("sub"))
                    step(dve.reciprocal(stat[:, 3], stat[:, 2]))
                    for m in range(TILES):
                        o = tokm[:, m].rearrange("p (h d) -> p h d", d=2 * HD)
                        r = stat[:, 3, 8 * m:8 * m + 8].unsqueeze(2).to_broadcast([P, DIFF_HEADS, 2 * HD])
                        tt(o, o, r, ALU.mult).then_inc(s_on, 1)
                else:
                    dve.wait_ge(s_bias_done, 2)

                    def scale_out(u):
                        t, h = units[1][u]
                        step(dve.reciprocal(att[:, u % 4, 3:4], att[:, u % 4, 2:3]))
                        dve.wait_ge(s_pv[1], u + 1)
                        ts(tokm[:, t, h * HD:(h + 1) * HD], ps[:, 5 + u % 2, 0:HD], att[:, u % 4, 3:4], None,
                           ALU.mult).then_inc(s_oe[1], 1)

                    for u, (t, h) in enumerate(units[1]):
                        a = att[:, u % 4]
                        lo = 2 - 2 * (t - CTX_TILES)
                        dve.wait_ge(s_sc[1], u + 1)
                        loc = ps[:, u % 4, CTX:CTX + SEQ]
                        step(tt(loc, loc, bias[:, h, lo:lo + GRID_H].rearrange("p r c -> p (r c)"), ALU.add))
                        dve.tensor_reduce(a[:, 0:1], ps[:, u % 4], X_AXIS, ALU.max, negate=True).then_inc(s_nm[1], 1)
                        if u >= 3:
                            scale_out(u - 3)
                    for u in range(len(units[1]) - 3, len(units[1])):
                        scale_out(u)

                if l == 0:
                    dve.wait_ge(s_rows, 16 * 8)
                else:
                    dve.wait_ge(s_rows, 16 * (8 + 4))

                def row(piece, t):
                    return rows[:, 2 * piece + (t >= CTX_TILES) if l == 0 else piece]

                def add_out(m, hf):
                    t = TILES_OF[l][m]
                    j = 2 * m + hf
                    cols = slice(hf * HALF, (hf + 1) * HALF)
                    dve.wait_ge(s_wm[l], j + 1)
                    step(tt(val[:, 0, cols], ps[:, j % 2], row(0, t)[:, cols], ALU.mult))
                    sync(tt(resid[:, t, cols], resid[:, t, cols], val[:, 0, cols], ALU.add), s_we[l])

                def norm2(m):
                    t = TILES_OF[l][m]
                    dve.wait_ge(s_sq, squares(f"2 of {l}") + m)
                    sync(mean_square(stat[:, 1, t:t + 1], stat[:, 0, t:t + 1], D), s_ms)
                    dve.wait_ge(s_rt, norm_step(f"2 of {l}") + m)
                    step(dve.reciprocal(stat[:, 3, t:t + 1], stat[:, 2, t:t + 1]))
                    step(stt(tokm[:, t], resid[:, t], stat[:, 3, t:t + 1], row(2, t), ALU.mult, ALU.mult))
                    sync(tt(tokm[:, t], tokm[:, t], row(1, t), ALU.add), s_h[l])

                def turned_h(m):
                    t = TILES_OF[l][m]
                    dve.wait_ge(s_h2t[l], 2 * m + 2)
                    dve.tensor_copy(hT[:, 4:8, t * P:(t + 1) * P],
                                    ps[:, 3].rearrange("p (k t) -> p k t", t=P)).then_inc(s_h2D[l], 1)

                for m in range(NT[l]):
                    add_out(m, 0)
                    add_out(m, 1)
                    norm2(m)
                    turned_h(m)

                nt = NT[l]
                w = nt * N_EXP

                def r3(i, a=nt, b=N_EXP, off=0):
                    return rt[:, i, off:off + a * b].rearrange("p (a b) -> p a b", b=b)

                dve.wait_ge(s_le[l], 1)
                step(ts(rt[:, 0, 0:w], rt[:, 0, 0:w], 1.0, None, ALU.add))
                step(dve.reciprocal(rt[:, 1, 0:w], rt[:, 0, 0:w]))
                rb = rbias[:].unsqueeze(1).to_broadcast([P, nt, N_EXP])
                step(tt(r3(2), r3(1), rb, ALU.add))
                sel = r3(2, nt * N_GRP, GRP)
                hi, lo = r3(3, nt * N_GRP, 2), r3(4, nt * N_GRP, 2)
                step(tt(hi, sel[:, :, 0:2], sel[:, :, 2:4], ALU.max))
                step(tt(lo, sel[:, :, 0:2], sel[:, :, 2:4], ALU.min))
                g5, g6, g7 = rt[:, 5, 0:nt * N_GRP], rt[:, 6, 0:nt * N_GRP], rt[:, 7, 0:nt * N_GRP]
                step(tt(g5.unsqueeze(2), hi[:, :, 0:1], hi[:, :, 1:2], ALU.max))
                step(tt(g6.unsqueeze(2), hi[:, :, 0:1], hi[:, :, 1:2], ALU.min))
                step(tt(g7.unsqueeze(2), lo[:, :, 0:1], lo[:, :, 1:2], ALU.max))
                step(tt(g6, g6, g7, ALU.max))
                step(tt(g5, g5, g6, ALU.add))

                def first_best(dst, src, rev, a, b, tmp):
                    mx = rt[:, 15, 0:a]
                    step(dve.tensor_reduce(mx, src, X_AXIS, ALU.max))
                    step(tt(tmp, src, mx.unsqueeze(2).to_broadcast([P, a, b]), ALU.is_equal))
                    step(tt(tmp, tmp, rev.unsqueeze(1).to_broadcast([P, a, b]), ALU.mult))
                    step(dve.tensor_reduce(mx, tmp, X_AXIS, ALU.max))
                    step(tt(dst, tmp, mx.unsqueeze(2).to_broadcast([P, a, b]), ALU.is_equal))

                first_best(r3(6, nt, N_GRP), r3(5, nt, N_GRP), const("rev_group"), nt, N_GRP, r3(7, nt, N_GRP))
                step(ts(g7, g6, NEG, -NEG, ALU.mult, ALU.add))
                s4 = r3(3, nt * N_GRP, GRP)
                step(tt(s4, sel, g6.unsqueeze(2).to_broadcast([P, nt * N_GRP, GRP]), ALU.mult))
                step(tt(s4, s4, g7.unsqueeze(2).to_broadcast([P, nt * N_GRP, GRP]), ALU.add))
                first_best(r3(8), r3(3), const("rev_expert"), nt, N_EXP, r3(4))
                step(stt(rt[:, 3, 0:w], rt[:, 8, 0:w], -3.0 * NEG, rt[:, 3, 0:w], ALU.mult, ALU.add))
                first_best(r3(9), r3(3), const("rev_expert"), nt, N_EXP, r3(4))
                sync(tt(rt[:, 10, 0:w], rt[:, 8, 0:w], rt[:, 9, 0:w], ALU.add), s_ch[l])
                for k in range(2):
                    step(tt(r3(4), r3(1), r3(8 + k), ALU.mult))
                    step(dve.tensor_reduce(wts[:, k, 0:nt], r3(4), X_AXIS, ALU.add))
                step(tt(rt[:, 5, 0:nt], wts[:, 0, 0:nt], wts[:, 1, 0:nt], ALU.add))
                step(dve.reciprocal(rt[:, 6, 0:nt], rt[:, 5, 0:nt]))
                step(tt(wts[:, :, 0:nt], wts[:, :, 0:nt], rt[:, 6, 0:nt].unsqueeze(1).to_broadcast([P, 2, nt]), ALU.mult))

                if l == 0:
                    for a in range(ADA_PLAN, ADA_PLAN + 2):
                        sum_mod(a)
                dve.wait_ge(s_rk[l], 1)
                total = ps[:, 4, 64:64 + N_EXP]
                nb, cum, base = rt[:, 5, 0:N_EXP], rt[:, 6, 0:N_EXP], rt[:, 7, 0:N_EXP]
                step(dve.tensor_copy(rt[:, 12, 0:N_EXP], total))
                step(ts(nb, rt[:, 12, 0:N_EXP], 0.0, None, ALU.is_gt))
                for b in range(1, nt):
                    step(stt(nb, rt[:, 12, 0:N_EXP], float(P * b), nb, ALU.is_gt, ALU.add))
                step(dve.tensor_tensor_scan(cum, nb, zeros[:], 0.0, ALU.add, ALU.add))
                step(tt(base, cum, nb, ALU.subtract))
                rank, full = rt[:, 2, 0:w], rt[:, 3, 0:w]
                step(dve.tensor_copy(rank, ps[:, 4, 0:w]))
                step(ts(full, rank, float(P), None, ALU.is_ge))
                for b in range(2, nt):
                    step(stt(full, rank, float(P * b), full, ALU.is_ge, ALU.add))
                step(stt(rank, full, -float(P), rank, ALU.mult, ALU.add))
                step(tt(r3(3), r3(3), base.unsqueeze(1).to_broadcast([P, nt, N_EXP]), ALU.add))
                for k in range(2):
                    for i, src in ((13, 3), (14, 2)):
                        step(tt(r3(4), r3(8 + k), r3(src), ALU.mult))
                        step(dve.tensor_reduce(rt[:, i, nt * k:nt * (k + 1)], r3(4), X_AXIS, ALU.add))
                for k in range(2):
                    for m in range(nt):
                        q = k * nt + m
                        dest = CONST_AT["dest"][0] + k * TILES + m
                        tok = CONST_AT["token"][0] + m
                        at_blk = rt[:, 13, q:q + 1]
                        ts(oh_slot[:, q], const("slot"), rt[:, 14, q:q + 1], None, ALU.is_equal).then_inc(s_oh[l], 1)
                        ts(oh_blk[:, q, 0:BLK_COLS], const("block"), at_blk, cst[:, tok:tok + 1],
                           ALU.is_equal, ALU.mult).then_inc(s_oh[l], 1)
                        ts(oh_blk[:, q, BLK_COLS:], const("block"), at_blk, cst[:, dest:dest + 1],
                           ALU.is_equal, ALU.mult).then_inc(s_oh[l], 1)
                pf = plan_f.rearrange("p (b e) -> p b e", e=N_EXP)
                blk0 = cst[0:1, CONST_AT["block"][0]:CONST_AT["block"][1]]
                step(tt(pf, blk0.unsqueeze(2).to_broadcast([1, BLK_COLS, N_EXP]),
                        cum[0:1].unsqueeze(1).to_broadcast([1, BLK_COLS, N_EXP]), ALU.is_ge))
                step(dve.tensor_reduce(slot_tab[0:1, 0:BLK_COLS], pf, X_AXIS, ALU.add))
                step(dve.tensor_copy(plan[:, 0:BLK_COLS], slot_tab[0:1, 0:BLK_COLS]))
                step(dve.tensor_copy(plan[:, BLK_COLS:], cum[0:1, N_EXP - 1:N_EXP]))
                if l == 0:
                    for a in range(ADA_PLAN + 2, 2 * ADA - 1):
                        sum_mod(a)
                dve.wait_ge(s_tab[l], 1)
                tab = ps[:, 4, P:P + 2 * BLK_COLS]
                step(ts(slot_tab, tab, 0.0, float(NO_ROW), ALU.is_equal, ALU.mult))
                sync(stt(slot_idx[:], tab, -1.0, slot_tab, ALU.add, ALU.add), s_idx[l])

                if l == 0:
                    sum_mod(2 * ADA - 1)
                    modulation(1, 0, 6)
                    modulation_rows(1)

                n = dve.value_load(plan[0:1, BLK_COLS:BLK_COLS + 1], min_val=1, max_val=MAX_BLOCKS)
                dve.sem_inc(m_ac[l], 1)
                dve.sem_inc(m_yD[l], 1)
                dve.wait_ge(m_xt[l], 2)
                dve.tensor_copy(blk_inT[:, 4:8], ps[:, 3].rearrange("p (k t) -> p k t", t=P)).then_inc(m_xD[l], 1)
                with dve.Fori(0, n) as i:
                    dve.wait_ge(m_si[l], i + 1)
                    dve.wait_ge(m_up[l], i + 2)
                    dve.wait_ge(m_at[l], i + 1)
                    tt(blk_act, ps[:, 1], blk_silu, ALU.mult).then_inc(m_ac[l], 1)
                    dve.wait_ge(m_xt[l], i * 2 + 4)
                    dve.tensor_copy(blk_inT[:, 4:8], ps[:, 3].rearrange("p (k t) -> p k t", t=P)).then_inc(m_xD[l], 1)
                    dve.wait_ge(m_dn[l], i * 2 + 4)
                    dve.wait_ge(m_sc[l], i * 16 + 16)
                    dve.tensor_copy(blk_out[:, HALF:], ps[:, 6]).then_inc(m_yD[l], 1)

                for m, t in enumerate(TILES_OF[l]):
                    dve.wait_ge(s_w1[l], m + 1)
                    y1, y2 = val[:, 2 * (m % 2)], val[:, 2 * (m % 2) + 1]
                    step(stt(y1, y2, wts[:, 1, m:m + 1], y1, ALU.mult, ALU.add))
                    step(tt(y1, y1, row(3, t), ALU.mult))
                    sync(tt(resid[:, t], resid[:, t], y1, ALU.add), s_cb[l])
                    if l == 0 and m >= 1:
                        norm1(1, m - 1)
                if l == 0:
                    norm1(1, TILES - 1)

            dve.wait_ge(s_sq, squares("2 of 1") + 2 * NT[1] - 1)
            dve.wait_ge(s_fg, 16)
            sync(mean_square(stat[:, 1, 0:TILES], stat[:, 0, 0:TILES], D), s_fms)
            dve.wait_ge(s_frt, 1)
            step(dve.reciprocal(stat[:, 3, 0:TILES], stat[:, 2, 0:TILES]))
            for m, t in enumerate(TILES_OF[1]):
                stt(tokm[:, t], resid[:, t], stat[:, 3, t:t + 1], rows[:, 4], ALU.mult, ALU.mult).then_inc(s_fin, 1)

        @block.tensor
        def _(pe):
            def turn(dst, src, rows_n=P):
                return pe.transpose(dst, src, ident[0:rows_n, 0:rows_n])

            def turn_mirrored(dst, src):
                return pe.matmul(dst, src, const("mirror"), start=True, stop=True)

            pe.wait_ge(s_small, 16 * SMALL_LOADS_ALL)
            turn(ps[:, 7, 0:N_VEC], vec_rows[0:N_VEC, :], N_VEC).then_inc(s_vec_t, 1)
            turn(ps[:, 7, P:P + 96], adab_rows[0:96, :], 96).then_inc(s_vec_t, 1)
            pe.wait_ge(s_cond, 2)
            pe.wait_ge(s_v, 1)
            pe.wait_ge(s_set, 1)

            def mod_products(a):
                wait_strip(pe, 0, at[0]["ada", a])
                if a >= 1:
                    pe.wait_ge(s_adc, a)
                    pe.wait_ge(s_adr, a)
                if a == ADA:
                    pe.wait_ge(s_modR, 1)
                if a == ADA_PLAN:
                    pe.wait_ge(s_we[0], 2 * NT[0])
                for k in range(KC):
                    q = 32 * (k % 4)
                    mm = pe.matmul(ps[q:q + 32, mod_banks(a)[0], :], cond[:, k, :], strip(0, at[0]["ada", a])[:, k, :],
                                   start=(k < 4), stop=(k >= 4), skip_group_check=True)
                mm.then_inc(s_ada, 1)

            def mod_turn(a):
                pe.wait_ge(s_adc, a + 1)
                for k in range(4):
                    mm = turn(ps[:, mod_banks(a)[1], k * P:(k + 1) * P], mod_part(a)[:, k * P:(k + 1) * P])
                mm.then_inc(s_adt, 1)

            def modulation_rows(l):
                pe.wait_ge(s_mod, l + 2)
                turn(ps[0:96, (6, 1)[l], 0:P], mod[:, l].rearrange("p j s -> p (j s)")).then_inc(s_modT, 1)

            for a in range(ADA_QKV):
                mod_products(a)
                mod_turn(a)

            for l in range(LAYERS):
                for s in range(2):
                    for k in range(KC):
                        if k == 0:
                            pe.wait_ge(s_xn[l], CTX_TILES * (s + 1))
                        if k >= 2:
                            pe.wait_ge(s_he[l][s], k - 1)
                        for t in range(2):
                            mm = turn(ps[:, 2 * s + k % 2, t * P:(t + 1) * P],
                                      tokm[:, 2 * s + t, k * P:(k + 1) * P])
                        mm.then_inc(s_ht[l][s], 1)
                for s in range(2):
                    pe.wait_ge(s_he[l][s], KC)

                def turn_qk(n):
                    m = qk_index[l][n]
                    _, copied, value = qkv_copy[l][n]
                    pe.wait_ge(copied, value)
                    if m >= 2:
                        pe.wait_ge(s_qc[l], m - 1)
                    mirrored = l == 1 and qkv_jobs[l][n][0] < 2
                    for k in range(4):
                        mm = (turn_mirrored if mirrored else turn)(ps[:, 4 + m % 2, k * P:(k + 1) * P],
                                  tokm[:, 0, (m % 2) * STRIP + k * P:(m % 2) * STRIP + (k + 1) * P])
                    mm.then_inc(s_qt[l], 1)

                for n, (g, t) in enumerate(qkv_jobs[l]):
                    st = at[l]["qkv", g]
                    wait_strip(pe, l, st)
                    if n >= 2:
                        kind, copied, value = qkv_copy[l][n - 2]
                        pe.wait_ge(copied, value)
                    for k in range(KC):
                        mm = pe.matmul(ps[:, n % 2], hT[:, k, t * P:(t + 1) * P], strip(l, st)[:, k, :],
                                       start=(k == 0), stop=(k == KC - 1))
                    mm.then_inc(s_qm[l], 1)
                    if n >= 1 and qk_index[l][n - 1] is not None:
                        turn_qk(n - 1)
                    if l == 0 and n % TILES == 1:
                        mod_products(ADA_QKV + n // TILES)
                    if l == 0 and n % TILES == 3:
                        mod_turn(ADA_QKV + n // TILES)
                pe.wait_ge(s_qc[l], N_QK[l])
                for _, copied, value in qkv_copy[l][-2:]:
                    pe.wait_ge(copied, value)

                if l == 0:
                    def scores(u):
                        t, h = units[0][u]
                        nk = key_tiles(t) * P
                        if u >= 2:
                            pe.wait_ge(s_ex[0], 2 * (u - 1))
                        for cc in range(2):
                            part = slice(cc * HD, (cc + 1) * HD)
                            mm = pe.matmul(ps[:, 2 * (u % 2) + cc, 0:nk], qT[part, h, t * P:(t + 1) * P],
                                           kT[part, h, 0:nk], start=True, stop=True)
                        mm.then_inc(s_sc[0], 1)

                    def turn_probs(u):
                        t, h = units[0][u]
                        pe.wait_ge(s_pr, u + 1)
                        if u >= 2:
                            pe.wait_ge(s_pc[0], u - 1)
                        for k in range(key_tiles(t)):
                            mm = turn(ps[:, (4, 7)[u % 2], k * P:(k + 1) * P], hT[:, 2 * (u % 3), k * P:(k + 1) * P])
                        mm.then_inc(s_pt[0], 1)

                    def attend(u):
                        t, h = units[0][u]
                        nk = key_tiles(t)
                        pe.wait_ge(s_pc[0], u + 1)
                        if u >= 1:
                            pe.wait_ge(s_oe[0], u)
                        for k in range(nk):
                            mm = pe.matmul(ps[:, 5, 0:2 * HD], hT[:, 6 + u % 2, k * P:(k + 1) * P],
                                           val[:, k, h * 2 * HD:(h + 1) * 2 * HD], start=(k == 0), stop=(k == nk - 1))
                        mm.then_inc(s_pv[0], 1)

                    U = len(units[0])
                    for u in range(U + 3):
                        if u < U:
                            scores(u)
                        if u % 3 == 0 and u // 3 < ADA_PLAN - ADA_ATT:
                            mod_products(ADA_ATT + u // 3)
                        if 2 <= u < U + 2:
                            turn_probs(u - 2)
                        if u >= 3:
                            attend(u - 3)
                        if u % 3 == 1 and u // 3 < ADA_PLAN - ADA_ATT:
                            mod_turn(ADA_ATT + u // 3)
                        if u == 3 * (ADA - ADA_ATT - 1) + 2:
                            modulation_rows(0)
                else:
                    def scores1(u):
                        t, h = units[1][u]
                        if u >= 4:
                            pe.wait_ge(s_ex[1], u - 3)
                        part = slice((h % 2) * HD, (h % 2 + 1) * HD)
                        pe.matmul(ps[:, u % 4], qT[part, h // 2, t * P:(t + 1) * P], kT[part, h // 2, :],
                                  start=True, stop=True).then_inc(s_sc[1], 1)

                    def turn_probs1(u):
                        pe.wait_ge(s_ex[1], u + 1)
                        if u >= 2:
                            pe.wait_ge(s_pc[1], u - 1)
                        for k in range(TILES):
                            mm = turn(ps[:, (4, 7)[u % 2], k * P:(k + 1) * P], hT[:, u % 4, k * P:(k + 1) * P])
                        mm.then_inc(s_pt[1], 1)

                    def attend1(u):
                        t, h = units[1][u]
                        pe.wait_ge(s_pc[1], u + 1)
                        if u >= 2:
                            pe.wait_ge(s_oe[1], u - 1)
                        for k in range(TILES):
                            mm = pe.matmul(ps[:, 5 + u % 2, 0:HD], hT[:, 4 + u % 2, k * P:(k + 1) * P],
                                           val[:, k, h * HD:(h + 1) * HD], start=(k == 0), stop=(k == TILES - 1))
                        mm.then_inc(s_pv[1], 1)

                    U = len(units[1])
                    for u in range(U + 3):
                        if u < U:
                            scores1(u)
                        if 2 <= u < U + 2:
                            turn_probs1(u - 2)
                        if u >= 3:
                            attend1(u - 3)

                def turn_out(m):
                    t = TILES_OF[l][m]
                    if l == 0:
                        pe.wait_ge(s_on, m + 1)
                    elif m == 0:
                        pe.wait_ge(s_oe[1], len(units[1]))
                    for hf in range(2):
                        if m >= 1:
                            pe.wait_ge(s_oc[l], 2 * (m - 1) + hf + 1)
                        for k in range(4):
                            mm = (turn_mirrored if l == 1 else turn)(
                                ps[:, 4 + hf, k * P:(k + 1) * P], tokm[:, t, (4 * hf + k) * P:(4 * hf + k + 1) * P])
                        mm.then_inc(s_ot[l], 1)

                def project_out(m):
                    t = TILES_OF[l][m]
                    pe.wait_ge(s_oc[l], 2 * m + 2)
                    for hf in range(2):
                        j = 2 * m + hf
                        wait_strip(pe, l, at[l]["wo", hf])
                        if j >= 2:
                            pe.wait_ge(s_we[l], j - 1)
                        for k in range(KC):
                            mm = pe.matmul(ps[:, j % 2], hT[:, k, t * P:(t + 1) * P],
                                           strip(l, at[l]["wo", hf])[:, k, :], start=(k == 0), stop=(k == KC - 1))
                        mm.then_inc(s_wm[l], 1)

                def logits(m):
                    t = TILES_OF[l][m]
                    pe.wait_ge(s_h[l], m + 1)
                    for hf in range(2):
                        if m >= 1:
                            pe.wait_ge((s_h2A, s_h2D)[hf][l], m)
                        for k in range(4):
                            mm = turn(ps[:, 2 + hf, k * P:(k + 1) * P], tokm[:, t, (4 * hf + k) * P:(4 * hf + k + 1) * P])
                        mm.then_inc(s_h2t[l], 1)
                    pe.wait_ge(s_h2A[l], m + 1)
                    pe.wait_ge(s_h2D[l], m + 1)
                    for k in range(KC):
                        mm = pe.matmul(ps[:, 6, m * N_EXP:(m + 1) * N_EXP], hT[:, k, t * P:(t + 1) * P], rw[:, k, :],
                                       start=(k == 0), stop=(k == KC - 1))
                    mm.then_inc(s_lg[l], 1)

                for m in range(NT[l]):
                    turn_out(m)
                    project_out(m)
                    if m >= 1:
                        logits(m - 1)
                logits(NT[l] - 1)

                pe.wait_ge(s_set, 3 + l)
                if l == 0:
                    for a in range(ADA_PLAN, ADA_PLAN + 2):
                        mod_products(a)
                        mod_turn(a)
                pe.wait_ge(s_oc[l], 2 * NT[l])
                pe.wait_ge(s_ch[l], 1)
                nt = NT[l]
                for m in range(nt):
                    for j in range(m + 1):
                        pe.matmul(ps[:, 4, m * N_EXP:(m + 1) * N_EXP], const("before") if j == m else ones,
                                  rt[:, 10, j * N_EXP:(j + 1) * N_EXP], start=(j == 0), stop=(j == m))
                for j in range(nt):
                    mm = pe.matmul(ps[:, 4, 64:64 + N_EXP], ones, rt[:, 10, j * N_EXP:(j + 1) * N_EXP],
                                   start=(j == 0), stop=(j == nt - 1))
                mm.then_inc(s_rk[l], 1)
                if l == 0:
                    for a in range(ADA_PLAN + 2, 2 * ADA - 1):
                        mod_products(a)
                        mod_turn(a)
                pe.wait_ge(s_oh[l], 3 * 2 * nt)
                for q in range(2 * nt):
                    mm = pe.matmul(ps[:, 4, P:P + 2 * BLK_COLS], oh_slot[:, q], oh_blk[:, q], start=(q == 0),
                                   stop=(q == 2 * nt - 1))
                mm.then_inc(s_tab[l], 1)

                if l == 0:
                    mod_products(2 * ADA - 1)
                    mod_turn(2 * ADA - 1)
                    modulation_rows(1)
                    pe.wait_ge(s_modR, 2)

                def turn_block(gathered):
                    pe.wait_ge(m_ga[l], gathered)
                    for hf in range(2):
                        for k in range(4):
                            mm = turn(ps[:, 2 + hf, k * P:(k + 1) * P],
                                      blk_in[:, (4 * hf + k) * P:(4 * hf + k + 1) * P])
                        mm.then_inc(m_xt[l], 1)

                pe.wait_ge(s_idx[l], 1)
                n = pe.value_load(plan[0:1, BLK_COLS:BLK_COLS + 1], min_val=1, max_val=MAX_BLOCKS)
                for count, start in ((m_gt, 1), (m_up, 1), (m_dn, 2), (m_at, 1)):
                    pe.sem_inc(count[l], start)
                turn_block(16)
                down = ring[:, 2].rearrange("p k n -> p (k n)").rearrange("p (k n) -> p k n", n=D)
                with pe.Fori(0, n) as i:
                    pe.wait_ge(m_xA[l], i + 1)
                    pe.wait_ge(m_xD[l], i + 1)
                    pe.wait_ge(m_wl[l][0], i * 16 + 16)
                    for k in range(KC):
                        mm = pe.matmul(ps[:, 0], blk_inT[:, k, :], ring[:, 0, k, :], start=(k == 0), stop=(k == KC - 1))
                    mm.then_inc(m_gt[l], 1)
                    pe.wait_ge(m_wl[l][1], i * 16 + 16)
                    for k in range(KC):
                        mm = pe.matmul(ps[:, 1], blk_inT[:, k, :], ring[:, 1, k, :], start=(k == 0), stop=(k == KC - 1))
                    mm.then_inc(m_up[l], 1)
                    turn_block(i * 16 + 32)
                    pe.wait_ge(m_ac[l], i + 2)
                    for k in range(FF // P):
                        mm = turn(ps[:, 4, k * P:(k + 1) * P], blk_act[:, k * P:(k + 1) * P])
                    mm.then_inc(m_at[l], 1)
                    pe.wait_ge(m_ae[l], i + 1)
                    pe.wait_ge(m_wl[l][2], i * 16 + 16)
                    for hf in range(2):
                        pe.wait_ge((m_yA, m_yD)[hf][l], i + 1)
                        for k in range(FF // P):
                            mm = pe.matmul(ps[:, 5 + hf], blk_actT[:, k, :], down[:, k, hf * HALF:(hf + 1) * HALF],
                                           start=(k == 0), stop=(k == FF // P - 1))
                        mm.then_inc(m_dn[l], 1)
                pe.wait_ge(m_xA[l], n + 1)
                pe.wait_ge(m_xD[l], n + 1)
                pe.wait_ge(m_yA[l], n + 1)
                pe.wait_ge(m_yD[l], n + 1)


_INS = ["x", "c", "ctx", "c_ctx", "ada_w", "ada_b", "norm1_g", "norm2_g", "final_norm_g", "diff_w_qkv", "diff_w_o",
        "diff_lambda_q1", "diff_lambda_k1", "diff_lambda_q2", "diff_lambda_k2", "diff_subln_g",
        "na_w_qkv", "na_w_o", "na_rpb", "router_w", "router_bias", "moe_w_gate", "moe_w_up", "moe_w_down"]


def kernel(**inputs):
    import concourse.bacc as bacc
    from concourse.bass_utils import run_bass_kernel_spmd

    nc = bacc.Bacc("TRN2", target_bir_lowering=False, num_devices=1)
    arrays, args = {}, []
    for name in _INS + ["consts"]:
        a = constants() if name == "consts" else np.ascontiguousarray(inputs[name])
        arrays[f"in_{name}_dram"] = a
        args.append(nc.dram_tensor(f"in_{name}_dram", a.shape, mybir.dt.from_np(a.dtype), kind="ExternalInput").ap())
    out = nc.dram_tensor("out_dram", (1, SEQ, D), F32, kind="ExternalOutput").ap()
    build_trunk(nc, *args, out)
    r = run_bass_kernel_spmd(nc, [arrays], core_ids=[0])
    return r.results[0]["out_dram"]
```

```python
import math
from contextlib import ExitStack

import numpy as np

import concourse.bass as bass
from concourse import mybir

F32 = mybir.dt.float32
F32R = mybir.dt.float32r
I32 = mybir.dt.int32
ALU = mybir.AluOpType
ACT = mybir.ActivationFunctionType
X_AXIS = mybir.AxisListType.X

P = 128
D = 1024
KC = D // P
SEQ = 256
CTX = 256
LAYERS = 2
TILES = (SEQ + CTX) // P
CTX_TILES = CTX // P
GRID_W = 64
GRID_H = SEQ // GRID_W
HD = 64
SCALE = HD ** -0.5
EPS = 1e-6
DIFF_HEADS = D // (2 * HD)
NA_HEADS = D // HD
NA_WR, NA_WC = 8, 16
RPB_H, RPB_W = 2 * NA_WR - 1, 2 * NA_WC - 1
ROPE_THETA = 10000.0
LAMBDA_INIT = 0.8 - 0.6 * math.exp(-0.3 * 0)
N_EXP, N_GRP = 16, 4
GRP = N_EXP // N_GRP
FF = 512
STRIP = 512
NEG = 1e30
NO_ROW = 100000
SLOTS = 64
GROUPS = P // SLOTS
MAX_BLOCKS = N_EXP + (2 * (SEQ + CTX) - N_EXP) // SLOTS
BLK_COLS = MAX_BLOCKS + 1
LIMITS = 2 * (SEQ + CTX) // SLOTS // 2

TILES_OF = [list(range(TILES)), list(range(CTX_TILES, TILES))]

CONST_PARTS = [("ident", P), ("mirror", P), ("before", P), ("slot", SLOTS), ("half", 1), ("limit", LIMITS), ("block", BLK_COLS), ("rev_expert", N_EXP),
               ("rev_group", N_GRP), ("token", TILES), ("dest", 2 * TILES), ("cos", 2 * 32), ("sin", 2 * 32),
               ("valid", GRID_W), ("invalid", GRID_W)]
CONST_AT, _at = {}, 0
for _name, _n in CONST_PARTS:
    CONST_AT[_name] = (_at, _at + _n)
    _at += _n
CONST_COLS = _at

VEC_ROWS = {"c_ctx": (0, 8), "c": (8, 16), "norm1": (16, 32), "norm2": (32, 48), "subln": (48, 49)}
N_VEC = 49


def constants():
    t = np.zeros((P, CONST_COLS), np.float32)

    def put(name, a):
        lo, hi = CONST_AT[name]
        t[:, lo:hi] = a

    p = np.arange(P)
    put("ident", np.eye(P))
    mirrored = p // GRID_W * GRID_W + GRID_W - 1 - p % GRID_W
    put("mirror", mirrored[:, None] == p[None, :])
    put("before", p[:, None] < p[None, :])
    put("slot", np.broadcast_to(np.arange(SLOTS), (P, SLOTS)))
    put("half", (p // SLOTS)[:, None] - GROUPS)
    put("limit", np.broadcast_to(SLOTS * np.arange(LIMITS), (P, LIMITS)))
    put("block", np.broadcast_to(np.arange(BLK_COLS), (P, BLK_COLS)))
    put("rev_expert", np.broadcast_to(N_EXP - np.arange(N_EXP), (P, N_EXP)))
    put("rev_group", np.broadcast_to(N_GRP - np.arange(N_GRP), (P, N_GRP)))
    put("token", p[:, None] + P * np.arange(TILES) + 1)
    put("dest", p[:, None] + P * np.arange(2 * TILES) + 1)
    tok = np.arange(SEQ)
    inv = (np.float32(ROPE_THETA) ** (-np.arange(HD // 4, dtype=np.float32) / np.float32(HD // 4))).astype(np.float32)
    row, col = (tok // GRID_W).astype(np.float32), (tok % GRID_W).astype(np.float32)
    ang = np.concatenate([row[:, None] * inv, col[:, None] * inv], -1).astype(np.float32)
    put("cos", np.cos(ang).reshape(2, P, 32).transpose(1, 0, 2).reshape(P, 64))
    put("sin", np.sin(ang).reshape(2, P, 32).transpose(1, 0, 2).reshape(P, 64))
    c = mirrored % GRID_W
    c0 = np.clip(c - NA_WC // 2, 0, GRID_W - NA_WC)[:, None]
    keys = np.arange(GRID_W)[None, :]
    valid = (keys >= c0) & (keys < c0 + NA_WC)
    put("valid", valid)
    put("invalid", np.where(valid, 0.0, -NEG))
    return t


def build_trunk(nc, x, c, ctx, c_ctx, ada_w, ada_b, norm1_g, norm2_g, final_norm_g, diff_w_qkv, diff_w_o,
                diff_lambda_q1, diff_lambda_k1, diff_lambda_q2, diff_lambda_k2, diff_subln_g,
                na_w_qkv, na_w_o, na_rpb, router_w, router_bias, moe_w_gate, moe_w_up, moe_w_down,
                consts, out):
    with ExitStack() as stack:
        def sb(name, shape, dt=F32):
            return stack.enter_context(nc.sbuf_tensor(name, shape, dt))

        def sem(name):
            return stack.enter_context(nc.semaphore(name))

        with ExitStack() as shared:
            def part(name, shape):
                return shared.enter_context(nc.sbuf_tensor(name, shape, F32R))

            part("over_val", [P, TILES // 2, D])
            o_high = part("o_high", [P, 2, KC, P])
            x_low = part("x_low", [P, KC, TILES * P])
            part("over_tokm", [P, TILES // 2, D])
            w_high = [part("w_high_2", [P, KC // 2, STRIP])]
            w_low = part("w_low", [P, 3, KC, STRIP])
            x_high = part("x_high", [P, KC, TILES * P])
            w_high = [part(f"w_high_{i}", [P, KC // 2, STRIP]) for i in range(2)] + w_high
            part("over_cst", [P, CONST_COLS])
            part("over_resid", [P, TILES, D])
            wo_high = part("wo_high", [P, 2, KC, STRIP])
        with nc.sbuf_tensor("expert_sets", [P, 2, 3, KC * STRIP], F32) as expert_sets:
            pass
        val = sb("val", [P, TILES, D])
        hT = sb("hT", [P, KC, TILES * P])
        tokm = sb("tokm", [P, TILES, D])
        ring = sb("ring", [P, 3, KC, STRIP])
        rows = sb("rows", [P, 8, D])
        cst = sb("cst", [P, CONST_COLS])
        resid = sb("resid", [P, TILES, D])
        qT = sb("qT", [P, KC, TILES * P])
        kT = sb("kT", [P, KC, TILES * P])
        bias = sb("bias", [P, NA_HEADS, 6, GRID_W])
        vec = sb("vec", [P, N_VEC])
        adab = sb("adab", [P, LAYERS * 48])
        cond = sb("cond", [P, KC, 32])
        mod = sb("mod", [P, LAYERS, 48, 2])
        mod_rows = sb("mod_rows", [96, P])
        rw = sb("rw", [P, KC, N_EXP])
        rbias = sb("rbias", [P, N_EXP])
        lam = sb("lam", [P, 8])
        subln = sb("subln", [P, 1])
        stat = sb("stat", [P, 4, 4 * DIFF_HEADS])
        att = sb("att", [P, 4, 8])
        zeros = cond[:, 0, 2:2 + N_EXP]
        wts = sb("wts", [P, 2, TILES])
        slot_idx = sb("slot_idx", [P, 2 * BLK_COLS], I32)
        plan = sb("plan", [1, 1 + N_EXP], I32)
        gather_idx = sb("gather_idx", [P, 1], I32)
        scatter_idx = sb("scatter_idx", [P, 1], I32)
        ps = stack.enter_context(nc.psum_tensor("ps", [P, 8, 512], F32))

        vec_rows = val[:, 1, 0:P]
        adab_rows = val[:, 2, 0:P]
        lam_in = val[:, 3, 0:4 * HD].rearrange("p (a b) -> p a b", b=HD)

        NORM_AT = {"1 of 0": 0, "sub": TILES, "2 of 0": TILES + 1, "1 of 1": 2 * TILES + 1, "2 of 1": 3 * TILES + 1}

        def norm_step(name):
            return NORM_AT[name] + 1

        def squares(name):
            return NORM_AT[name] + (name == "1 of 0")

        FG = FF // GROUPS
        DG = D // GROUPS
        blk_in = qT[:, 0, :]
        blk_inT = qT[:, 1, :].rearrange("p (k t) -> p k t", t=P)
        blk_silu = qT[:, 2, 0:FG]
        blk_act = qT[:, 3, 0:FG]
        blk_actT = qT[:, 4, 0:FG].rearrange("p (k t) -> p k t", t=P)
        blk_out = kT[:, 0, :]

        q_odd0 = bias[:].rearrange("p h r c -> p (h r c)")[:, 0:KC * TILES * P].rearrange("p (k t) -> p k t", k=KC)

        last_gate0 = [bias[:].rearrange("p h r c -> p (h r c)")[:, s * D:(s + 1) * D] for s in range(2)]

        oh_slot = kT[:, 2, :].rearrange("p (q s) -> p q s", s=SLOTS)
        oh_blk = kT[:, 3:5, :].rearrange("p a b -> p (a b)").rearrange("p (i q s) -> p i q s", i=2, s=BLK_COLS)
        above = kT[:, 4, :]
        rt = kT[:, 5:7, :].rearrange("p a b -> p (a b)").rearrange("p (i w) -> p i w", w=TILES * N_EXP)
        slot_tab = rt[:, 0, 0:2 * BLK_COLS]
        ones = kT[:, 1, 0:P]

        h_dram = [nc.dram_tensor(f"h_rows_{l}", [TILES * P, D], F32).ap() for l in range(LAYERS)]
        y_dram = [nc.dram_tensor(f"expert_rows_{l}", [2 * TILES * P, D], F32).ap() for l in range(LAYERS)]
        mod_dram = [nc.dram_tensor(f"mod_rows_{l}", [96, P], F32) for l in range(LAYERS)]

        def const(name, n=None):
            lo, hi = CONST_AT[name]
            return cst[:, lo:hi]

        ident = const("ident")

        s_small = sem("vectors_loaded")
        s_late = sem("late_vectors_loaded")
        s_whi, s_wlo = sem("weights_high"), sem("weights_low")
        s_xhi, s_xlo = sem("inputs_high"), sem("inputs_low")
        s_half = sem("first_halves_used")
        s_x = sem("streams_loaded")
        s_bias = sem("bias_loaded")
        s_bias_done = sem("bias_masked")
        s_set = sem("fills_done")
        s_vec_t = sem("vectors_turned")
        s_vec = sem("vectors_copied")
        s_cond = sem("cond_ready")
        s_lam = sem("lambda_steps")
        s_lam_exp = sem("lambda_exps")
        s_v = sem("vector_steps")
        s_ada = sem("mod_products")
        s_adc = sem("mod_products_copied")
        s_adt = sem("mod_products_turned")
        s_adr = sem("mod_products_summed")
        s_mod = sem("mod_ready")
        s_modT = sem("mod_turned")
        s_modR = sem("mod_rows_copied")
        s_modD = sem("mod_rows_stored")
        s_rows = sem("rows_loaded")
        s_sq = sem("squares")
        s_ms = sem("mean_squares")
        s_rt = sem("roots")
        s_xn = [sem(f"normalised_{l}") for l in range(LAYERS)]
        s_ht = [[sem(f"h_turned_{l}_{s}") for s in range(2)] for l in range(LAYERS)]
        s_heA = [sem(f"h_modulated_act_{l}") for l in range(LAYERS)]
        s_heD = [sem(f"h_modulated_dve_{l}") for l in range(LAYERS)]
        s_qm = [sem(f"qkv_products_{l}") for l in range(LAYERS)]
        s_qeA = [sem(f"qkv_copied_act_{l}") for l in range(LAYERS)]
        s_qeD = [sem(f"qkv_copied_dve_{l}") for l in range(LAYERS)]
        s_qt = [sem(f"qk_turned_{l}") for l in range(LAYERS)]
        s_qc = [sem(f"qk_turned_copied_{l}") for l in range(LAYERS)]
        s_sc = [sem(f"scores_{l}") for l in range(LAYERS)]
        s_nm = [sem(f"maxima_{l}") for l in range(LAYERS)]
        s_ex = [sem(f"exps_{l}") for l in range(LAYERS)]
        s_pr = sem("diff_probs")
        s_pt = [sem(f"probs_turned_{l}") for l in range(LAYERS)]
        s_pc = [sem(f"probs_turned_copied_{l}") for l in range(LAYERS)]
        s_pv = [sem(f"attended_{l}") for l in range(LAYERS)]
        s_oe = [sem(f"attended_copied_{l}") for l in range(LAYERS)]
        s_on = sem("heads_normalised")
        s_hs = sem("head_squares")
        s_w1 = [sem(f"first_experts_weighed_{l}") for l in range(LAYERS)]
        s_ot = [sem(f"o_turned_{l}") for l in range(LAYERS)]
        s_oc = [sem(f"o_turned_copied_{l}") for l in range(LAYERS)]
        s_wm = [sem(f"wo_products_{l}") for l in range(LAYERS)]
        s_we = [sem(f"wo_added_{l}") for l in range(LAYERS)]
        s_h = [sem(f"h2_ready_{l}") for l in range(LAYERS)]
        s_hst = [sem(f"h2_stored_{l}") for l in range(LAYERS)]
        s_h2t = [sem(f"h2_turned_{l}") for l in range(LAYERS)]
        s_h2A = [sem(f"h2_turned_copied_act_{l}") for l in range(LAYERS)]
        s_h2D = [sem(f"h2_turned_copied_dve_{l}") for l in range(LAYERS)]
        s_lg = [sem(f"logits_{l}") for l in range(LAYERS)]
        s_le = [sem(f"logit_exps_{l}") for l in range(LAYERS)]
        s_ch = [sem(f"choices_{l}") for l in range(LAYERS)]
        s_rk = [sem(f"ranks_{l}") for l in range(LAYERS)]
        s_oh = [sem(f"slot_marks_{l}") for l in range(LAYERS)]
        s_tab = [sem(f"slot_table_{l}") for l in range(LAYERS)]
        s_idx = [sem(f"plan_ready_{l}") for l in range(LAYERS)]
        m_wl = [[sem(f"expert_{w}_loaded_{l}") for w in ("gate", "up", "down")] for l in range(LAYERS)]
        m_gt = [sem(f"block_gates_{l}") for l in range(LAYERS)]
        m_up = [sem(f"block_ups_{l}") for l in range(LAYERS)]
        m_dn = [sem(f"block_downs_{l}") for l in range(LAYERS)]
        m_xt = [sem(f"block_in_turned_{l}") for l in range(LAYERS)]
        m_xc = [sem(f"block_in_copied_{l}") for l in range(LAYERS)]
        m_si = [sem(f"block_silu_{l}") for l in range(LAYERS)]
        m_ac = [sem(f"block_act_{l}") for l in range(LAYERS)]
        m_at = [sem(f"block_act_turned_{l}") for l in range(LAYERS)]
        m_ae = [sem(f"block_act_turned_copied_{l}") for l in range(LAYERS)]
        m_y = [sem(f"block_out_{l}") for l in range(LAYERS)]
        m_ix = [sem(f"block_indices_{l}") for l in range(LAYERS)]
        m_ga = [sem(f"block_gathered_{l}") for l in range(LAYERS)]
        m_sc = [sem(f"block_scattered_{l}") for l in range(LAYERS)]
        s_yl = [[sem(f"expert_rows_loaded_{l}_{b}") for b in range(2)] for l in range(LAYERS)]
        s_cb = [sem(f"combined_{l}") for l in range(LAYERS)]
        s_fg = sem("final_gain_loaded")
        s_fms, s_frt = sem("final_mean_squares"), sem("final_roots")
        s_turn = sem("pool_turns")
        s_turn_sp = sem("sp_turns")
        s_fin = sem("final_ready")
        s_out = sem("out_stored")
        s_ld = [[sem(f"strip_loaded_{l}_{s}") for s in range(3)] for l in range(LAYERS)]

        QKV = [diff_w_qkv, na_w_qkv]
        WO = [diff_w_o, na_w_o]
        ADA, ADA_QKV, ADA_ATT, ATT_STEP = 12, 4, 16, 3
        qkv_jobs, strips, at = [], [], []
        slot_of_next = 0
        for l in range(LAYERS):
            groups = (range(6), (2, 3, 4, 5, 0, 1))[l]
            jobs = [(g, t) for g in groups for t in (TILES_OF[l] if g < 2 else range(TILES))]
            qkv_jobs.append(jobs)
            plan_l = []
            index = {}

            def add(kind, j, entry, slot=None):
                global_slot = (plan_l[-1][4] + 1) % 3 if plan_l else slot_of_next
                index[kind, j] = len(plan_l)
                plan_l.append(entry + (global_slot if slot is None else slot,))

            def add_ada(a, slot=None):
                add("ada", a, (ada_w[a // ADA], a % ADA, s_ada, a + 1), slot)

            def add_qkv(g, slot=None):
                last = max(n for n, (gg, _) in enumerate(jobs) if gg == g)
                add("qkv", g, (QKV[l][0], g, s_qm[l], last + 1), slot)

            if l == 0:
                for a, slot in enumerate((1, 0, 2, 1)):
                    add_ada(a, slot)
                add_qkv(0, 0)
                add_ada(ADA_QKV, 1)
                for g in range(1, 6):
                    add_qkv(g, 2 * (g % 2))
                    add_ada(ADA_QKV + 2 * g - 1, 1)
                    add_ada(ADA_QKV + 2 * g, 1)
                add_ada(ADA_QKV + 11, 1)
                for a in range(ADA_ATT, 2 * ADA):
                    add_ada(a, (a - ADA_ATT) % 3)
            else:
                for g in groups:
                    add_qkv(g)
            for j in range(2):
                add("wo", j, (WO[l][0], j, s_wm[l], 2 * len(TILES_OF[l]) - 1 + j))
            strips.append(plan_l)
            at.append(index)
            slot_of_next = (plan_l[-1][4] + 1) % 3

        def strip(l, j):
            return ring[:, strips[l][j][4]]

        def before_in_slot(l, slot, j):
            return max((i for i in range(j) if strips[l][i][4] == slot), default=None)

        def expert_slot(l, w):
            return (strips[l][-1][4] + 1 + w) % 3

        def expert_strip(l, w, which):
            return expert_sets[:, which, expert_slot(l, w), :].rearrange("p (k n) -> p k n", n=D if w == 2 else STRIP)

        def wait_strip(eng, l, j):
            slot = strips[l][j][4]
            eng.wait_ge(s_ld[l][slot], 16 * sum(entry[4] == slot for entry in strips[l][:j + 1]))

        qkv_pos = []
        for l in range(LAYERS):
            gs = list(dict.fromkeys(g for g, _ in qkv_jobs[l]))
            qkv_pos.append([(gs.index(g), sum(gg == g for gg, _ in qkv_jobs[l][:n]), g not in
                             [gg for gg, _ in qkv_jobs[l][n + 1:]]) for n, (g, _) in enumerate(qkv_jobs[l])])

        HALF_STRIPS = 2 * (6 + 2)
        HALF_INPUTS = [4 + 2 * len(t) for t in TILES_OF]

        def split_wo(eng, l, j):
            st = at[l]["wo", j]
            for half in range(2):
                ks = slice(half * KC // 2, (half + 1) * KC // 2)
                if eng is nc.scalar:
                    wait_strip(eng, l, st)
                    eng.wait_ge(s_sc[l], len(units[l]))
                    eng.copy(wo_high[:, j, ks], strip(l, st)[:, ks]).then_inc(s_whi, 1)
                else:
                    eng.wait_ge(s_whi, HALF_STRIPS * l + 12 + 2 * j + half + 1)
                    eng.tensor_tensor(w_low[:, strips[l][st][4], ks], strip(l, st)[:, ks], wo_high[:, j, ks],
                                      ALU.subtract).then_inc(s_wlo, 1)

        def split_out(eng, l, m):
            t = TILES_OF[l][m]
            for half in range(2):
                ks, cols = slice(half * KC // 2, (half + 1) * KC // 2), slice(t * P, (t + 1) * P)
                if eng is nc.scalar:
                    eng.wait_ge(s_oc[l], 2 * m + half + 1)
                    if m >= 2:
                        eng.wait_ge(s_wm[l], 2 * (m - 1))
                    eng.copy(o_high[:, m % 2, ks], hT[:, ks, cols]).then_inc(s_xhi, 1)
                else:
                    eng.wait_ge(s_xhi, sum(HALF_INPUTS[:l]) + 4 + 2 * m + half + 1)
                    eng.tensor_tensor(x_low[:, ks, cols], hT[:, ks, cols], o_high[:, m % 2, ks],
                                      ALU.subtract).then_inc(s_xlo, 1)

        def split_weights(eng, l, p, half):
            g = qkv_jobs[l][[pos[0] for pos in qkv_pos[l]].index(p)][0]
            st = at[l]["qkv", g]
            number = HALF_STRIPS * l + 2 * p + half
            high = w_high[(2 * p + half) % 3][:]
            ks = slice(half * KC // 2, (half + 1) * KC // 2)
            if eng is nc.scalar:
                wait_strip(eng, l, st)
                if p == 1 and half == 0:
                    eng.wait_ge(s_ht[l][1], KC // 2)
                if half == 1 and p > 0:
                    eng.wait_ge(s_half, 6 * l + p)
                elif p > 1:
                    first = [pos[0] for pos in qkv_pos[l]].index(p - 1)
                    eng.wait_ge(s_qm[l], first)
                eng.copy(high, strip(l, st)[:, ks]).then_inc(s_whi, 1)
            else:
                eng.wait_ge(s_whi, number + 1)
                eng.tensor_tensor(w_low[:, strips[l][st][4], ks], strip(l, st)[:, ks], high,
                                  ALU.subtract).then_inc(s_wlo, 1)

        def split_inputs(eng, l, s, half):
            ks, cols = slice(half * KC // 2, (half + 1) * KC // 2), slice(s * CTX, s * CTX + (CTX, SEQ)[s])
            number = sum(HALF_INPUTS[:l]) + 2 * s + half
            if eng is nc.scalar:
                for copied in (s_heA, s_heD):
                    eng.wait_ge(copied[l], s * KC // 2 + (half + 1) * KC // 4)
                eng.copy(x_high[:, ks, cols], hT[:, ks, cols]).then_inc(s_xhi, 1)
            else:
                eng.wait_ge(s_xhi, number + 1)
                eng.tensor_tensor(x_low[:, ks, cols], hT[:, ks, cols], x_high[:, ks, cols],
                                  ALU.subtract).then_inc(s_xlo, 1)

        STREAM_BANKS = [(0, 1, 2, 3), (2, 3, 6, 7)]

        def stream_in(eng, l, s):
            for half in range(2):
                j = 2 * half + (eng is nc.vector)
                eng.wait_ge(s_ht[l][s], j + 1)
                for c in range(2):
                    k = 2 * j + c
                    src = ps[:, STREAM_BANKS[s][j], c * 2 * P:(c + 1) * 2 * P]
                    dst = hT[:, k, s * 2 * P:(s + 1) * 2 * P]
                    shift, scale = mod[:, l, k, s:s + 1], mod[:, l, KC + k, s:s + 1]
                    if eng is nc.scalar:
                        eng.activation(dst, src, ACT.Identity, bias=shift, scale=scale).then_inc(s_heA[l], 1)
                    else:
                        eng.tensor_scalar(dst, src, scale, shift, ALU.mult, ALU.add).then_inc(s_heD[l], 1)
                split_inputs(eng, l, s, half)

        qkv_copy, qk_index = [], []
        for l in range(LAYERS):
            n_act = n_dve = n_qk = 0
            copies, index = [], []
            for g, t in qkv_jobs[l]:
                if l == 0 and g < 4 and t >= CTX_TILES:
                    n_dve += 1
                    copies.append(("dve", s_qeD[l], n_dve))
                else:
                    n_act += 1
                    copies.append(("act", s_qeA[l], n_act))
                index.append(n_qk if g < 4 else None)
                n_qk += g < 4
            qkv_copy.append(copies)
            qk_index.append(index)
        N_QK = [sum(i is not None for i in qk_index[l]) for l in range(LAYERS)]

        units = [[(t, h) for t in TILES_OF[0] for h in range(DIFF_HEADS)],
                 [(t, h) for t in TILES_OF[1] for h in range(NA_HEADS)]]

        def mod_banks(a):
            return (6, 7) if a < ADA_ATT else (6, 6)

        def mod_part(a):
            return bias[:].rearrange("p h r c -> p (h r c)")[:, KC * TILES * P:KC * TILES * P + STRIP]

        def key_tiles(t):
            return CTX_TILES if t < CTX_TILES else TILES

        NT = [len(t) for t in TILES_OF]
        HALF = D // 2
        VECTOR_LOADS = 7
        LATE_LOADS = 6
        block = stack.enter_context(nc.Block())

        @block.sync
        def _(sp):
            def small(dst, src):
                sp.dma_start(dst, src).then_inc(s_small, 16)

            small(cst[:], consts)
            small(vec_rows[8:16, :], c.rearrange("a (r p) -> (a r) p", p=P))
            small(vec_rows[0:8, :], c_ctx.rearrange("(r p) -> r p", p=P))
            small(vec_rows[16:32, :], norm1_g.rearrange("l (r p) -> (l r) p", p=P))
            small(vec_rows[32:48, :], norm2_g.rearrange("l (r p) -> (l r) p", p=P))
            small(vec_rows[48:49, :], diff_subln_g)
            small(adab_rows[0:96, :], ada_b.rearrange("l (r p) -> (l r) p", p=P))

            def load_strip(l, j):
                src, g, _, _, slot = strips[l][j]
                last = before_in_slot(l, slot, j)
                if last is not None:
                    _, _, used, value, _ = strips[l][last]
                    sp.wait_ge(used, value)
                sp.dma_start(strip(l, j), src.rearrange("(k p) n -> p k n", p=P)[:, :, g * STRIP:(g + 1) * STRIP]) \
                    .then_inc(s_ld[l][slot], 16)

            for j in range(2):
                load_strip(0, j)
            sp.dma_start(resid[:, 0:CTX_TILES], ctx.rearrange("a (t p) d -> p (a t) d", p=P)).then_inc(s_x, 16)
            sp.dma_start(resid[:, CTX_TILES:TILES], x.rearrange("a (t p) d -> p (a t) d", p=P)).then_inc(s_x, 16)
            load_strip(0, 2)
            for i, v in enumerate((diff_lambda_q1, diff_lambda_k1, diff_lambda_q2, diff_lambda_k2)):
                sp.dma_start(lam_in[:, i, :], v.broadcast_to([P, HD])).then_inc(s_late, 16)
            sp.dma_start(rbias[:], router_bias.partition_broadcast(P)).then_inc(s_late, 16)
            sp.dma_start(rw[:], router_w.rearrange("(k p) e -> p k e", p=P)).then_inc(s_late, 16)

            def load_rows(l, targets):
                for dst, piece, s in targets:
                    src = bass.AP(mod_dram[l], (piece * KC * 2 + s) * P, [[0, P], [2 * P, KC], [1, P]])
                    sp.dma_start(dst.rearrange("p (k n) -> p k n", n=P), src).then_inc(s_rows, 16)

            first_rows = at[0]["ada", ADA_ATT + 1] + 1
            for j in range(3, first_rows):
                load_strip(0, j)
            sp.wait_ge(s_modR, 1)
            sp.dma_start(mod_dram[0].ap(), mod_rows[:]).then_inc(s_modD, 16)
            sp.wait_ge(s_modD, 16)
            sp.wait_ge(s_qm[0], len(qkv_jobs[0]))
            load_rows(0, [(rows[:, 2 * i + s], piece, s) for i, piece in enumerate((2, 3, 4)) for s in range(2)])
            for j in range(first_rows, len(strips[0])):
                load_strip(0, j)

            def store_h(l, tiles):
                for n in tiles:
                    sp.wait_ge(s_h[l], n + 1)
                    sp.dma_start(h_dram[l][n * P:(n + 1) * P, :], tokm[:, TILES_OF[l][n]]).then_inc(s_hst[l], 16)

            def expert_weights(l, w, e, which):
                w_dram = (moe_w_gate, moe_w_up, moe_w_down)[w][l].rearrange("e (k p) n -> e p k n", p=P)
                sp.dma_start(expert_strip(l, w, which), w_dram[bass.ds(e, 1)].rearrange("a p k n -> p (a k) n")) \
                    .then_inc(m_wl[l][w], 16)

            def first_expert(l, ws):
                for w in ws:
                    _, _, used, value, _ = strips[l][before_in_slot(l, expert_slot(l, w), len(strips[l]))]
                    sp.wait_ge(used, value)
                    expert_weights(l, w, 0, 1)

            def load_experts(l):
                free = {0: [(s_we, 2 * NT[l])], 2: [(s_hst, 16 * NT[l]), (s_h2t, 2 * NT[l])], 1: [(s_lg, NT[l])]}
                for slot, waits in free.items():
                    w = [expert_slot(l, w) for w in range(3)].index(slot)
                    for used, value in waits:
                        sp.wait_ge(used[l], value)
                    sp.wait_ge(m_wl[l][w], 16)
                    expert_weights(l, w, 1, 0)
                for w in range(3):
                    sp.wait_ge(m_wl[l][w], 16)
                sp.wait_ge(m_wl[l][0], 32)
                sp.wait_ge(s_idx[l], 1)
                with sp.Fori(0, (N_EXP - 2) // 2) as i:
                    for which in (1, 0):
                        e = 2 * i + (3 - which)
                        blocks = sp.value_load(plan[0:1, bass.ds(e - 1, 1)], min_val=0, max_val=MAX_BLOCKS)
                        for w, used in enumerate((m_gt, m_up, m_dn)):
                            sp.wait_ge(m_wl[l][(w + 1) % 3], e * 16 + 16 * (w == 2))
                            sp.sem_inc(s_turn_sp, 1)
                            sp.wait_ge(used[l], blocks + 1)
                            expert_weights(l, w, e, which)
                for w in range(3):
                    sp.wait_ge(m_wl[l][w], 16 * N_EXP)
                return (sp.value_load(plan[0:1, N_EXP - 1:N_EXP], min_val=0, max_val=MAX_BLOCKS),
                        sp.value_load(plan[0:1, N_EXP:], min_val=1, max_val=MAX_BLOCKS))

            def load_expert_rows(l, n):
                sp.wait_ge(m_sc[l], n * 16 + 32)
                for m, t in enumerate(TILES_OF[l]):
                    if m >= 2:
                        sp.wait_ge(s_cb[l], m - 1)
                    for k in range(2):
                        src = y_dram[l][k * TILES * P + m * P:k * TILES * P + (m + 1) * P, :]
                        sp.dma_start(val[:, 2 * (m % 2) + k], src).then_inc(s_yl[l][m % 2], 16)

            sp.wait_ge(s_modR, 2)
            sp.dma_start(mod_dram[1].ap(), mod_rows[:]).then_inc(s_modD, 16)
            sp.wait_ge(s_sc[0], len(units[0]))
            load_rows(0, [(last_gate0[s], 5, s) for s in range(2)])
            first_expert(0, (0,))
            store_h(0, range(NT[0] - 1))
            first_expert(0, (1, 2))
            store_h(0, range(NT[0] - 1, NT[0]))
            sp.wait_ge(s_modD, 32)
            ring_blocks, n0 = load_experts(0)
            for j, used in enumerate((m_gt, m_up, m_dn)):
                sp.wait_ge(used[0], ring_blocks + 1)
                load_strip(1, j)
            load_expert_rows(0, n0)
            sp.wait_ge(s_cb[0], NT[0])
            for par in range(2):
                for h in range(NA_HEADS):
                    src = bass.AP(na_rpb.tensor, h * RPB_H * RPB_W + (NA_WR - 1 - 2 - par) * RPB_W + NA_WC - GRID_W,
                                  [[1, GRID_W], [RPB_W, 6], [1, GRID_W]])
                    sp.dma_start(bias[par * GRID_W:(par + 1) * GRID_W, h], src).then_inc(s_bias, 16)
            for j in range(3, len(strips[1])):
                load_strip(1, j)
            sp.wait_ge(s_qm[1], len(qkv_jobs[1]))
            load_rows(1, [(rows[:, i], piece, 1) for i, piece in enumerate((2, 3, 4, 5))])
            sp.dma_start(rows[:, 4], final_norm_g.partition_broadcast(P)).then_inc(s_fg, 16)
            first_expert(1, (0,))
            store_h(1, range(NT[1] - 1))
            first_expert(1, (1, 2))
            store_h(1, range(NT[1] - 1, NT[1]))
            _, n1 = load_experts(1)
            load_expert_rows(1, n1)
            for m, t in enumerate(TILES_OF[1]):
                sp.wait_ge(s_fin, m + 1)
                sp.dma_start(out[0, m * P:(m + 1) * P, :], tokm[:, t]).then_inc(s_out, 16)
            sp.wait_ge(s_out, 16 * NT[1])

        @block.gpsimd
        def _(pool):
            def in_turn():
                pool.sem_inc(s_turn, 1)

            fills = [0]

            def fill(dst, value):
                fills[0] += 1
                pool.memset(dst, value).then_inc(s_set, 1)
                pool.wait_ge(s_set, fills[0])

            fill(cond[:], 0.0)
            fill(qT[HD:P], 0.0)
            fill(q_odd0[0:HD], 0.0)

            for l in range(LAYERS):
                pool.wait_ge(s_wm[l], 2 * NT[l])
                fill(ones, 1.0)
                h_rows = h_dram[l][0:NT[l] * P].rearrange("n (g f) -> (n g) f", g=GROUPS)
                made = y_dram[l].rearrange("n (g f) -> (n g) f", g=GROUPS)
                pool.memset(blk_in, 0.0).then_inc(m_ix[l], 1)
                pool.wait_ge(m_ix[l], 1)
                pool.wait_ge(s_idx[l], 1)
                n = pool.value_load(plan[0:1, N_EXP:], min_val=1, max_val=MAX_BLOCKS)
                last_row, last_made = pool.to_reg(GROUPS * NT[l] * P - 1), pool.to_reg(GROUPS * 2 * TILES * P - 1)
                pool.tensor_copy(gather_idx[:], slot_idx[:, 0:1]).then_inc(m_ix[l], 1)
                pool.wait_ge(m_ix[l], 2)
                pool.wait_ge(s_hst[l], 16 * NT[l])
                pool.indirect_dma_start(blk_in, None, h_rows, bass.IndirectOffsetOnAxis(ap=gather_idx[:], axis=0),
                                        bounds_check=last_row, oob_is_err=False).then_inc(m_ga[l], 16)
                pool.memset(blk_out, 0.0).then_inc(m_ix[l], 1)
                pool.wait_ge(m_ix[l], 3)

                pool.tensor_copy(scatter_idx[:], slot_idx[:, BLK_COLS:BLK_COLS + 1]).then_inc(m_ix[l], 1)
                pool.wait_ge(m_ix[l], 4)
                pool.indirect_dma_start(made, bass.IndirectOffsetOnAxis(ap=scatter_idx[:], axis=0), blk_out, None,
                                        bounds_check=last_made, oob_is_err=False).then_inc(m_sc[l], 16)
                with pool.Fori(0, n) as i:
                    pool.wait_ge(m_ga[l], i * 16 + 16)
                    pool.wait_ge(m_xt[l], i + 1)
                    in_turn()
                    pool.tensor_copy(gather_idx[:], slot_idx[:, bass.ds(i + 1, 1)]).then_inc(m_ix[l], 1)
                    pool.wait_ge(m_ix[l], i * 2 + 5)
                    in_turn()
                    pool.indirect_dma_start(blk_in, None, h_rows, bass.IndirectOffsetOnAxis(ap=gather_idx[:], axis=0),
                                            bounds_check=last_row, oob_is_err=False).then_inc(m_ga[l], 16)
                    pool.wait_ge(m_sc[l], i * 16 + 16)
                    in_turn()
                    pool.tensor_copy(scatter_idx[:], slot_idx[:, bass.ds(i + BLK_COLS, 1)]).then_inc(m_ix[l], 1)
                    pool.wait_ge(m_ix[l], i * 2 + 6)
                    pool.wait_ge(m_y[l], i + 1)
                    in_turn()
                    pool.indirect_dma_start(made, bass.IndirectOffsetOnAxis(ap=scatter_idx[:], axis=0), blk_out, None,
                                            bounds_check=last_made, oob_is_err=False).then_inc(m_sc[l], 16)
                pool.wait_ge(m_sc[l], n * 16 + 16)
                in_turn()
                pool.tensor_copy(scatter_idx[:], slot_idx[:, bass.ds(n + BLK_COLS, 1)]).then_inc(m_ix[l], 1)
                pool.wait_ge(m_ix[l], n * 2 + 5)
                pool.wait_ge(m_y[l], n + 1)
                in_turn()
                pool.indirect_dma_start(made, bass.IndirectOffsetOnAxis(ap=scatter_idx[:], axis=0), blk_out, None,
                                        bounds_check=last_made, oob_is_err=False).then_inc(m_sc[l], 16)
                if l == 0:
                    pool.wait_ge(m_dn[0], n + 1)
                    pool.wait_ge(m_xt[0], n + 1)
                    pool.wait_ge(m_xc[0], n + 1)
                    pool.wait_ge(m_ga[0], n * 16 + 16)
                    in_turn()
                    fill(qT[0:HD, :, 0:CTX], 0.0)
                    fill(qT[HD:P, :, CTX:], 0.0)
                    pool.wait_ge(s_small, 16 * VECTOR_LOADS)
                    pool.wait_ge(s_bias, 16 * 2 * NA_HEADS)
                    table = bias[:].rearrange("p h r c -> p (h r) c")
                    valid = const("valid").unsqueeze(1).to_broadcast([P, NA_HEADS * 6, GRID_W])
                    invalid = const("invalid").unsqueeze(1).to_broadcast([P, NA_HEADS * 6, GRID_W])
                    pool.tensor_tensor(table, table, valid, ALU.mult).then_inc(s_bias_done, 1)
                    pool.wait_ge(s_bias_done, 1)
                    pool.tensor_tensor(table, table, invalid, ALU.add).then_inc(s_bias_done, 1)

        @block.scalar
        def _(act):
            def square_rows(t, src, dst):
                act.activation(dst, src, ACT.Square, accum_out=stat[:, 0, t:t + 1]).then_inc(s_sq, 1)

            act.wait_ge(s_vec, 1)
            act.wait_ge(s_set, 1)
            for s in range(2):
                act.activation(cond[:, :, s], vec[:, 8 * s:8 * s + 8], ACT.Silu).then_inc(s_cond, 1)
            def copy_mod(a):
                act.wait_ge(s_ada, a + 1)
                if a >= 1:
                    act.wait_ge(s_adt, a)
                act.copy(mod_part(a), ps[:, mod_banks(a)[0]]).then_inc(s_adc, 1)

            def norm1(l, t):
                square_rows(t, resid[:, t], tokm[:, t])
                act.wait_ge(s_ms, norm_step(f"1 of {l}") + t)
                act.activation(stat[:, 2, t:t + 1], stat[:, 1, t:t + 1], ACT.Sqrt).then_inc(s_rt, 1)

            def weigh_first(l, m):
                act.wait_ge(s_yl[l][m % 2], 32 * (m // 2 + 1))
                y1 = val[:, 2 * (m % 2)]
                act.activation(y1, y1, ACT.Copy, scale=wts[:, 0, m:m + 1]).then_inc(s_w1[l], 1)

            for a in range(ADA_QKV // 2):
                copy_mod(a)
            act.wait_ge(s_x, 32)
            for t in range(TILES):
                norm1(0, t)
            for a in range(ADA_QKV // 2, ADA_QKV):
                copy_mod(a)

            for l in range(LAYERS):
                if l == 0:
                    split_weights(act, 0, 0, 0)
                act.wait_ge(s_mod, (1, 3)[l])
                stream_in(act, l, 0)
                if l == 0:
                    split_weights(act, 0, 0, 1)
                    stream_in(act, 0, 1)
                    act.wait_ge(s_lam, 1)
                    act.activation(lam[:, 2:4], lam[:, 0:2], ACT.Exp).then_inc(s_lam_exp, 1)
                else:
                    for m in range(CTX_TILES, TILES):
                        weigh_first(0, m)
                    for t in range(CTX_TILES, TILES):
                        act.wait_ge(s_cb[0], t + 1)
                        norm1(1, t)

                def copy_turned(m, g, t):
                    act.wait_ge(s_qt[l], m + 1)
                    src = ps[:, 4 + m % 2].rearrange("p (k t) -> p k t", t=P)
                    kk = slice(4 * (g % 2), 4 * (g % 2) + 4)
                    if g >= 2:
                        act.copy(kT[:, kk, t * P:(t + 1) * P], src).then_inc(s_qc[l], 1)
                        return
                    if l == 1 and m == N_QK[1] - 4:
                        act.wait_ge(s_set, 6)
                    act.copy(qT[0:HD, kk, t * P:(t + 1) * P], src[0:HD])
                    odd, t0 = (q_odd0, t) if l == 0 else (qT, t - CTX_TILES)
                    act.copy(odd[HD:P, kk, t0 * P:(t0 + 1) * P], src[HD:P]).then_inc(s_qc[l], 1)

                last = None
                for n, (g, t) in enumerate(qkv_jobs[l]):
                    pos, job, is_last = qkv_pos[l][n]
                    if l == 1 and n == CTX_TILES:
                        stream_in(act, 1, 1)
                    if pos < 5 and job == (2 if pos == 0 else 1):
                        split_weights(act, l, pos + 1, 0)
                    if pos < 5 and is_last:
                        split_weights(act, l, pos + 1, 1)
                    if qkv_copy[l][n][0] == "act":
                        m = qk_index[l][n]
                        act.wait_ge(s_qm[l], n + 1)
                        if m is None:
                            dst = val[:, t, (g - 4) * STRIP:(g - 3) * STRIP]
                        else:
                            if m >= 2:
                                act.wait_ge(s_qt[l], m - 1)
                            dst = tokm[:, 0, (m % 2) * STRIP:(m % 2 + 1) * STRIP]
                        act.activation(dst, ps[:, n % 2], ACT.Copy,
                                       scale=SCALE if g < 2 else 1.0).then_inc(s_qeA[l], 1)
                    if last is not None:
                        copy_turned(*last)
                    last = (qk_index[l][n], g, t) if g < 4 else None
                    if l == 0 and n % 2 == 0:
                        copy_mod(ADA_QKV + n // 2)
                if last is not None:
                    copy_turned(*last)

                if l == 0:
                    def exps(u):
                        t, h = units[0][u]
                        nk = key_tiles(t) * P
                        act.wait_ge(s_nm[0], u + 1)
                        if u >= 3:
                            act.wait_ge(s_pt[0], u - 2)
                        for cc in range(2):
                            act.activation(hT[:, 2 * (u % 3) + cc, 0:nk], ps[:, 2 * (u % 2) + cc, 0:nk], ACT.Exp,
                                           bias=att[:, u % 3, cc:cc + 1],
                                           accum_out=att[:, u % 3, 4 + cc:5 + cc]).then_inc(s_ex[0], 1)

                    def copy_probs(u):
                        t, h = units[0][u]
                        nk = key_tiles(t) * P
                        act.wait_ge(s_pt[0], u + 1)
                        if u >= 2:
                            act.wait_ge(s_pv[0], u - 1)
                        act.copy(hT[:, 6 + u % 2, 0:nk], ps[:, (4, 7)[u % 2], 0:nk]).then_inc(s_pc[0], 1)

                    def copy_out(u):
                        t, h = units[0][u]
                        act.wait_ge(s_pv[0], u + 1)
                        act.activation(ps[:, 5, 2 * HD:4 * HD], ps[:, 5, 0:2 * HD], ACT.Square,
                                       accum_out=stat[:, 0, 8 * t + h:8 * t + h + 1]).then_inc(s_hs, 1)
                        act.copy(tokm[:, t, h * 2 * HD:(h + 1) * 2 * HD], ps[:, 5, 0:2 * HD]).then_inc(s_oe[0], 1)

                    U = len(units[0])
                    for u in range(U + 3):
                        if u < U:
                            exps(u)
                        if u % ATT_STEP == 0 and u // ATT_STEP < 2 * ADA - ADA_ATT:
                            copy_mod(ADA_ATT + u // ATT_STEP)
                        if 2 <= u < U + 2:
                            copy_probs(u - 2)
                        if u >= 3:
                            copy_out(u - 3)
                    act.wait_ge(s_ms, norm_step("sub"))
                    act.activation(stat[:, 2], stat[:, 1], ACT.Sqrt).then_inc(s_rt, 1)
                else:
                    def copy_probs1(u):
                        act.wait_ge(s_pt[1], u + 1)
                        if u >= 2:
                            act.wait_ge(s_pv[1], u - 1)
                        act.copy(hT[:, 4 + u % 2], ps[:, (4, 7)[u % 2]]).then_inc(s_pc[1], 1)

                    U = len(units[1])
                    for u, (t, h) in enumerate(units[1]):
                        act.wait_ge(s_nm[1], u + 1)
                        if u >= 4:
                            act.wait_ge(s_pt[1], u - 3)
                        act.activation(hT[:, u % 4], ps[:, u % 4], ACT.Exp, bias=att[:, u % 4, 0:1],
                                       accum_out=att[:, u % 4, 2:3]).then_inc(s_ex[1], 1)
                        if u >= 2:
                            copy_probs1(u - 2)
                    copy_probs1(U - 2)
                    copy_probs1(U - 1)

                def turned_out(m):
                    t = TILES_OF[l][m]
                    if l == 0 and m == 0:
                        act.wait_ge(s_lam, 3)
                    for hf in range(2):
                        act.wait_ge(s_ot[l], 2 * m + hf + 1)
                        dst = hT[:, 4 * hf:4 * hf + 4, t * P:(t + 1) * P]
                        src = ps[:, 4 + hf].rearrange("p (k t) -> p k t", t=P)
                        if l == 0:
                            act.activation(dst, src, ACT.Copy, scale=subln[:, 0:1]).then_inc(s_oc[l], 1)
                        else:
                            act.copy(dst, src).then_inc(s_oc[l], 1)

                def norm2(m):
                    t = TILES_OF[l][m]
                    act.wait_ge(s_we[l], 2 * m + 2)
                    act.wait_ge(s_ot[l], 2 * m + 2)
                    square_rows(t, resid[:, t], tokm[:, t])
                    act.wait_ge(s_ms, norm_step(f"2 of {l}") + m)
                    act.activation(stat[:, 2, t:t + 1], stat[:, 1, t:t + 1], ACT.Sqrt).then_inc(s_rt, 1)

                def turned_h(m):
                    t = TILES_OF[l][m]
                    act.wait_ge(s_h2t[l], 2 * m + 1)
                    act.copy(hT[:, 0:4, t * P:(t + 1) * P],
                             ps[:, 2].rearrange("p (k t) -> p k t", t=P)).then_inc(s_h2A[l], 1)

                split_wo(act, l, 0)
                turned_out(0)
                split_out(act, l, 0)
                split_wo(act, l, 1)
                for m in range(NT[l]):
                    if m + 1 < NT[l]:
                        turned_out(m + 1)
                        split_out(act, l, m + 1)
                    if m >= 1:
                        norm2(m - 1)
                        turned_h(m - 1)
                norm2(NT[l] - 1)
                turned_h(NT[l] - 1)

                act.wait_ge(s_lg[l], NT[l])
                act.activation(rt[:, 0, 0:NT[l] * N_EXP], ps[:, 6, 0:NT[l] * N_EXP], ACT.Exp, scale=-1.0).then_inc(s_le[l], 1)

                act.wait_ge(s_idx[l], 1)
                n = act.value_load(plan[0:1, N_EXP:], min_val=1, max_val=MAX_BLOCKS)

                def block_inT():
                    act.copy(blk_inT, ps[:, 2].rearrange("p (k t) -> p k t", t=P)).then_inc(m_xc[l], 1)

                act.wait_ge(m_xt[l], 1)
                block_inT()
                with act.Fori(0, n) as i:
                    act.wait_ge(m_gt[l], i + 2)
                    act.wait_ge(m_ac[l], i + 1)
                    act.activation(blk_silu, ps[:, 0, 0:FG], ACT.Silu).then_inc(m_si[l], 1)
                    act.wait_ge(m_xt[l], i + 2)
                    block_inT()

                if l == 0:
                    for half in range(2):
                        split_weights(act, 1, 0, half)
                for m in range(2):
                    weigh_first(l, m)
                if l == 0:
                    for t in range(CTX_TILES):
                        act.wait_ge(s_cb[0], t + 1)
                        norm1(1, t)

            for m, t in enumerate(TILES_OF[1]):
                act.wait_ge(s_cb[1], m + 1)
                act.activation(tokm[:, t], resid[:, t], ACT.Square, accum_out=stat[:, 0, t:t + 1]).then_inc(s_sq, 1)
            act.wait_ge(s_fms, 1)
            act.activation(stat[:, 2, 0:TILES], stat[:, 1, 0:TILES], ACT.Sqrt).then_inc(s_frt, 1)

        @block.vector
        def _(dve):
            steps = [0]

            def step(ins):
                steps[0] += 1
                ins.then_inc(s_v, 1)
                dve.wait_ge(s_v, steps[0])

            def sync(ins, s, counts={}):
                counts[s.name] = counts.get(s.name, 0) + 1
                ins.then_inc(s, 1)
                dve.wait_ge(s, counts[s.name])

            tt, ts, stt = dve.tensor_tensor, dve.tensor_scalar, dve.scalar_tensor_tensor

            step(dve.memset(plan[:, 0:1], 0))
            dve.wait_ge(s_vec_t, 2)
            sync(dve.tensor_copy(vec[:], ps[:, 7, 0:N_VEC]), s_vec)
            step(dve.tensor_copy(adab[:], ps[:, 7, P:P + 96]))
            def mean_square(dst, src, n):
                return ts(dst, src, 1.0 / n, EPS, ALU.mult, ALU.add)

            def sum_mod(a):
                dve.wait_ge(s_adt, a + 1)
                part = ps[:, mod_banks(a)[1]].rearrange("p (c q s) -> p c s q", q=4, s=32)[:, :, 0:2, :]
                j = a % ADA
                sync(dve.tensor_reduce(mod[:, a // ADA, 4 * j:4 * j + 4], part, X_AXIS, ALU.add), s_adr)

            def modulation(l, first, last):
                cols = slice(first * KC, last * KC)
                b = adab[:, 48 * l + first * KC:48 * l + last * KC].unsqueeze(2).to_broadcast([P, (last - first) * KC, 2])
                step(tt(mod[:, l, cols], mod[:, l, cols], b, ALU.add))
                for piece, gain in ((1, 16), (4, 32)):
                    if first <= piece < last:
                        g = vec[:, gain + 8 * l:gain + 8 * l + 8].unsqueeze(2).to_broadcast([P, KC, 2])
                        m = mod[:, l, piece * KC:(piece + 1) * KC]
                        step(stt(m, m, 1.0, g, ALU.add, ALU.mult))
                dve.sem_inc(s_mod, 1)

            def modulation_rows(l):
                dve.wait_ge(s_modT, l + 1)
                if l == 1:
                    dve.wait_ge(s_modD, 16)
                dve.tensor_copy(mod_rows[:], ps[0:96, 6, 0:P]).then_inc(s_modR, 1)

            def norm1(l, t):
                dve.wait_ge(s_sq, squares(f"1 of {l}") + t)
                sync(mean_square(stat[:, 1, t:t + 1], stat[:, 0, t:t + 1], D), s_ms)
                dve.wait_ge(s_rt, norm_step(f"1 of {l}") + t)
                step(dve.reciprocal(stat[:, 3, t:t + 1], stat[:, 2, t:t + 1]))
                ts(tokm[:, t], resid[:, t], stat[:, 3, t:t + 1], None, ALU.mult).then_inc(s_xn[l], 1)

            def row(l, piece, t):
                s = int(t >= CTX_TILES)
                if l == 0 and piece == 3:
                    return last_gate0[s]
                return rows[:, 2 * piece + s if l == 0 else piece]

            def add_experts(l, m):
                t = TILES_OF[l][m]
                dve.wait_ge(s_w1[l], m + 1)
                y1, y2 = val[:, 2 * (m % 2)], val[:, 2 * (m % 2) + 1]
                step(stt(y1, y2, wts[:, 1, m:m + 1], y1, ALU.mult, ALU.add))
                step(tt(y1, y1, row(l, 3, t), ALU.mult))
                sync(tt(resid[:, t], resid[:, t], y1, ALU.add), s_cb[l])

            for l in range(LAYERS):
                if l == 0:
                    for a in range(ADA_QKV // 2):
                        sum_mod(a)
                    for t in range(TILES):
                        norm1(0, t)
                    for a in range(ADA_QKV // 2, ADA_QKV):
                        sum_mod(a)
                    modulation(0, 0, 2)
                stream_in(dve, l, 0)
                if l == 0:
                    for half in range(2):
                        split_weights(dve, l, 0, half)
                    stream_in(dve, 0, 1)
                    dve.wait_ge(s_late, 16 * LATE_LOADS)
                    step(tt(val[:, 0, 0:2 * HD].rearrange("p (a b) -> p a b", b=HD), lam_in[:, 0::2, :], lam_in[:, 1::2, :], ALU.mult))
                    sync(dve.tensor_reduce(lam[:, 0:2], val[:, 0, 0:2 * HD].rearrange("p (a b) -> p a b", b=HD), X_AXIS, ALU.add), s_lam)
                    dve.wait_ge(s_lam_exp, 1)
                    step(tt(lam[:, 4:5], lam[:, 3:4], lam[:, 2:3], ALU.subtract))
                    sync(ts(lam[:, 5:6], lam[:, 4:5], -LAMBDA_INIT, None, ALU.add), s_lam)
                    sync(ts(subln[:], vec[:, 48:49], 1.0 - LAMBDA_INIT, None, ALU.mult), s_lam)
                else:
                    for t in range(CTX_TILES, TILES):
                        add_experts(0, t)
                    for t in range(CTX_TILES, TILES):
                        norm1(1, t)

                for n, (g, t) in enumerate(qkv_jobs[l]):
                    if l == 0 and n % 2 == 0 and n > 0:
                        a = ADA_QKV + n // 2 - 1
                        sum_mod(a)
                        if a == ADA - 1:
                            modulation(0, 2, 6)
                            modulation_rows(0)
                    if l == 1 and n == CTX_TILES:
                        stream_in(dve, 1, 1)
                    pos, job, is_last = qkv_pos[l][n]
                    if pos < 5 and job == (2 if pos == 0 else 1):
                        split_weights(dve, l, pos + 1, 0)
                    if pos < 5 and is_last:
                        split_weights(dve, l, pos + 1, 1)
                    if qkv_copy[l][n][0] != "dve":
                        continue
                    m = qk_index[l][n]
                    dve.wait_ge(s_qm[l], n + 1)
                    lo = CONST_AT["cos"][0] + 32 * (t - CTX_TILES)
                    cos = cst[:, lo:lo + 32].unsqueeze(1).to_broadcast([P, 16, 32])
                    lo = CONST_AT["sin"][0] + 32 * (t - CTX_TILES)
                    sin = cst[:, lo:lo + 32].unsqueeze(1).to_broadcast([P, 16, 32])
                    src = ps[:, n % 2].rearrange("p (a b) -> p a b", b=32)
                    by_cos = tokm[:, 1, 0:STRIP].rearrange("p (a b) -> p a b", b=32)
                    by_sin = tokm[:, 1, STRIP:2 * STRIP].rearrange("p (a b) -> p a b", b=32)
                    scale = SCALE if g < 2 else 1.0
                    step(stt(by_cos, src, scale, cos, ALU.mult, ALU.mult))
                    step(stt(by_sin, src, scale, sin, ALU.mult, ALU.mult))
                    if m >= 2:
                        dve.wait_ge(s_qt[l], m - 1)
                    dst = tokm[:, 0, (m % 2) * STRIP:(m % 2 + 1) * STRIP].rearrange("p (a b) -> p a b", b=32)
                    step(tt(dst[:, 0::2], by_cos[:, 0::2], by_sin[:, 1::2], ALU.subtract))
                    sync(tt(dst[:, 1::2], by_cos[:, 1::2], by_sin[:, 0::2], ALU.add), s_qeD[l])

                if l == 0:
                    sum_mod(ADA_ATT - 1)

                    def maxima(u):
                        t, h = units[0][u]
                        nk = key_tiles(t) * P
                        dve.wait_ge(s_sc[0], u + 1)
                        if u >= 3:
                            dve.wait_ge(s_ex[0], 2 * (u - 2))
                        dve.tensor_reduce(att[:, u % 3, 0:2], ps[:, 2 * (u % 2):2 * (u % 2) + 2, 0:nk], X_AXIS, ALU.max,
                                          negate=True).then_inc(s_nm[0], 1)

                    def probs(u):
                        t, h = units[0][u]
                        nk = key_tiles(t) * P
                        a = att[:, u % 3]
                        dve.wait_ge(s_ex[0], 2 * u + 2)
                        step(dve.reciprocal(a[:, 6:8], a[:, 4:6]))
                        p0, p1 = hT[:, 2 * (u % 3), 0:nk], hT[:, 2 * (u % 3) + 1, 0:nk]
                        step(ts(p1, p1, a[:, 7:8], lam[:, 5:6], ALU.mult, ALU.mult))
                        stt(p0, p0, a[:, 6:7], p1, ALU.mult, ALU.add).then_inc(s_pr, 1)

                    U = len(units[0])
                    for u in range(U + 1):
                        if u < U:
                            maxima(u)
                        if u % ATT_STEP == 1 and u // ATT_STEP < 2 * ADA - ADA_ATT:
                            a = ADA_ATT + u // ATT_STEP
                            sum_mod(a)
                            if a == 2 * ADA - 1:
                                modulation(1, 0, 6)
                                modulation_rows(1)
                        if u >= 1:
                            probs(u - 1)
                    dve.wait_ge(s_hs, U)
                    dve.wait_ge(s_oe[0], U)
                    sync(mean_square(stat[:, 1], stat[:, 0], 2 * HD), s_ms)
                    dve.wait_ge(s_rt, norm_step("sub"))
                    step(dve.reciprocal(stat[:, 3], stat[:, 2]))

                    def normalise_heads(m):
                        o = tokm[:, m].rearrange("p (h d) -> p h d", d=2 * HD)
                        r = stat[:, 3, 8 * m:8 * m + 8].unsqueeze(2).to_broadcast([P, DIFF_HEADS, 2 * HD])
                        tt(o, o, r, ALU.mult).then_inc(s_on, 1)

                    normalise_heads(0)
                else:
                    dve.wait_ge(s_bias_done, 2)

                    def scale_out(u):
                        t, h = units[1][u]
                        step(dve.reciprocal(att[:, u % 4, 3:4], att[:, u % 4, 2:3]))
                        dve.wait_ge(s_pv[1], u + 1)
                        ts(tokm[:, t, h * HD:(h + 1) * HD], ps[:, 5 + u % 2, 0:HD], att[:, u % 4, 3:4], None,
                           ALU.mult).then_inc(s_oe[1], 1)

                    for u, (t, h) in enumerate(units[1]):
                        a = att[:, u % 4]
                        lo = 2 - 2 * (t - CTX_TILES)
                        dve.wait_ge(s_sc[1], u + 1)
                        loc = ps[:, u % 4, CTX:CTX + SEQ]
                        step(tt(loc, loc, bias[:, h, lo:lo + GRID_H].rearrange("p r c -> p (r c)"), ALU.add))
                        dve.tensor_reduce(a[:, 0:1], ps[:, u % 4], X_AXIS, ALU.max, negate=True).then_inc(s_nm[1], 1)
                        if u >= 3:
                            scale_out(u - 3)
                    for u in range(len(units[1]) - 3, len(units[1])):
                        scale_out(u)

                split_wo(dve, l, 0)
                split_out(dve, l, 0)
                if l == 0:
                    normalise_heads(1)
                split_wo(dve, l, 1)
                if l == 0:
                    for m in range(2, TILES):
                        normalise_heads(m)

                if l == 0:
                    dve.wait_ge(s_rows, 16 * 8)
                else:
                    dve.wait_ge(s_rows, 16 * (8 + 4))

                def add_out(m, hf):
                    t = TILES_OF[l][m]
                    j = 2 * m + hf
                    cols = slice(hf * HALF, (hf + 1) * HALF)
                    dve.wait_ge(s_wm[l], j + 1)
                    step(tt(val[:, 0, cols], ps[:, j % 2], row(l, 0, t)[:, cols], ALU.mult))
                    sync(tt(resid[:, t, cols], resid[:, t, cols], val[:, 0, cols], ALU.add), s_we[l])

                def norm2(m):
                    t = TILES_OF[l][m]
                    dve.wait_ge(s_sq, squares(f"2 of {l}") + m)
                    sync(mean_square(stat[:, 1, t:t + 1], stat[:, 0, t:t + 1], D), s_ms)
                    dve.wait_ge(s_rt, norm_step(f"2 of {l}") + m)
                    step(dve.reciprocal(stat[:, 3, t:t + 1], stat[:, 2, t:t + 1]))
                    step(stt(tokm[:, t], resid[:, t], stat[:, 3, t:t + 1], row(l, 2, t), ALU.mult, ALU.mult))
                    sync(tt(tokm[:, t], tokm[:, t], row(l, 1, t), ALU.add), s_h[l])

                def turned_h(m):
                    t = TILES_OF[l][m]
                    dve.wait_ge(s_h2t[l], 2 * m + 2)
                    dve.tensor_copy(hT[:, 4:8, t * P:(t + 1) * P],
                                    ps[:, 3].rearrange("p (k t) -> p k t", t=P)).then_inc(s_h2D[l], 1)

                for m in range(NT[l]):
                    if m + 1 < NT[l]:
                        split_out(dve, l, m + 1)
                    add_out(m, 0)
                    add_out(m, 1)
                    norm2(m)
                    turned_h(m)

                nt = NT[l]
                w = nt * N_EXP

                def r3(i, a=nt, b=N_EXP, off=0):
                    return rt[:, i, off:off + a * b].rearrange("p (a b) -> p a b", b=b)

                dve.wait_ge(s_le[l], 1)
                step(ts(rt[:, 0, 0:w], rt[:, 0, 0:w], 1.0, None, ALU.add))
                step(dve.reciprocal(rt[:, 1, 0:w], rt[:, 0, 0:w]))
                rb = rbias[:].unsqueeze(1).to_broadcast([P, nt, N_EXP])
                step(tt(r3(2), r3(1), rb, ALU.add))
                sel = r3(2, nt * N_GRP, GRP)
                hi, lo = r3(3, nt * N_GRP, 2), r3(4, nt * N_GRP, 2)
                step(tt(hi, sel[:, :, 0:2], sel[:, :, 2:4], ALU.max))
                step(tt(lo, sel[:, :, 0:2], sel[:, :, 2:4], ALU.min))
                g5, g6, g7 = rt[:, 5, 0:nt * N_GRP], rt[:, 6, 0:nt * N_GRP], rt[:, 7, 0:nt * N_GRP]
                step(tt(g5.unsqueeze(2), hi[:, :, 0:1], hi[:, :, 1:2], ALU.max))
                step(tt(g6.unsqueeze(2), hi[:, :, 0:1], hi[:, :, 1:2], ALU.min))
                step(tt(g7.unsqueeze(2), lo[:, :, 0:1], lo[:, :, 1:2], ALU.max))
                step(tt(g6, g6, g7, ALU.max))
                step(tt(g5, g5, g6, ALU.add))

                def first_best(dst, src, rev, a, b, tmp):
                    mx = rt[:, 15, 0:a]
                    step(dve.tensor_reduce(mx, src, X_AXIS, ALU.max))
                    step(tt(tmp, src, mx.unsqueeze(2).to_broadcast([P, a, b]), ALU.is_equal))
                    step(tt(tmp, tmp, rev.unsqueeze(1).to_broadcast([P, a, b]), ALU.mult))
                    step(dve.tensor_reduce(mx, tmp, X_AXIS, ALU.max))
                    step(tt(dst, tmp, mx.unsqueeze(2).to_broadcast([P, a, b]), ALU.is_equal))

                first_best(r3(6, nt, N_GRP), r3(5, nt, N_GRP), const("rev_group"), nt, N_GRP, r3(7, nt, N_GRP))
                step(ts(g7, g6, NEG, -NEG, ALU.mult, ALU.add))
                s4 = r3(3, nt * N_GRP, GRP)
                step(tt(s4, sel, g6.unsqueeze(2).to_broadcast([P, nt * N_GRP, GRP]), ALU.mult))
                step(tt(s4, s4, g7.unsqueeze(2).to_broadcast([P, nt * N_GRP, GRP]), ALU.add))
                first_best(r3(8), r3(3), const("rev_expert"), nt, N_EXP, r3(4))
                step(stt(rt[:, 3, 0:w], rt[:, 8, 0:w], -3.0 * NEG, rt[:, 3, 0:w], ALU.mult, ALU.add))
                first_best(r3(9), r3(3), const("rev_expert"), nt, N_EXP, r3(4))
                step(dve.memset(rt[:, 10 + w // (TILES * N_EXP), w % (TILES * N_EXP):w % (TILES * N_EXP) + N_EXP], 0.0))
                sync(tt(rt[:, 10, 0:w], rt[:, 8, 0:w], rt[:, 9, 0:w], ALU.add), s_ch[l])
                w4 = rt[:, 4:6, 0:w]
                step(tt(w4, rt[:, 8:10, 0:w], rt[:, 1, 0:w].unsqueeze(1).to_broadcast([P, 2, w]), ALU.mult))
                step(dve.tensor_reduce(wts[:, :, 0:nt], w4.rearrange("p i (a b) -> p i a b", b=N_EXP), X_AXIS, ALU.add))
                step(tt(rt[:, 6, 0:nt], wts[:, 0, 0:nt], wts[:, 1, 0:nt], ALU.add))
                step(dve.reciprocal(rt[:, 7, 0:nt], rt[:, 6, 0:nt]))
                step(tt(wts[:, :, 0:nt], wts[:, :, 0:nt], rt[:, 7, 0:nt].unsqueeze(1).to_broadcast([P, 2, nt]), ALU.mult))

                dve.wait_ge(s_rk[l], 1)
                limits = CONST_AT["limit"][0]

                def count_limits(dst, src, first, op):
                    last = NT[l] * P // SLOTS
                    c, b = src.shape[-1], last - first
                    lim = cst[:, limits + first:limits + last].unsqueeze(1).to_broadcast([P, c, b])
                    tmp = above[:, 0:c * b].rearrange("p (a b) -> p a b", b=b)
                    step(tt(tmp, src.unsqueeze(2).to_broadcast([P, c, b]), lim, op))
                    step(dve.tensor_reduce(dst, tmp, X_AXIS, ALU.add))

                total = ps[:, 4, w:w + N_EXP]
                nb, cum, base = rt[:, 5, 0:N_EXP], rt[:, 6, 0:N_EXP], rt[:, 7, 0:N_EXP]
                count_limits(nb, total, 0, ALU.is_gt)
                step(dve.tensor_tensor_scan(cum, nb, zeros, 0.0, ALU.add, ALU.add))
                step(tt(base, cum, nb, ALU.subtract))
                rank, full = ps[:, 4, 0:w], rt[:, 3, 0:w]
                count_limits(full, rank, 1, ALU.is_ge)
                step(stt(rt[:, 2, 0:w], full, -float(SLOTS), rank, ALU.mult, ALU.add))
                step(tt(r3(3), r3(3), base.unsqueeze(1).to_broadcast([P, nt, N_EXP]), ALU.add))
                for k in range(2):
                    step(tt(w4, rt[:, 2:4, 0:w], rt[:, 8 + k, 0:w].unsqueeze(1).to_broadcast([P, 2, w]), ALU.mult))
                    step(dve.tensor_reduce(rt[:, 13:15, nt * k:nt * (k + 1)],
                                           w4.rearrange("p i (a b) -> p i a b", b=N_EXP), X_AXIS, ALU.add))
                Q = 2 * nt
                slot = const("slot").unsqueeze(1).to_broadcast([P, Q, SLOTS])
                tt(oh_slot[:, 0:Q], slot, rt[:, 13, 0:Q].unsqueeze(2).to_broadcast([P, Q, SLOTS]), ALU.is_equal).then_inc(s_oh[l], 1)
                blk = const("block").unsqueeze(1).to_broadcast([P, Q, BLK_COLS])
                step(tt(oh_blk[:, 0, 0:Q], blk, rt[:, 14, 0:Q].unsqueeze(2).to_broadcast([P, Q, BLK_COLS]), ALU.is_equal))
                here = oh_blk[:, 0, 0:Q].rearrange("p (k m) s -> p k m s", m=nt)
                rows_to = oh_blk[:, 1, 0:Q].rearrange("p (k m) s -> p k m s", m=nt)
                dest = const("dest").rearrange("p (k m) -> p k m", m=TILES)[:, :, 0:nt]
                step(dve.memset(oh_blk[:, 1, 0:Q, 0:1], 0.0))
                step(tt(rows_to[:, :, :, 1:], here[:, :, :, :-1], dest.unsqueeze(3).to_broadcast([P, 2, nt, BLK_COLS - 1]),
                        ALU.mult))
                token = const("token")[:, 0:nt].unsqueeze(1).unsqueeze(3)
                tt(here, here, token.to_broadcast([P, 2, nt, BLK_COLS]), ALU.mult).then_inc(s_oh[l], 1)
                step(dve.tensor_copy(plan[:, 1:], cum[0:1]))
                dve.wait_ge(s_tab[l], 1)
                tab = ps[:, 4, P:P + 2 * BLK_COLS]
                step(ts(slot_tab, tab, 0.0, float(NO_ROW), ALU.is_equal, ALU.mult))
                step(ts(slot_tab, slot_tab, const("half"), None, ALU.add))
                sync(stt(slot_idx[:], tab, float(GROUPS), slot_tab, ALU.mult, ALU.add), s_idx[l])

                n = dve.value_load(plan[0:1, N_EXP:], min_val=1, max_val=MAX_BLOCKS)
                dve.sem_inc(m_ac[l], 1)
                dve.sem_inc(m_y[l], 1)
                with dve.Fori(0, n) as i:
                    dve.wait_ge(m_si[l], i + 1)
                    dve.wait_ge(m_up[l], i + 2)
                    dve.wait_ge(m_at[l], i + 1)
                    tt(blk_act, ps[:, 1, 0:FG], blk_silu, ALU.mult).then_inc(m_ac[l], 1)
                    dve.wait_ge(m_at[l], i + 2)
                    dve.tensor_copy(blk_actT, ps[:, 4, 0:FG].rearrange("p (k t) -> p k t", t=P)).then_inc(m_ae[l], 1)
                    dve.wait_ge(m_dn[l], i + 2)
                    dve.wait_ge(m_sc[l], i * 16 + 32)
                    dve.tensor_copy(blk_out, ps[:, 5]).then_inc(m_y[l], 1)

                if l == 0:
                    for half in range(2):
                        split_weights(dve, 1, 0, half)
                for m in range(2):
                    add_experts(l, m)
                if l == 0:
                    for t in range(CTX_TILES):
                        norm1(1, t)

            dve.wait_ge(s_sq, squares("2 of 1") + 2 * NT[1] - 1)
            dve.wait_ge(s_fg, 16)
            sync(mean_square(stat[:, 1, 0:TILES], stat[:, 0, 0:TILES], D), s_fms)
            dve.wait_ge(s_frt, 1)
            step(dve.reciprocal(stat[:, 3, 0:TILES], stat[:, 2, 0:TILES]))
            for m, t in enumerate(TILES_OF[1]):
                stt(tokm[:, t], resid[:, t], stat[:, 3, t:t + 1], rows[:, 4], ALU.mult, ALU.mult).then_inc(s_fin, 1)

        @block.tensor
        def _(pe):
            def turn(dst, src, rows_n=P):
                return pe.transpose(dst, src, ident[0:rows_n, 0:rows_n])

            def turn_mirrored(dst, src):
                return pe.matmul(dst, src, const("mirror"), start=True, stop=True)

            pe.wait_ge(s_small, 16 * VECTOR_LOADS)
            turn(ps[:, 7, 0:N_VEC], vec_rows[0:N_VEC, :], N_VEC).then_inc(s_vec_t, 1)
            turn(ps[:, 7, P:P + 96], adab_rows[0:96, :], 96).then_inc(s_vec_t, 1)
            pe.wait_ge(s_cond, 2)
            pe.wait_ge(s_v, 2)
            pe.wait_ge(s_set, 1)

            def mod_products(a):
                wait_strip(pe, 0, at[0]["ada", a])
                if a >= 1:
                    pe.wait_ge(s_adc, a)
                    pe.wait_ge(s_adr, a)
                if a == ADA:
                    pe.wait_ge(s_modR, 1)
                for k in range(KC):
                    q = 32 * (k % 4)
                    mm = pe.matmul(ps[q:q + 32, mod_banks(a)[0], :], cond[:, k, :], strip(0, at[0]["ada", a])[:, k, :],
                                   start=(k < 4), stop=(k >= 4), skip_group_check=True)
                mm.then_inc(s_ada, 1)

            def mod_turn(a):
                pe.wait_ge(s_adc, a + 1)
                for k in range(4):
                    mm = turn(ps[:, mod_banks(a)[1], k * P:(k + 1) * P], mod_part(a)[:, k * P:(k + 1) * P])
                mm.then_inc(s_adt, 1)

            def modulation_rows(l):
                pe.wait_ge(s_mod, l + 2)
                turn(ps[0:96, 6, 0:P], mod[:, l].rearrange("p j s -> p (j s)")).then_inc(s_modT, 1)

            for a in range(ADA_QKV):
                mod_products(a)
                mod_turn(a)

            for l in range(LAYERS):
                def turn_stream(s):
                    pe.wait_ge(s_xn[l], CTX_TILES * (s + 1))
                    if s == 1:
                        for copied in (s_heA, s_heD):
                            pe.wait_ge(copied[l], KC // 2)
                        if l == 0:
                            pe.wait_ge(s_adr, ADA_QKV)
                    for j, bank in enumerate(STREAM_BANKS[s]):
                        for c in range(2):
                            for t in range(2):
                                mm = turn(ps[:, bank, (2 * c + t) * P:(2 * c + t + 1) * P],
                                          tokm[:, 2 * s + t, (2 * j + c) * P:(2 * j + c + 1) * P])
                        mm.then_inc(s_ht[l][s], 1)

                def turn_qk(n):
                    m = qk_index[l][n]
                    _, copied, value = qkv_copy[l][n]
                    pe.wait_ge(copied, value)
                    if m >= 2:
                        pe.wait_ge(s_qc[l], m - 1)
                    mirrored = l == 1 and qkv_jobs[l][n][0] < 2
                    for k in range(4):
                        mm = (turn_mirrored if mirrored else turn)(ps[:, 4 + m % 2, k * P:(k + 1) * P],
                                  tokm[:, 0, (m % 2) * STRIP + k * P:(m % 2) * STRIP + (k + 1) * P])
                    mm.then_inc(s_qt[l], 1)

                for n, (g, t) in enumerate(qkv_jobs[l]):
                    if n == 0:
                        turn_stream(0)
                        for copied in (s_heA, s_heD):
                            pe.wait_ge(copied[l], KC // 2)
                    if n == (0, CTX_TILES)[l]:
                        turn_stream(1)
                    st = at[l]["qkv", g]
                    wait_strip(pe, l, st)
                    if n >= 2:
                        kind, copied, value = qkv_copy[l][n - 2]
                        pe.wait_ge(copied, value)
                    pos, job, is_last = qkv_pos[l][n]
                    half_strip = HALF_STRIPS * l + 2 * pos
                    for k in range(KC):
                        half = k // (KC // 2)
                        if k % (KC // 2) == 0:
                            if pos == 0:
                                pe.wait_ge(s_xlo, sum(HALF_INPUTS[:l]) + 2 * (t // CTX_TILES) + half + 1)
                            if job == 0:
                                pe.wait_ge(s_wlo, half_strip + half + 1)
                        tok = slice(t * P, (t + 1) * P)
                        high = w_high[(2 * pos + half) % 3][:, k % (KC // 2), :]
                        low = w_low[:, strips[l][st][4], k, :]
                        for i, (x_part, w_part) in enumerate(((x_high, high), (x_high, low), (x_low, high))):
                            mm = pe.matmul(ps[:, n % 2], x_part[:, k, tok], w_part, start=(k == 0 and i == 0),
                                           stop=(k == KC - 1 and i == 2))
                        if k == KC // 2 - 1 and is_last:
                            mm.then_inc(s_half, 1)
                    mm.then_inc(s_qm[l], 1)
                    if n >= 1 and qk_index[l][n - 1] is not None:
                        turn_qk(n - 1)
                    if l == 0:
                        a = ADA_QKV + n // 2
                        if n == 0:
                            for copied in (s_heA, s_heD):
                                pe.wait_ge(copied[0], KC)
                        if n % 2 == 0:
                            if a == ADA:
                                modulation_rows(0)
                            mod_products(a)
                        else:
                            mod_turn(a)
                if qk_index[l][-1] is not None:
                    turn_qk(len(qkv_jobs[l]) - 1)
                pe.wait_ge(s_qc[l], N_QK[l])
                for _, copied, value in qkv_copy[l][-2:]:
                    pe.wait_ge(copied, value)

                pe.wait_ge(s_set, (3, 6)[l])
                if l == 0:
                    def scores(u):
                        t, h = units[0][u]
                        nk = key_tiles(t) * P
                        if u >= 2:
                            pe.wait_ge(s_ex[0], 2 * (u - 1))
                        for cc in range(2):
                            mm = pe.matmul(ps[:, 2 * (u % 2) + cc, 0:nk], (qT, q_odd0)[cc][:, h, t * P:(t + 1) * P],
                                           kT[:, h, 0:nk], start=True, stop=True)
                        mm.then_inc(s_sc[0], 1)

                    def turn_probs(u):
                        t, h = units[0][u]
                        pe.wait_ge(s_pr, u + 1)
                        if u >= 2:
                            pe.wait_ge(s_pc[0], u - 1)
                        for k in range(key_tiles(t)):
                            mm = turn(ps[:, (4, 7)[u % 2], k * P:(k + 1) * P], hT[:, 2 * (u % 3), k * P:(k + 1) * P])
                        mm.then_inc(s_pt[0], 1)

                    def attend(u):
                        t, h = units[0][u]
                        nk = key_tiles(t)
                        pe.wait_ge(s_pc[0], u + 1)
                        if u >= 1:
                            pe.wait_ge(s_oe[0], u)
                        for k in range(nk):
                            mm = pe.matmul(ps[:, 5, 0:2 * HD], hT[:, 6 + u % 2, k * P:(k + 1) * P],
                                           val[:, k, h * 2 * HD:(h + 1) * 2 * HD], start=(k == 0), stop=(k == nk - 1))
                        mm.then_inc(s_pv[0], 1)

                    U = len(units[0])
                    for u in range(U + 3):
                        if u < U:
                            scores(u)
                        if u % ATT_STEP == 0 and u // ATT_STEP < 2 * ADA - ADA_ATT:
                            mod_products(ADA_ATT + u // ATT_STEP)
                        if 2 <= u < U + 2:
                            turn_probs(u - 2)
                        if u >= 3:
                            attend(u - 3)
                        if u % ATT_STEP == 1 and u // ATT_STEP < 2 * ADA - ADA_ATT:
                            a = ADA_ATT + u // ATT_STEP
                            mod_turn(a)
                            if a == 2 * ADA - 1:
                                modulation_rows(1)
                else:
                    def scores1(u):
                        t, h = units[1][u]
                        if u >= 4:
                            pe.wait_ge(s_ex[1], u - 3)
                        t0 = t - CTX_TILES * (h % 2)
                        pe.matmul(ps[:, u % 4], qT[:, h // 2, t0 * P:(t0 + 1) * P], kT[:, h // 2, :],
                                  start=True, stop=True).then_inc(s_sc[1], 1)

                    def turn_probs1(u):
                        pe.wait_ge(s_ex[1], u + 1)
                        if u >= 2:
                            pe.wait_ge(s_pc[1], u - 1)
                        for k in range(TILES):
                            mm = turn(ps[:, (4, 7)[u % 2], k * P:(k + 1) * P], hT[:, u % 4, k * P:(k + 1) * P])
                        mm.then_inc(s_pt[1], 1)

                    def attend1(u):
                        t, h = units[1][u]
                        pe.wait_ge(s_pc[1], u + 1)
                        if u >= 2:
                            pe.wait_ge(s_oe[1], u - 1)
                        for k in range(TILES):
                            mm = pe.matmul(ps[:, 5 + u % 2, 0:HD], hT[:, 4 + u % 2, k * P:(k + 1) * P],
                                           val[:, k, h * HD:(h + 1) * HD], start=(k == 0), stop=(k == TILES - 1))
                        mm.then_inc(s_pv[1], 1)

                    U = len(units[1])
                    for u in range(U + 3):
                        if u < U:
                            scores1(u)
                        if 2 <= u < U + 2:
                            turn_probs1(u - 2)
                        if u >= 3:
                            attend1(u - 3)

                def turn_out(m):
                    t = TILES_OF[l][m]
                    if l == 0:
                        pe.wait_ge(s_on, m + 1)
                    elif m == 0:
                        pe.wait_ge(s_oe[1], len(units[1]))
                    for hf in range(2):
                        if m >= 1:
                            pe.wait_ge(s_oc[l], 2 * (m - 1) + hf + 1)
                        for k in range(4):
                            mm = (turn_mirrored if l == 1 else turn)(
                                ps[:, 4 + hf, k * P:(k + 1) * P], tokm[:, t, (4 * hf + k) * P:(4 * hf + k + 1) * P])
                        mm.then_inc(s_ot[l], 1)

                def project_out(m):
                    t = TILES_OF[l][m]
                    for hf in range(2):
                        j = 2 * m + hf
                        if j >= 2:
                            pe.wait_ge(s_we[l], j - 1)
                        for k in range(KC):
                            half = k // (KC // 2)
                            if k % (KC // 2) == 0:
                                pe.wait_ge(s_xlo, sum(HALF_INPUTS[:l]) + 4 + 2 * m + half + 1)
                                pe.wait_ge(s_wlo, HALF_STRIPS * l + 12 + 2 * hf + half + 1)
                            o_low = x_low[:, k, t * P:(t + 1) * P]
                            high, low = wo_high[:, hf, k], w_low[:, strips[l][at[l]["wo", hf]][4], k, :]
                            for i, (o_part, w_part) in enumerate(((o_high[:, m % 2, k], high), (o_high[:, m % 2, k], low),
                                                                  (o_low, high))):
                                mm = pe.matmul(ps[:, j % 2], o_part, w_part, start=(k == 0 and i == 0),
                                               stop=(k == KC - 1 and i == 2))
                        mm.then_inc(s_wm[l], 1)

                def logits(m):
                    t = TILES_OF[l][m]
                    pe.wait_ge(s_h[l], m + 1)
                    for hf in range(2):
                        if m >= 1:
                            pe.wait_ge((s_h2A, s_h2D)[hf][l], m)
                        for k in range(4):
                            mm = turn(ps[:, 2 + hf, k * P:(k + 1) * P], tokm[:, t, (4 * hf + k) * P:(4 * hf + k + 1) * P])
                        mm.then_inc(s_h2t[l], 1)
                    pe.wait_ge(s_h2A[l], m + 1)
                    pe.wait_ge(s_h2D[l], m + 1)
                    if l == 0 and m == 0:
                        pe.wait_ge(s_late, 16 * LATE_LOADS)
                        pe.wait_ge(s_modR, 2)
                    for k in range(KC):
                        mm = pe.matmul(ps[:, 6, m * N_EXP:(m + 1) * N_EXP], hT[:, k, t * P:(t + 1) * P], rw[:, k, :],
                                       start=(k == 0), stop=(k == KC - 1))
                    mm.then_inc(s_lg[l], 1)

                turn_out(0)
                for m in range(NT[l]):
                    if m + 1 < NT[l]:
                        turn_out(m + 1)
                    project_out(m)
                    if m >= 1:
                        logits(m - 1)
                logits(NT[l] - 1)

                pe.wait_ge(s_set, (4, 7)[l])
                pe.wait_ge(s_oc[l], 2 * NT[l])
                pe.wait_ge(s_ch[l], 1)
                nt = NT[l]
                w = nt * N_EXP
                both = rt[:, 10:12, :].rearrange("p i w -> p (i w)")
                pe.matmul(ps[:, 4, 0:w + N_EXP], const("before"), both[:, 0:w + N_EXP], start=True, stop=False)
                for j in range(nt):
                    later = both[:, j * N_EXP:(j + 1) * N_EXP].unsqueeze(1).to_broadcast([P, nt - j, N_EXP])
                    mm = pe.matmul(ps[:, 4, (j + 1) * N_EXP:w + N_EXP].rearrange("p (a b) -> p a b", b=N_EXP), ones, later,
                                   start=False, stop=(j == nt - 1))
                mm.then_inc(s_rk[l], 1)
                pe.wait_ge(s_oh[l], 2)
                for q in range(2 * nt):
                    for g in range(GROUPS):
                        mm = pe.matmul(ps[g * SLOTS:(g + 1) * SLOTS, 4, P:P + 2 * BLK_COLS].rearrange("p (i s) -> p i s", i=2),
                                       oh_slot[:, q], oh_blk[:, :, q], start=(q == 0), stop=(q == 2 * nt - 1),
                                       skip_group_check=True)
                mm.then_inc(s_tab[l], 1)

                def turn_block(gathered):
                    pe.wait_ge(m_ga[l], gathered)
                    for k in range(DG // P):
                        mm = turn(ps[:, 2, k * P:(k + 1) * P], blk_in[:, k * P:(k + 1) * P])
                    mm.then_inc(m_xt[l], 1)

                def block_products(bank, n_out, lhs_T, n_chunks, weights):
                    for k in range(n_chunks):
                        g_in, c = k // (n_chunks // GROUPS), k % (n_chunks // GROUPS)
                        for g in range(GROUPS):
                            mm = pe.matmul(ps[g * SLOTS:(g + 1) * SLOTS, bank, 0:n_out],
                                           lhs_T[:, c, g_in * SLOTS:(g_in + 1) * SLOTS],
                                           weights[:, k, g * n_out:(g + 1) * n_out],
                                           start=(k == 0), stop=(k == n_chunks - 1), skip_group_check=True)
                    return mm

                pe.wait_ge(s_idx[l], 1)
                n = pe.value_load(plan[0:1, N_EXP:], min_val=1, max_val=MAX_BLOCKS)
                for count in (m_gt, m_up, m_dn, m_at):
                    pe.sem_inc(count[l], 1)
                turn_block(16)

                def block_of(e, which, i):
                    pe.wait_ge(m_xc[l], i + 1)
                    pe.wait_ge(m_wl[l][0], e * 16 + 16)
                    block_products(0, FG, blk_inT, KC, expert_strip(l, 0, which)).then_inc(m_gt[l], 1)
                    pe.wait_ge(m_wl[l][1], e * 16 + 16)
                    block_products(1, FG, blk_inT, KC, expert_strip(l, 1, which)).then_inc(m_up[l], 1)
                    turn_block(i * 16 + 32)
                    pe.wait_ge(m_ac[l], i + 2)
                    for k in range(FG // P):
                        mm = turn(ps[:, 4, k * P:(k + 1) * P], blk_act[:, k * P:(k + 1) * P])
                    mm.then_inc(m_at[l], 1)
                    pe.wait_ge(m_ae[l], i + 1)
                    pe.wait_ge(m_wl[l][2], e * 16 + 16)
                    pe.wait_ge(m_y[l], i + 1)
                    block_products(5, DG, blk_actT, FF // P, expert_strip(l, 2, which)).then_inc(m_dn[l], 1)

                with pe.Fori(0, N_EXP // 2) as pair:
                    for odd in range(2):
                        e = 2 * pair + odd
                        first = pe.value_load(plan[0:1, bass.ds(e, 1)], min_val=0, max_val=MAX_BLOCKS)
                        end = pe.value_load(plan[0:1, bass.ds(e + 1, 1)], min_val=0, max_val=MAX_BLOCKS)
                        with pe.If(first < end):
                            with pe.Fori(first, end) as i:
                                block_of(e, 1 - odd, i)
                pe.wait_ge(m_xc[l], n + 1)
                pe.wait_ge(m_y[l], n + 1)


_INS = ["x", "c", "ctx", "c_ctx", "ada_w", "ada_b", "norm1_g", "norm2_g", "final_norm_g", "diff_w_qkv", "diff_w_o",
        "diff_lambda_q1", "diff_lambda_k1", "diff_lambda_q2", "diff_lambda_k2", "diff_subln_g",
        "na_w_qkv", "na_w_o", "na_rpb", "router_w", "router_bias", "moe_w_gate", "moe_w_up", "moe_w_down"]


def kernel(**inputs):
    import concourse.bacc as bacc
    from concourse.bass_utils import run_bass_kernel_spmd

    nc = bacc.Bacc("TRN2", target_bir_lowering=False, num_devices=1)
    arrays, args = {}, []
    for name in _INS + ["consts"]:
        a = constants() if name == "consts" else np.ascontiguousarray(inputs[name])
        arrays[f"in_{name}_dram"] = a
        args.append(nc.dram_tensor(f"in_{name}_dram", a.shape, mybir.dt.from_np(a.dtype), kind="ExternalInput").ap())
    out = nc.dram_tensor("out_dram", (1, SEQ, D), F32, kind="ExternalOutput").ap()
    build_trunk(nc, *args, out)
    r = run_bass_kernel_spmd(nc, [arrays], core_ids=[0])
    return r.results[0]["out_dram"]
```
